# Optimizing a Trainium2 kernel written in Bass

```python
import math
import jax, jax.numpy as jnp
from jax import lax
import numpy as np

D_MODEL = 1024
BATCH = 1
SEQ = 2048
DEPTH = 1
DEC_BATCH = 1
DEC_SEQ = 64
PAST_LEN = 256

CHUNK = 64
D_MIX = D_MODEL
HEAD_DIM = 64
POOL_WIDTH = D_MIX // 4
POOL_WINDOWS = (2, 4, 8, 16)
POOL_GROUP_DIM = POOL_WIDTH // len(POOL_WINDOWS)
POOL_HIST = max(POOL_WINDOWS) - 1
FOX_WIDTH = (D_MIX - POOL_WIDTH) // 2
FOX_HEADS = FOX_WIDTH // HEAD_DIM
Q_BLOCK = 128
FORGET_BIAS_INIT = 3.0
SSD_WIDTH = D_MIX - POOL_WIDTH - FOX_WIDTH
SSD_HEADS = SSD_WIDTH // HEAD_DIM
SSD_GROUPS = 2
SSD_HEADS_PER_GROUP = SSD_HEADS // SSD_GROUPS
SSD_STATE = 128
SSD_CHUNK = CHUNK
CONV_WIDTH = 4
CONV_DIM = SSD_WIDTH + 2 * SSD_GROUPS * SSD_STATE
D_FF = -(-(8 * D_MODEL) // (3 * 256)) * 256
SPLIT_SIZES = (POOL_WIDTH, FOX_WIDTH, FOX_WIDTH, FOX_WIDTH, FOX_HEADS, SSD_WIDTH, CONV_DIM, SSD_HEADS)
SPLIT_POINTS = tuple(int(v) for v in np.cumsum(SPLIT_SIZES)[:-1])
D_IN = sum(SPLIT_SIZES)
ALPHA = (2 * DEPTH) ** 0.25
BETA = (8 * DEPTH) ** -0.25
LN_EPS = 1e-5
RMS_EPS = 1e-5

kernel_name = 'hymba_pool_fox_ssd_stream'

def layer_norm(x, g, b):
    xf = x.astype(jnp.float32)
    mu = jnp.mean(xf, axis=-1, keepdims=True)
    var = jnp.mean(jnp.square(xf - mu), axis=-1, keepdims=True)
    return ((xf - mu) * lax.rsqrt(var + LN_EPS) * g + b).astype(x.dtype)

def gated_rms_norm(y, z, g):
    hz = y.astype(jnp.float32) * jax.nn.silu(z.astype(jnp.float32))
    hg = hz.reshape(hz.shape[:-1] + (SSD_GROUPS, SSD_WIDTH // SSD_GROUPS))
    hg = hg * lax.rsqrt(jnp.mean(hg * hg, axis=-1, keepdims=True) + RMS_EPS)
    return hg.reshape(hz.shape) * g

def swiglu(h, w_gate, w_up, w_down):
    gate = jnp.einsum('bld,df->blf', h, w_gate)
    up = jnp.einsum('bld,df->blf', h, w_up)
    return jnp.einsum('blf,fd->bld', jax.nn.silu(gate) * up, w_down)

def pool_mixer(u, u_hist, pos, pool_w, pool_scale):
    bsz, seq = u.shape[:2]
    ext = jnp.concatenate([u_hist.astype(u.dtype), u], axis=1)
    cs = jnp.cumsum(ext.astype(jnp.float32), axis=1)
    cs = jnp.pad(cs, ((0, 0), (1, 0), (0, 0)))
    uf = u.astype(jnp.float32)
    groups = []
    for gi, w in enumerate(POOL_WINDOWS):
        sl = slice(gi * POOL_GROUP_DIM, (gi + 1) * POOL_GROUP_DIM)
        window_sum = cs[:, POOL_HIST + 1:, sl] - cs[:, POOL_HIST + 1 - w:POOL_HIST + 1 - w + seq, sl]
        count = jnp.minimum(pos + 1, w).astype(jnp.float32)[None, :, None]
        groups.append(window_sum / count - uf[:, :, sl])
    d = jnp.stack(groups, axis=2)
    y = jnp.einsum('blgc,gcd->blgd', d, pool_w.astype(jnp.float32)).reshape(bsz, seq, POOL_WIDTH)
    return y * pool_scale, ext[:, -POOL_HIST:]

def fox_attend(q, k, v, c_q, c_k, pos_q, pos_k):
    s = jnp.einsum('bqhd,bkhd->bhqk', q, k).astype(jnp.float32) * (HEAD_DIM ** -0.5)
    s = s + jnp.swapaxes(c_q, 1, 2)[..., :, None] - jnp.swapaxes(c_k, 1, 2)[..., None, :]
    s = jnp.where(pos_k[None, :] <= pos_q[:, None], s, -jnp.inf)
    p = jax.nn.softmax(s, axis=-1)
    return jnp.einsum('bhqk,bkhd->bqhd', p.astype(v.dtype), v)

def ssd_scan(x, dt, a, bm, cm, h0, q_len):
    bsz, seq = x.shape[:2]
    n_chunks = seq // q_len

    def chunks(t):
        return jnp.swapaxes(t.reshape((bsz, n_chunks, q_len) + t.shape[2:]), 0, 1)

    tri = jnp.tril(jnp.ones((q_len, q_len), dtype=bool))[None, :, :, None, None]

    def step(h, inp):
        xc, dtc, bc, cc = inp
        cum = jnp.cumsum(dtc * a, axis=1)
        seg = cum[:, :, None] - cum[:, None, :]
        decay = jnp.exp(jnp.where(tri, seg, -jnp.inf))
        cb = jnp.einsum('btgn,bsgn->btsg', cc, bc)
        m = cb[..., None] * decay * dtc[:, None]
        y = jnp.einsum('btsgr,bsgrp->btgrp', m, xc)
        y = y + jnp.einsum('btgn,bgrpn->btgrp', cc, h) * jnp.exp(cum)[..., None]
        last = cum[:, -1]
        w_s = jnp.exp(last[:, None] - cum) * dtc
        h_new = h * jnp.exp(last)[..., None, None] + jnp.einsum('bsgr,bsgrp,bsgn->bgrpn', w_s, xc, bc)
        return h_new, y

    h_last, ys = lax.scan(step, h0, tuple(chunks(t) for t in (x, dt, bm, cm)))
    y = jnp.swapaxes(ys, 0, 1).reshape(x.shape)
    return y, h_last

def token_mixers(h, pos, fox_past, pool_hist, conv_hist, ssm_h0, w_in, pool_w, pool_scale, fox_b_f,
                 conv_w, conv_b, dt_bias, a_log, d_skip, ssm_norm_g, w_out):
    bsz, seq, _ = h.shape
    f32 = jnp.float32
    proj = jnp.einsum('bld,de->ble', h, w_in)
    u, q, k, v, f_raw, z, xbc, dt_raw = jnp.split(proj, SPLIT_POINTS, axis=-1)

    y_pool, pool_new = pool_mixer(u, pool_hist, pos, pool_w, pool_scale)

    q = q.reshape(bsz, seq, FOX_HEADS, HEAD_DIM)
    k = k.reshape(bsz, seq, FOX_HEADS, HEAD_DIM)
    v = v.reshape(bsz, seq, FOX_HEADS, HEAD_DIM)
    logf = jax.nn.log_sigmoid(f_raw.astype(f32) + fox_b_f.astype(f32))
    if fox_past is None:
        c = jnp.cumsum(logf, axis=1)
        n_blocks = seq // Q_BLOCK
        q_blocks = jnp.swapaxes(q.reshape(bsz, n_blocks, Q_BLOCK, FOX_HEADS, HEAD_DIM), 0, 1)
        c_blocks = jnp.swapaxes(c.reshape(bsz, n_blocks, Q_BLOCK, FOX_HEADS), 0, 1)
        pos_blocks = pos.reshape(n_blocks, Q_BLOCK)
        o = lax.map(lambda blk: fox_attend(blk[0], k, v, blk[1], c, blk[2], pos), (q_blocks, c_blocks, pos_blocks))
        o = jnp.swapaxes(o, 0, 1).reshape(bsz, seq, FOX_WIDTH)
    else:
        k_past, v_past, logf_past = fox_past
        n_past = k_past.shape[1]
        k_all = jnp.concatenate([k_past.astype(k.dtype), k], axis=1)
        v_all = jnp.concatenate([v_past.astype(v.dtype), v], axis=1)
        c_all = jnp.cumsum(jnp.concatenate([logf_past.astype(f32), logf], axis=1), axis=1)
        pos_all = jnp.arange(n_past + seq)
        o = fox_attend(q, k_all, v_all, c_all[:, n_past:], c_all, pos, pos_all).reshape(bsz, seq, FOX_WIDTH)

    ext = jnp.concatenate([conv_hist.astype(xbc.dtype), xbc], axis=1)
    conv_new = ext[:, -(CONV_WIDTH - 1):]
    conv = lax.conv_general_dilated(ext, conv_w.reshape(CONV_WIDTH, 1, CONV_DIM).astype(ext.dtype),
                                    window_strides=(1,), padding='VALID',
                                    dimension_numbers=('NWC', 'WIO', 'NWC'),
                                    feature_group_count=CONV_DIM)
    xbc_act = jax.nn.silu((conv + conv_b).astype(f32))
    xs, bm, cm = jnp.split(xbc_act, (SSD_WIDTH, SSD_WIDTH + SSD_GROUPS * SSD_STATE), axis=-1)
    xs = xs.reshape(bsz, seq, SSD_GROUPS, SSD_HEADS_PER_GROUP, HEAD_DIM)
    bm = bm.reshape(bsz, seq, SSD_GROUPS, SSD_STATE)
    cm = cm.reshape(bsz, seq, SSD_GROUPS, SSD_STATE)
    dt = jax.nn.softplus(dt_raw.astype(f32) + dt_bias.astype(f32)).reshape(bsz, seq, SSD_GROUPS, SSD_HEADS_PER_GROUP)
    a = -jnp.exp(a_log.astype(f32)).reshape(SSD_GROUPS, SSD_HEADS_PER_GROUP)
    h0 = ssm_h0.astype(f32).reshape(bsz, SSD_GROUPS, SSD_HEADS_PER_GROUP, HEAD_DIM, SSD_STATE)
    y_ssd, h_last = ssd_scan(xs, dt, a, bm, cm, h0, min(SSD_CHUNK, seq))
    y_ssd = y_ssd + xs * d_skip.astype(f32).reshape(SSD_GROUPS, SSD_HEADS_PER_GROUP)[:, :, None]
    y_ssd = gated_rms_norm(y_ssd.reshape(bsz, seq, SSD_WIDTH), z, ssm_norm_g)

    mixed = jnp.concatenate([y_pool, o.astype(f32), y_ssd], axis=-1).astype(h.dtype)
    y = jnp.einsum('ble,ed->bld', mixed, w_out)
    new_state = (k, v, logf, pool_new, conv_new, h_last.reshape(bsz, SSD_HEADS, HEAD_DIM, SSD_STATE))
    return y, new_state

def run_trunk(x, pos, fox_k, fox_v, fox_logf, pool_hist, conv_hist, ssm_h0, params):
    (ln_in_g, ln_in_b, w_in, pool_w, pool_scale, fox_b_f, conv_w, conv_b, dt_bias, a_log, d_skip,
     ssm_norm_g, w_out, ln_mix_g, ln_mix_b, w_gate, w_up, w_down, ln_ffn_g, ln_ffn_b) = params
    h = layer_norm(x, ln_in_g, ln_in_b)
    layer_states = []
    for l in range(DEPTH):
        fox_past = None if fox_k is None else (fox_k[l], fox_v[l], fox_logf[l])
        y, st = token_mixers(h, pos, fox_past, pool_hist[l], conv_hist[l], ssm_h0[l], w_in[l], pool_w[l],
                             pool_scale[l], fox_b_f[l], conv_w[l], conv_b[l], dt_bias[l], a_log[l],
                             d_skip[l], ssm_norm_g[l], w_out[l])
        h = layer_norm(ALPHA * h + y, ln_mix_g[l], ln_mix_b[l])
        h = layer_norm(ALPHA * h + swiglu(h, w_gate[l], w_up[l], w_down[l]), ln_ffn_g[l], ln_ffn_b[l])
        layer_states.append(st)
    new_state = tuple(jnp.stack([st[i] for st in layer_states]) for i in range(len(layer_states[0])))
    return h, new_state

def setup_inputs(seed: int = 0) -> dict:
    key = jax.random.key(seed)
    ks = jax.random.split(key, 32)

    def nrm(k, shape, scale):
        return scale * jax.random.normal(k, shape, jnp.float32)

    dt0 = jnp.exp(jax.random.uniform(ks[16], (DEPTH, SSD_HEADS), jnp.float32,
                                     minval=math.log(1e-3), maxval=math.log(1e-1)))
    return {
        'x_prompt': nrm(ks[0], (BATCH, SEQ, D_MODEL), 1.0),
        'x_sample': nrm(ks[1], (DEC_BATCH, DEC_SEQ, D_MODEL), 1.0),
        'cache_fox_k': nrm(ks[2], (DEPTH, DEC_BATCH, PAST_LEN, FOX_HEADS, HEAD_DIM), 1.0),
        'cache_fox_v': nrm(ks[3], (DEPTH, DEC_BATCH, PAST_LEN, FOX_HEADS, HEAD_DIM), 1.0),
        'cache_fox_logf': jax.nn.log_sigmoid(FORGET_BIAS_INIT + nrm(ks[4], (DEPTH, DEC_BATCH, PAST_LEN, FOX_HEADS), 1.0)),
        'state_pool': nrm(ks[5], (DEPTH, DEC_BATCH, POOL_HIST, POOL_WIDTH), 1.0),
        'state_conv': nrm(ks[6], (DEPTH, DEC_BATCH, CONV_WIDTH - 1, CONV_DIM), 1.0),
        'state_ssm': nrm(ks[7], (DEPTH, DEC_BATCH, SSD_HEADS, HEAD_DIM, SSD_STATE), 0.1),
        'ln_in_g': 1.0 + nrm(ks[8], (D_MODEL,), 0.1),
        'ln_in_b': nrm(ks[9], (D_MODEL,), 0.02),
        'w_in': nrm(ks[10], (DEPTH, D_MODEL, D_IN), D_MODEL ** -0.5),
        'pool_w': nrm(ks[11], (DEPTH, len(POOL_WINDOWS), POOL_GROUP_DIM, POOL_GROUP_DIM), POOL_GROUP_DIM ** -0.5),
        'pool_scale': 1.0 + nrm(ks[12], (DEPTH, POOL_WIDTH), 0.1),
        'fox_b_f': FORGET_BIAS_INIT + nrm(ks[13], (DEPTH, FOX_HEADS), 0.5),
        'conv_w': nrm(ks[14], (DEPTH, CONV_WIDTH, CONV_DIM), CONV_WIDTH ** -0.5),
        'conv_b': nrm(ks[15], (DEPTH, CONV_DIM), 0.02),
        'dt_bias': dt0 + jnp.log(-jnp.expm1(-dt0)),
        'a_log': jnp.log(jax.random.uniform(ks[17], (DEPTH, SSD_HEADS), jnp.float32, minval=1.0, maxval=16.0)),
        'd_skip': 1.0 + nrm(ks[18], (DEPTH, SSD_HEADS), 0.1),
        'ssm_norm_g': 1.0 + nrm(ks[19], (DEPTH, SSD_WIDTH), 0.1),
        'w_out': nrm(ks[20], (DEPTH, D_MIX, D_MODEL), BETA * D_MIX ** -0.5),
        'ln_mix_g': 1.0 + nrm(ks[21], (DEPTH, D_MODEL), 0.1),
        'ln_mix_b': nrm(ks[22], (DEPTH, D_MODEL), 0.02),
        'w_gate': nrm(ks[23], (DEPTH, D_MODEL, D_FF), D_MODEL ** -0.5),
        'w_up': nrm(ks[24], (DEPTH, D_MODEL, D_FF), D_MODEL ** -0.5),
        'w_down': nrm(ks[25], (DEPTH, D_FF, D_MODEL), BETA * D_FF ** -0.5),
        'ln_ffn_g': 1.0 + nrm(ks[26], (DEPTH, D_MODEL), 0.1),
        'ln_ffn_b': nrm(ks[27], (DEPTH, D_MODEL), 0.02),
    }

def reference(x_prompt, x_sample, cache_fox_k, cache_fox_v, cache_fox_logf, state_pool, state_conv, state_ssm,
              ln_in_g, ln_in_b, w_in, pool_w, pool_scale, fox_b_f, conv_w, conv_b, dt_bias, a_log, d_skip,
              ssm_norm_g, w_out, ln_mix_g, ln_mix_b, w_gate, w_up, w_down, ln_ffn_g, ln_ffn_b):
    params = (ln_in_g, ln_in_b, w_in, pool_w, pool_scale, fox_b_f, conv_w, conv_b, dt_bias, a_log, d_skip,
              ssm_norm_g, w_out, ln_mix_g, ln_mix_b, w_gate, w_up, w_down, ln_ffn_g, ln_ffn_b)
    bsz, seq = x_prompt.shape[:2]
    zero_pool = jnp.zeros((DEPTH, bsz, POOL_HIST, POOL_WIDTH), x_prompt.dtype)
    zero_conv = jnp.zeros((DEPTH, bsz, CONV_WIDTH - 1, CONV_DIM), x_prompt.dtype)
    zero_ssm = jnp.zeros((DEPTH, bsz, SSD_HEADS, HEAD_DIM, SSD_STATE), jnp.float32)
    y_prompt, (p_fox_k, p_fox_v, p_fox_logf, p_pool, p_conv, p_ssm) = run_trunk(
        x_prompt, jnp.arange(seq), None, None, None, zero_pool, zero_conv, zero_ssm, params)
    n_past = cache_fox_k.shape[2]
    pos_s = n_past + jnp.arange(x_sample.shape[1])
    y_sample, (s_fox_k, s_fox_v, s_fox_logf, s_pool, s_conv, s_ssm) = run_trunk(
        x_sample, pos_s, cache_fox_k, cache_fox_v, cache_fox_logf, state_pool, state_conv, state_ssm, params)
    return (y_prompt, y_sample, p_fox_k, p_fox_v, p_fox_logf, p_pool, p_conv, p_ssm,
            s_fox_k, s_fox_v, s_fox_logf, s_pool, s_conv, s_ssm)


_drawn_inputs = setup_inputs


def setup_inputs(seed=0):
    import zlib

    import numpy as np

    out = dict(_drawn_inputs(seed))
    spreads = {}
    factors = {'cache_fox_k': 2.917,
     'cache_fox_logf': 8.0,
     'state_pool': 2.887,
     'pool_scale': 2.73,
     'd_skip': 2.831,
     'ln_mix_b': 2.734,
     'ln_ffn_b': 3.129}
    for name, (base, spread) in spreads.items():
        noise = np.random.default_rng([zlib.crc32(name.encode()), seed]).standard_normal(out[name].shape)
        drawn = base * np.exp(spread * noise) if base else spread * noise
        out[name] = __import__('jax').numpy.asarray(drawn.astype(out[name].dtype))
    for name, factor in factors.items():
        out[name] = (out[name] * factor).astype(out[name].dtype)
    return out
```

```python
from contextlib import ExitStack

import numpy as np

import concourse.bass as bass
from concourse import mybir

F32 = mybir.dt.float32
F32R = mybir.dt.float32r
BF16 = mybir.dt.bfloat16
ALU = mybir.AluOpType
ACT = mybir.ActivationFunctionType
AX = mybir.AxisListType

P = 128
D = 1024
KT = D // P
SEQ, DEC, PAST = 2048, 64, 256
TOKENS = SEQ + DEC
HD = 64
POOL_W, FOX_W, SSD_W = 256, 384, 384
FH, SH, SG, SR = 6, 6, 2, 3
WINDOWS = (2, 4, 8, 16)
PHIST, CHIST = 15, 3
NST = 128
CONV = 896
CB_ = CONV // P
DFF = 2816
FT = DFF // P
ALPHA = 2.0 ** 0.25
EPS = 1e-5
C_U, C_Q, C_K, C_V, C_F, C_Z, C_X, C_DT = 0, 256, 640, 1024, 1408, 1414, 1798, 2694
NCH = (POOL_W + FOX_W + CONV) // P
TOKW = C_X - C_K + SH
T_V, T_F, T_Z, T_DT = 384, 768, 774, 1158
TG = 3
TGW = TOKW // TG
MIX_FOX, MIX_SSD = POOL_W, POOL_W + FOX_W
SLAB = 256
SLABS = SEQ // SLAB


def host_constants():
    k, t = np.arange(P)[:, None], np.arange(P)[None, :]
    upto = (k <= t).astype(np.float32)
    after = (k > t).astype(np.float32)
    ident = np.eye(P, dtype=np.float32)
    ones = np.ones((P, P), np.float32)
    square = np.stack([ident, upto, after, ones], 1).copy()
    inv = np.zeros((P, 2, 16), np.float32)
    for g, w in enumerate(WINDOWS):
        rows = slice(64 * (g % 2), 64 * (g % 2) + 64)
        inv[rows, g // 2] = 1.0 / np.minimum(np.arange(16) + 1, w)
    return {"c_square": square, "c_inv": inv}


class Chain:

    def __init__(self, eng, sem):
        self.eng, self.sem, self.n, self.base = eng, sem, 0, 0

    def done(self, ins):
        ins.then_inc(self.sem, 1)
        self.n += 1

    def wait(self):
        if self.n or not isinstance(self.base, int) or self.base:
            self.eng.wait_ge(self.sem, self.base + self.n)

    def step(self, ins):
        self.done(ins)
        self.wait()

    def enter(self, turn, first, steps):
        self.before, self.steps = self.n, steps
        self.base, self.n = turn * steps + (self.before - first * steps), 0

    def leave(self, turns):
        assert self.n == self.steps, (self.n, self.steps)
        self.base, self.n = 0, self.before + turns * self.steps


def load_rows(ap, n=P):
    return ap.partition_broadcast(n)


def project_mix_scan(nc, sem, x_prompt, x_sample, state_pool, state_conv, state_ssm, ln_g, ln_b, w_in,
                     pool_w, pool_scale, fox_b_f, conv_w, conv_b, dt_bias, a_log, d_skip, norm_g,
                     c_square, c_inv, h_rows, q_ch, k_ch, mixed, outs):
    (p_k, p_v, p_logf, p_pool, p_conv, p_ssm, s_k, s_v, s_logf, s_pool, s_conv, s_ssm) = outs
    LAST = SLABS

    def width(s):
        return DEC if isinstance(s, int) and s == LAST else SLAB

    def tiles(s):
        return 1 if isinstance(s, int) and s == LAST else SLAB // P

    def rows(s):
        return DEC if isinstance(s, int) and s == LAST else P

    FIRST = 2 * (SLAB // P)
    TURN = NCH + (TG + 1 + 2) * (SLAB // P)

    def group0(s):
        return FIRST + s * TURN - (2 if isinstance(s, int) and s == LAST else 0)

    def g_tok(s):
        return group0(s) + NCH

    def g_kt(s):
        return g_tok(s) + TG * tiles(s)

    def g_next(s):
        return g_kt(s) + tiles(s)

    def chunk_no(q, c):
        return q * (SLAB // P) + c

    with ExitStack() as ctx:
        def sb(name, shape, dt=F32):
            return ctx.enter_context(nc.sbuf_tensor(name, shape, dt))

        def ps(name):
            return ctx.enter_context(nc.psum_tensor(name, [P, 2, 512], F32))

        w_ch = sb("w_ch", [P, KT, NCH * P])
        w_tok = sb("w_tok", [P, KT, TOKW])
        lng, lnb = sb("lng", [P, D]), sb("lnb", [P, D])
        square = sb("square", [P, 4, P])
        ident, upto, after, ones = (square[:, i, :] for i in range(4))
        inv = sb("inv", [P, 2, 16])
        poolw = sb("poolw", [P, 2, P])
        pscale, gnorm = sb("pscale", [P, POOL_W]), sb("gnorm", [P, SSD_W])
        cw, cbias = sb("cw", [P, 4, CB_]), sb("cbias", [P, CB_])
        bf, bdt, a_neg, dsk = sb("bf", [P, FH]), sb("bdt", [P, SH]), sb("a_neg", [P, SH]), sb("dsk", [P, SH])
        half = sb("half", [P, 2])
        xb = sb("xb", [P, 2, D])
        stats, mv = sb("stats", [P, 2, 6]), sb("mv", [P, 2])
        rstd = sb("rstd", [P, 1])
        idle = sb("idle", [1, 1])
        hT = sb("hT", [P, KT, SLAB])
        qs = sb("qs", [P, 3, SLAB])
        uT = sb("uT", [P, 2, PHIST + SLAB])
        win = [sb(f"win{w}", [P, 2, PHIST + SLAB]) for w in WINDOWS]
        pd = sb("pd", [P, 2, SLAB])
        pm = sb("pm", [P, 2, POOL_W])
        xr = sb("xr", [P, CB_, CHIST + SLAB])
        cv = sb("cv", [P, CB_, SLAB])
        tk = sb("tk", [P, 2, TOKW])
        ks = sb("ks", [P, 3, SLAB])
        spy, spa, spe, spw, spl, spr = (sb(f"sp{n}", [P, 2, FH + SH]) for n in "yaewlr")
        logf = sb("logf", [P, 2, FH])
        dta = sb("dta", [P, 2, SH])
        amask = sb("amask", [P, SH, P])
        dec = sb("dec", [P, SH, P])
        ex = sb("ex", [P, 3 * SH])
        xt, xdt, xw = sb("xt", [P, SSD_W]), sb("xdt", [P, SSD_W]), sb("xw", [P, SSD_W])
        bt, cbm = sb("bt", [P, SG * NST]), sb("cbm", [P, SG, P])
        w6 = sb("w6", [P, SH])
        ya, yb, yo = sb("ya", [P, SSD_W]), sb("yb", [P, SSD_W]), sb("yo", [P, SSD_W])
        ssum, rr = sb("ssum", [P, SG]), sb("rr", [P, SG])
        state = {0: sb("state_p", [NST, SSD_W]), 1: sb("state_s", [NST, SSD_W])}
        stin = sb("stin", [P, 3, NST])
        pp, psT, psG = ps("pp"), ps("psT"), ps("psG")
        psC = ctx.enter_context(nc.psum_tensor("psC", [P, 512], F32))
        psY = ctx.enter_context(nc.psum_tensor("psY", [P, 512], F32))

        first_in, hist_in = sem("norm_consts_in"), sem("histories_in")
        consts_in, w_in_sem = sem("consts_in"), [sem(f"w_block{i}_in") for i in range(NCH + 1)]
        x_in, h_done = [sem(f"x_tile{j}_in") for j in range(2)], sem("h_done")
        moments, rstd_done = sem("moments"), sem("rstd_done")
        full, evac = sem("group_full"), sem("group_evacuated")
        h_out, q_out, kv_out, kt_out, small_out, y_out, m_out = (
            sem("h_stored"), sem("q_stored"), sem("kv_stored"), sem("kt_stored"),
            sem("logf_stored"), sem("y_stored"), sem("pool_stored"))
        end_out = sem("states_stored")
        conv_done, pool_done, pool_mm, pm_done = sem("conv_done"), sem("pool_done"), sem("pool_mm"), sem("pm_done")
        silu_done = sem("silu_done")
        sp_ready, sp_exp, sp_one, sp_ln, dt_done = (
            sem("sp_ready"), sem("sp_exp"), sem("sp_one"), sem("sp_ln"), sem("dt_done"))
        amask_done, seg_done, sums_done, exp_done, mix_ready, mix_done, chunk_done = (
            sem("amask_done"), sem("seg_done"), sem("sums_done"), sem("exp_done"), sem("mix_ready"),
            sem("mix_done"), sem("chunk_done"))
        ss_done, rr_done, y_done = sem("ss_done"), sem("rr_done"), sem("y_done")
        a_exp, init_done = sem("a_exp"), sem("init_done")
        st_t, st_rows = sem("state_transposed"), sem("state_rows")
        dve_chain = sem("dve_chain")
        N_CONST = 1 + 4 + 6 + 4 + 1 + 3

        block = ctx.enter_context(nc.Block())

        def token0(s):
            return s * SLAB

        def tile_rows(s, j):
            return bass.ds(token0(s) + j * P, rows(s))

        def out_rows(s, j, prompt, sample):
            if isinstance(s, int) and s == LAST:
                return sample[bass.ds(j * P, DEC)]
            return prompt[tile_rows(s, j)]

        def program(s_body, eng, chain=None, steps=0):
            s_body(0)
            with eng.Fori(1, SLABS - 1) as s:
                if chain:
                    chain.enter(s, 1, steps)
                s_body(s)
            if chain:
                chain.leave(SLABS - 2)
            s_body(SLABS - 1)
            s_body(SLABS)

        @block.gpsimd
        def _(pool):
            nc.gpsimd.memset(half[:, :], -0.5).then_inc(init_done, 1)
            pool.wait_ge(init_done, 3)

            def norm(s):
                for j in range(tiles(s)):
                    n = s * 2 + j
                    pool.wait_ge(moments, n + 1)
                    nc.gpsimd.tensor_tensor(rstd[0:rows(s), :], mv[0:rows(s), 1:2], half[0:rows(s), 0:1],
                                            ALU.pow).then_inc(rstd_done, 1)

            def scan(q):
                for c in range(tiles(q)):
                    pool.wait_ge(ss_done, chunk_no(q, c) + 1)
                    nc.gpsimd.tensor_tensor(rr[0:rows(q), :], ssum[0:rows(q), :], half[0:rows(q), :],
                                            ALU.pow).then_inc(rr_done, 1)

            def slab(s):
                first = isinstance(s, int) and s == 0
                last = isinstance(s, int) and s == LAST
                if last:
                    scan(s - 1)
                    return
                nxt = s + 1
                if first:
                    norm(nxt)
                    return
                for c in range(2):
                    pool.wait_ge(ss_done, chunk_no(s - 1, c) + 1)
                    nc.gpsimd.tensor_tensor(rr[:, :], ssum[:, :], half[:, :], ALU.pow).then_inc(rr_done, 1)
                    if c < tiles(nxt):
                        n, r = nxt * 2 + c, rows(nxt)
                        pool.wait_ge(moments, n + 1)
                        nc.gpsimd.tensor_tensor(rstd[0:r, :], mv[0:r, 1:2], half[0:r, 0:1],
                                                ALU.pow).then_inc(rstd_done, 1)

            norm(0)
            program(slab, pool)
            scan(LAST)

        @block.sync
        def _(sp):
            def x_load(s):
                for j in range(tiles(s)):
                    if not (isinstance(s, int) and s == 0):
                        sp.wait_ge(h_out, 16 * (s * 2 - 2 + 2))
                        sp.wait_ge(full, group0(s - 1))
                    sp.dma_start(xb[0:rows(s), j, :], out_rows(s, j, x_prompt, x_sample)).then_inc(x_in[j], 16)

            def h_store(s):
                for j in range(tiles(s)):
                    sp.wait_ge(h_done, s * 2 + j + 1)
                    sp.dma_start(h_rows[tile_rows(s, j), :], xb[0:rows(s), j, :]).then_inc(h_out, 16)

            def const(dst, src, **kw):
                sp.dma_start(dst, src, **kw).then_inc(consts_in, 16)

            x_load(0)
            sp.dma_start(lng[:, :], load_rows(ln_g)).then_inc(first_in, 16)
            sp.dma_start(lnb[:, :], load_rows(ln_b)).then_inc(first_in, 16)
            sp.dma_start(square[:, :, :], c_square).then_inc(first_in, 16)
            w3 = w_in.rearrange("(k p) n -> p k n", p=P)
            cols = [C_U, C_U + P] + [C_Q + i * P for i in range(3)] + [C_X + i * P for i in range(CB_)]
            for i, c in enumerate(cols[:2]):
                sp.dma_start(w_ch[:, :, i * P:(i + 1) * P], w3[:, :, c:c + P]).then_inc(w_in_sem[i], 16)
            const(inv[:, :, :], c_inv)
            sp.wait_ge(init_done, 3)
            for g in range(4):
                a = 64 * (g % 2)
                const(poolw[a:a + 64, g // 2, a:a + 64], pool_w[g])
            const(pscale[:, :], load_rows(pool_scale))
            const(gnorm[:, :], load_rows(norm_g))
            const(bf[:, :], load_rows(fox_b_f))
            const(bdt[:, :], load_rows(dt_bias))
            const(a_neg[:, :], load_rows(a_log))
            const(dsk[:, :], load_rows(d_skip))
            for t in range(4):
                const(cw[:, t, :], conv_w[t].rearrange("(b p) -> p b", p=P), allow_slow_non_contiguous=True)
            const(cbias[:, :], conv_b.rearrange("(b p) -> p b", p=P), allow_slow_non_contiguous=True)
            for b in range(3):
                const(stin[:, b, :], state_ssm[b * P:(b + 1) * P, :])
            for i, c in enumerate(cols[2:], 2):
                sp.dma_start(w_ch[:, :, i * P:(i + 1) * P], w3[:, :, c:c + P]).then_inc(w_in_sem[i], 16)
            sp.dma_start(w_tok[:, :, 0:C_X - C_K], w3[:, :, C_K:C_X]).then_inc(w_in_sem[NCH], 16)
            sp.dma_start(w_tok[:, :, T_DT:TOKW], w3[:, :, C_DT:C_DT + SH]).then_inc(w_in_sem[NCH], 16)
            h_store(0)

            def y_store(q, c):
                sp.wait_ge(y_done, chunk_no(q, c) + 1)
                sp.dma_start(mixed[tile_rows(q, c), MIX_SSD:D], yo[0:rows(q), :]).then_inc(y_out, 16)

            def slab(s):
                first = isinstance(s, int) and s == 0
                last = isinstance(s, int) and s == LAST
                w = width(s)
                if not last:
                    x_load(s + 1)
                if last:
                    sp.wait_ge(pool_done, LAST)
                    sp.wait_ge(conv_done, LAST)
                    for b in range(2):
                        sp.dma_start(uT[:, b, 0:PHIST],
                                     state_pool[:, b * P:(b + 1) * P].rearrange("t p -> p t"),
                                     allow_slow_non_contiguous=True).then_inc(hist_in, 16)
                    for b in range(CB_):
                        sp.dma_start(xr[:, b, 0:CHIST],
                                     state_conv[:, b * P:(b + 1) * P].rearrange("t p -> p t"),
                                     allow_slow_non_contiguous=True).then_inc(hist_in, 16)
                if first:
                    h_store(s + 1)
                sp.wait_ge(evac, group0(s) + 5)
                for b in range(3):
                    sp.dma_start(q_ch[b * P:(b + 1) * P, bass.ds(token0(s), w)], qs[:, b, 0:w]).then_inc(q_out, 16)
                if not first:
                    for c in range(tiles(s - 1)):
                        y_store(s - 1, c)
                        if not last and c < tiles(s + 1):
                            j, n = c, s + 1
                            sp.wait_ge(h_done, n * 2 + j + 1)
                            sp.dma_start(h_rows[tile_rows(n, j), :], xb[0:rows(n), j, :]).then_inc(h_out, 16)
                for j in range(tiles(s)):
                    sp.wait_ge(evac, g_tok(s) + TG * (j + 1))
                    sp.dma_start(out_rows(s, j, p_k, s_k), tk[0:rows(s), j, 0:T_V]).then_inc(kv_out, 16)
                    sp.dma_start(out_rows(s, j, p_v, s_v), tk[0:rows(s), j, T_V:T_F]).then_inc(kv_out, 16)
                sp.wait_ge(evac, g_kt(s) + tiles(s))
                for b in range(3):
                    sp.dma_start(k_ch[b * P:(b + 1) * P, bass.ds(token0(s), w)], ks[:, b, 0:w]).then_inc(kt_out, 16)
                sp.wait_ge(dt_done, s + 1)
                for j in range(tiles(s)):
                    sp.dma_start(out_rows(s, j, p_logf, s_logf), logf[0:rows(s), j, :]).then_inc(small_out, 16)
                sp.wait_ge(pm_done, s + 1)
                for j in range(tiles(s)):
                    sp.dma_start(mixed[tile_rows(s, j), 0:POOL_W], pm[0:rows(s), j, :]).then_inc(m_out, 16)
                if isinstance(s, int) and s >= LAST - 1:
                    u_out, x_out = (s_pool, s_conv) if last else (p_pool, p_conv)
                    for b in range(2):
                        sp.dma_start(u_out[:, b * P:(b + 1) * P].rearrange("t p -> p t"),
                                     uT[:, b, w:w + PHIST], allow_slow_non_contiguous=True).then_inc(end_out, 16)
                    for b in range(CB_):
                        sp.dma_start(x_out[:, b * P:(b + 1) * P].rearrange("t p -> p t"),
                                     xr[:, b, w:w + CHIST], allow_slow_non_contiguous=True).then_inc(end_out, 16)
                    if not last:
                        sp.wait_ge(end_out, 16 * (2 + CB_))

            program(slab, sp)
            y_store(LAST, 0)
            for i, dst in enumerate((p_ssm, s_ssm)):
                sp.wait_ge(st_rows, 1 + 2 * i)
                for b in range(3):
                    sp.dma_start(dst[b * P:(b + 1) * P, :], stin[:, b, :]).then_inc(end_out, 16)
                sp.wait_ge(end_out, 16 * (2 * (2 + CB_) + 3 * (i + 1)))
                if i == 0:
                    sp.sem_inc(st_rows, 1)
            n = 2 * SLABS + 1
            sp.wait_ge(h_out, 16 * n)
            sp.wait_ge(q_out, 16 * 3 * (SLABS + 1))
            sp.wait_ge(kv_out, 16 * 2 * n)
            sp.wait_ge(kt_out, 16 * 3 * (SLABS + 1))
            sp.wait_ge(small_out, 16 * n)
            sp.wait_ge(y_out, 16 * n)
            sp.wait_ge(m_out, 16 * n)

        @block.tensor
        def _(pe):
            def begin(n, ok):
                if ok:
                    pe.wait_ge(evac, n - 1)

            def transposes(s, n0):
                for j in range(tiles(s)):
                    pe.wait_ge(h_done, s * 2 + j + 1)
                    for u in range(2):
                        n = n0 + 2 * j + u
                        begin(n, not isinstance(n, int) or n >= 2)
                        for i in range(4):
                            k = 4 * u + i
                            mm = pe.transpose(pp[:, u, i * P:i * P + rows(s)], xb[0:rows(s), j, k * P:(k + 1) * P],
                                              ident[0:rows(s), 0:rows(s)])
                        mm.then_inc(full, 1)

            def scan_a(q, c):
                r, n = rows(q), chunk_no(q, c)
                st = state[1 if isinstance(q, int) and q == LAST else 0]
                a = c * P
                if not (isinstance(q, int) and q == 0 and c == 0):
                    pe.wait_ge(chunk_done, n)
                if c == 0:
                    pe.wait_ge(pm_done, q + 1)
                pe.wait_ge(silu_done, 2 * q + 2)
                for b in range(5):
                    dst = psT[0:r, 0, b * P:(b + 1) * P] if b < 3 else psT[0:r, 1, (b - 3) * P:(b - 2) * P]
                    pe.transpose(dst, cv[:, b, a:a + r], ident)
                pe.wait_ge(dt_done, q + 1)
                for i, m in enumerate((upto, after)):
                    pe.matmul(psC[0:r, 256 + 6 * i:262 + 6 * i], m[0:r, 0:r], dta[0:r, c, :], start=True, stop=True)
                pe.matmul(psC[:, 268:274], ones[0:r, :], dta[0:r, c, :], start=True, stop=True)
                for g in range(SG):
                    pe.matmul(psC[0:r, g * P:g * P + r], cv[:, 3 + g, a:a + r], cv[:, 5 + g, a:a + r],
                              start=True, stop=True)
                for g in range(SG):
                    mm = pe.matmul(psY[0:r, g * 192:(g + 1) * 192], cv[:, 5 + g, a:a + r],
                                   st[:, g * 192:(g + 1) * 192], start=True, stop=True)
                mm.then_inc(sums_done, 1)
                pe.wait_ge(amask_done, n + 1)
                for h in range(SH):
                    mm = pe.matmul(psG[0:r, h // 3, (h % 3) * P:(h % 3) * P + r], amask[0:r, h, 0:r],
                                   upto[0:r, 0:r], start=True, stop=True)
                mm.then_inc(seg_done, 1)

            def scan_c(q, c):
                r, n = rows(q), chunk_no(q, c)
                pe.wait_ge(mix_ready, n + 1)
                for g in range(SG):
                    pe.matmul(psT[:, 0, g * 192:(g + 1) * 192], bt[0:r, g * P:(g + 1) * P],
                              xw[0:r, g * 192:(g + 1) * 192], start=True, stop=True)
                for h in range(SH):
                    mm = pe.matmul(psY[0:r, h * HD:(h + 1) * HD], dec[0:r, h, 0:r], xdt[0:r, h * HD:(h + 1) * HD],
                                   start=True, stop=True)
                mm.then_inc(mix_done, 1)

            def scan(q, slot):
                for c in range(tiles(q)):
                    if slot == 5 * c:
                        scan_a(q, c)
                    if slot == 5 * c + 3:
                        scan_c(q, c)

            pe.wait_ge(first_in, 16 * 3)
            transposes(0, 0)
            pe.wait_ge(consts_in, 16 * N_CONST)
            for b in range(3):
                mm = pe.transpose(psT[:, 0, b * P:(b + 1) * P], stin[:, b, :], ident)
            mm.then_inc(st_t, 1)

            def slab(s):
                first = isinstance(s, int) and s == 0
                last = isinstance(s, int) and s == LAST
                w, r = width(s), rows(s)
                pe.wait_ge(evac, group0(s))
                for i in range(NCH):
                    n = group0(s) + i
                    if first:
                        pe.wait_ge(w_in_sem[i], 16)
                    begin(n, True)
                    for k in range(KT):
                        mm = pe.matmul(pp[:, i % 2, 0:w], w_ch[:, k, i * P:(i + 1) * P], hT[:, k, 0:w],
                                       start=(k == 0), stop=(k == KT - 1))
                    mm.then_inc(full, 1)
                    if not first:
                        scan(s - 1, i)
                if first:
                    pe.wait_ge(w_in_sem[NCH], 32)
                for j in range(tiles(s)):
                    for u in range(TG):
                        i = j * TG + u
                        begin(g_tok(s) + i, True)
                        for k in range(KT):
                            mm = pe.matmul(pp[0:r, i % 2, 0:TGW], hT[:, k, j * P:j * P + r],
                                           w_tok[:, k, u * TGW:(u + 1) * TGW], start=(k == 0), stop=(k == KT - 1))
                        mm.then_inc(full, 1)
                pe.wait_ge(pool_done, s + 1)
                if not first:
                    pe.wait_ge(chunk_done, chunk_no(s, 0))
                else:
                    pe.wait_ge(init_done, 4)
                for j in range(tiles(s)):
                    for b in range(2):
                        mm = pe.matmul(psT[0:r, j, b * P:(b + 1) * P], pd[:, b, j * P:j * P + r], poolw[:, b, :],
                                       start=True, stop=True)
                mm.then_inc(pool_mm, 1)
                for j in range(tiles(s)):
                    i = tiles(s) * TG + j
                    begin(g_kt(s) + j, True)
                    pe.wait_ge(evac, g_tok(s) + TG * j + 1)
                    for b in range(3):
                        mm = pe.transpose(pp[:, i % 2, b * P:b * P + r], tk[0:r, j, b * P:(b + 1) * P],
                                          ident[0:r, 0:r])
                    mm.then_inc(full, 1)
                if not last:
                    transposes(s + 1, g_next(s))

            program(slab, pe)
            scan_a(LAST, 0)
            scan_c(LAST, 0)
            for i in range(2):
                pe.wait_ge(chunk_done, chunk_no(LAST, 0) + 1)
                if i:
                    pe.wait_ge(st_rows, 3 - 1)
                for b in range(3):
                    mm = pe.transpose(psT[:, 0, b * P:(b + 1) * P], state[i][:, b * P:(b + 1) * P], ident)
                mm.then_inc(st_t, 1)

        @block.scalar
        def _(act):
            def take(n, out, src, scale=1.0):
                act.wait_ge(full, n + 1)
                nc.scalar.activation(out, src, ACT.Copy, scale=scale).then_inc(evac, 1)

            def h_take(s, n0):
                for j in range(tiles(s)):
                    for u in range(2):
                        take(n0 + 2 * j + u, hT[:, 4 * u:4 * u + 4, j * P:j * P + rows(s)],
                             pp[:, u, :].rearrange("p (i c) -> p i c", c=P)[:, :, 0:rows(s)])

            def scan(q, slot):
                for c in range(tiles(q)):
                    if slot != 5 * c:
                        continue
                    r, n = rows(q), chunk_no(q, c)
                    act.wait_ge(sums_done, n + 1)
                    nc.scalar.activation(ex[0:r, 0:12], psC[0:r, 256:268], ACT.Exp)
                    nc.scalar.activation(ex[:, 12:18], psC[:, 268:274], ACT.Exp)
                    act.wait_ge(seg_done, n + 1)
                    for b in range(2):
                        i = nc.scalar.activation(dec[0:r, 3 * b:3 * b + 3, 0:r],
                                                 psG[0:r, b, 0:384].rearrange("p (h c) -> p h c", c=P)[:, :, 0:r],
                                                 ACT.Exp)
                    i.then_inc(exp_done, 1)

            h_take(0, 0)
            act.wait_ge(consts_in, 16 * N_CONST)
            nc.scalar.activation(a_neg[:, :], a_neg[:, :], ACT.Exp).then_inc(a_exp, 1)

            def slab(s):
                first = isinstance(s, int) and s == 0
                last = isinstance(s, int) and s == LAST
                w, r = width(s), rows(s)
                for i in range(NCH):
                    n = group0(s) + i
                    src = pp[:, i % 2, 0:w]
                    if i < 2:
                        if i == 0 and not first:
                            act.wait_ge(pool_done, s)
                            if last:
                                act.wait_ge(end_out, 16 * (2 + CB_))
                        take(n, uT[:, i, PHIST:PHIST + w], src)
                    elif i < 5:
                        if i == 2 and not first:
                            act.wait_ge(q_out, 16 * 3 * s)
                        take(n, qs[:, i - 2, 0:w], src, scale=HD ** -0.5)
                    else:
                        if i == 5 and not first:
                            act.wait_ge(conv_done, s)
                        take(n, xr[:, i - 5, CHIST:CHIST + w], src)
                    if not first:
                        scan(s - 1, i)
                if not first:
                    act.wait_ge(kv_out, 16 * 4 * s)
                    act.wait_ge(y_done, chunk_no(s, 0))
                for j in range(tiles(s)):
                    for u in range(TG):
                        i = j * TG + u
                        take(g_tok(s) + i, tk[0:r, j, u * TGW:(u + 1) * TGW], pp[0:r, i % 2, 0:TGW])
                if not first:
                    act.wait_ge(kt_out, 16 * 3 * s)
                for j in range(tiles(s)):
                    i = tiles(s) * TG + j
                    take(g_kt(s) + j, ks[:, :, j * P:j * P + r],
                         pp[:, i % 2, 0:384].rearrange("p (b c) -> p b c", c=P)[:, :, 0:r])
                if not last:
                    h_take(s + 1, g_next(s))
                act.wait_ge(sp_ready, s + 1)
                nc.scalar.activation(spe[0:r, 0:tiles(s), :], spa[0:r, 0:tiles(s), :], ACT.Exp,
                                     scale=-1.0).then_inc(sp_exp, 1)
                act.wait_ge(sp_one, s + 1)
                nc.scalar.activation(spl[0:r, 0:tiles(s), :], spw[0:r, 0:tiles(s), :], ACT.Ln).then_inc(sp_ln, 1)
                act.wait_ge(evac, g_tok(s) + TG * tiles(s))
                nc.scalar.activation(tk[0:r, 0:tiles(s), T_Z:T_DT], tk[0:r, 0:tiles(s), T_Z:T_DT],
                                     ACT.Silu).then_inc(silu_done, 1)
                act.wait_ge(conv_done, s + 1)
                nc.scalar.activation(cv[:, :, 0:w], cv[:, :, 0:w], ACT.Silu).then_inc(silu_done, 1)

            program(slab, act)
            scan(LAST, 0)
            for i in range(2):
                act.wait_ge(st_t, 2 + i)
                if i:
                    act.wait_ge(st_rows, 2)
                nc.scalar.activation(stin[:, :, :], psT[:, 0, 0:384].rearrange("p (b c) -> p b c", c=P),
                                     ACT.Copy).then_inc(st_rows, 1)

        @block.vector
        def _(dve):
            ch = Chain(dve, dve_chain)
            v = nc.vector

            def norm(s, j):
                r, n = rows(s), s * 2 + j
                dve.wait_ge(x_in[j], 16 * (s + 1))
                x = xb[0:r, j, :]
                for u in range(2):
                    ch.done(v.bn_stats(stats[0:r, u, :], x[:, u * 512:(u + 1) * 512]))
                ch.wait()
                v.memset(idle[:, :], 0.0)
                ch.step(v.bn_aggr(mv[0:r, :], stats[0:r, :, :]))
                v.tensor_scalar(mv[0:r, 1:2], mv[0:r, 1:2], EPS, None, ALU.add).then_inc(moments, 1)
                dve.wait_ge(rstd_done, n + 1)
                ch.step(v.tensor_scalar(x, x, mv[0:r, 0:1], rstd[0:r, 0:1], ALU.subtract, ALU.mult))
                ch.step(v.tensor_tensor(x, x, lng[0:r, :], ALU.mult))
                v.tensor_tensor(x, x, lnb[0:r, :], ALU.add).then_inc(h_done, 1)

            def scan_0(q, c):
                r = rows(q)
                dve.wait_ge(dt_done, q + 1)
                v.tensor_tensor(amask[0:r, :, 0:r], after[0:r, 0:r].unsqueeze(1).broadcast_to([r, SH, r]),
                                dta[0:r, c, :].unsqueeze(2).broadcast_to([r, SH, r]),
                                ALU.mult).then_inc(amask_done, 1)

            def heads(ap, r):
                return ap.unsqueeze(2).broadcast_to([r, SH, HD])

            def by_head(ap):
                return ap.rearrange("p (h c) -> p h c", c=HD)

            def scan_b(q, c):
                r, n = rows(q), chunk_no(q, c)
                dve.wait_ge(exp_done, n + 1)
                ch.done(v.tensor_copy(xt[0:r, :], psT[0:r, 0, 0:384]))
                ch.done(v.tensor_tensor(w6[0:r, :], ex[0:r, 6:12], spl[0:r, c, 6:12], ALU.mult))
                ch.done(v.tensor_tensor(cbm[0:r, :, 0:r], psC[0:r, 0:256].rearrange("p (g c) -> p g c", c=P)[:, :, 0:r],
                                        upto[0:r, 0:r].unsqueeze(1).broadcast_to([r, SG, r]), ALU.mult))
                ch.wait()
                ch.done(v.tensor_copy(bt[0:r, :], psT[0:r, 1, 0:256]))
                ch.done(v.tensor_tensor(by_head(xdt[0:r, :]), by_head(xt[0:r, :]), heads(spl[0:r, c, 6:12], r), ALU.mult))
                ch.done(v.tensor_tensor(by_head(xw[0:r, :]), by_head(xt[0:r, :]), heads(w6[0:r, :], r), ALU.mult))
                ch.done(v.tensor_tensor(by_head(ya[0:r, :]), by_head(psY[0:r, 0:384]), heads(ex[0:r, 0:6], r), ALU.mult))
                for g in range(SG):
                    e = dec[0:r, 3 * g:3 * g + 3, 0:r]
                    ch.done(v.tensor_tensor(e, e, cbm[0:r, g, 0:r].unsqueeze(1).broadcast_to([r, SR, r]), ALU.mult))
                ch.wait()
                v.tensor_tensor(by_head(yb[0:r, :]), by_head(xt[0:r, :]), heads(dsk[0:r, :], r),
                                ALU.mult).then_inc(mix_ready, 1)

            def scan_c(q, c):
                r, n = rows(q), chunk_no(q, c)
                sample = isinstance(q, int) and q == LAST
                st = state[1 if sample else 0]
                dve.wait_ge(mix_ready, n + 1)
                if not (isinstance(q, int) and q == 0 and c == 0):
                    dve.wait_ge(chunk_done, n)
                ch.done(v.tensor_tensor(ya[0:r, :], ya[0:r, :], yb[0:r, :], ALU.add))
                ch.done(v.tensor_tensor(by_head(st[:, :]), by_head(st[:, :]), heads(ex[:, 12:18], P), ALU.mult))
                dve.wait_ge(mix_done, n + 1)
                ch.wait()
                ch.done(v.tensor_tensor(ya[0:r, :], ya[0:r, :], psY[0:r, 0:384], ALU.add))
                v.tensor_tensor(st[:, :], st[:, :], psT[:, 0, 0:384], ALU.add).then_inc(chunk_done, 1)
                ch.wait()
                ch.step(v.tensor_tensor(ya[0:r, :], ya[0:r, :], tk[0:r, c, T_Z:T_DT], ALU.mult))
                for g in range(SG):
                    ch.done(v.tensor_tensor_reduce(yb[0:r, g * 192:(g + 1) * 192], ya[0:r, g * 192:(g + 1) * 192],
                                                   ya[0:r, g * 192:(g + 1) * 192], 1.0, 0.0, ALU.mult, ALU.add,
                                                   ssum[0:r, g:g + 1]))
                ch.wait()
                v.tensor_scalar(ssum[0:r, :], ssum[0:r, :], 1.0 / 192, EPS, ALU.mult, ALU.add).then_inc(ss_done, 1)
                dve.wait_ge(rr_done, n + 1)
                if not (isinstance(q, int) and q == 0 and c == 0):
                    dve.wait_ge(y_out, 16 * n)
                for g in range(SG):
                    a, b = g * 192, (g + 1) * 192
                    i = v.scalar_tensor_tensor(yo[0:r, a:b], ya[0:r, a:b], rr[0:r, g:g + 1], gnorm[0:r, a:b],
                                               ALU.mult, ALU.mult)
                i.then_inc(y_done, 1)

            def convolve(s):
                w = width(s)
                keep = not (isinstance(s, int) and s >= LAST - 1)
                dve.wait_ge(evac, g_tok(s))
                if not (isinstance(s, int) and s == 0):
                    dve.wait_ge(conv_done, s)
                if isinstance(s, int) and s == LAST:
                    dve.wait_ge(hist_in, 16 * (2 + CB_))
                for t in range(4):
                    for b in range(CB_):
                        x = xr[:, b, t:t + w]
                        if t == 0:
                            i = v.tensor_scalar(cv[:, b, 0:w], x, cw[:, 0, b:b + 1], cbias[:, b:b + 1],
                                                ALU.mult, ALU.add)
                        else:
                            i = v.scalar_tensor_tensor(cv[:, b, 0:w], x, cw[:, t, b:b + 1], cv[:, b, 0:w],
                                                       ALU.mult, ALU.add)
                        if t == 3 and b == CB_ - 1 and not keep:
                            i.then_inc(conv_done, 1)
                        else:
                            ch.done(i)
                    if t < 3:
                        ch.wait()
                if keep:
                    v.tensor_copy(xr[:, :, 0:CHIST], xr[:, :, w:w + CHIST]).then_inc(conv_done, 1)

            def pool_mix(s):
                w = width(s)
                keep = not (isinstance(s, int) and s >= LAST - 1)
                if not (isinstance(s, int) and s == 0):
                    dve.wait_ge(pool_done, s)
                n = PHIST + w
                lo = 1
                src = uT
                for i, step in enumerate((1, 2, 4, 8)):
                    ch.step(v.tensor_tensor(win[i][:, :, lo:n], src[:, :, lo:n], src[:, :, lo - step:n - step], ALU.add))
                    src, lo = win[i], lo + 2 * step
                for g, wd in enumerate(WINDOWS):
                    a, b = 64 * (g % 2), g // 2
                    i = v.scalar_tensor_tensor(pd[a:a + 64, b, 0:w], win[g][a:a + 64, b, PHIST:n], 1.0 / wd,
                                               uT[a:a + 64, b, PHIST:n], ALU.mult, ALU.subtract)
                    if g == 3 and not keep:
                        i.then_inc(pool_done, 1)
                    else:
                        ch.done(i)
                if isinstance(s, int) and s == 0:
                    ch.wait()
                    for g in range(4):
                        a, b = 64 * (g % 2), g // 2
                        ch.step(v.tensor_tensor(pd[a:a + 64, b, 0:16], win[g][a:a + 64, b, PHIST:PHIST + 16],
                                                inv[a:a + 64, b, :], ALU.mult))
                        ch.step(v.tensor_tensor(pd[a:a + 64, b, 0:16], pd[a:a + 64, b, 0:16],
                                                uT[a:a + 64, b, PHIST:PHIST + 16], ALU.subtract))
                if keep:
                    v.tensor_copy(uT[:, :, 0:PHIST], uT[:, :, w:n]).then_inc(pool_done, 1)

            def pool_take(s):
                r = rows(s)
                if not (isinstance(s, int) and s == 0):
                    dve.wait_ge(m_out, 16 * 2 * s)
                dve.wait_ge(pool_mm, s + 1)
                v.tensor_tensor(pm[0:r, 0:tiles(s), :], psT[0:r, 0:tiles(s), 0:256],
                                pscale[0:r, :].unsqueeze(1).broadcast_to([r, tiles(s), 256]),
                                ALU.mult).then_inc(pm_done, 1)

            def gates_0(s):
                r, m = rows(s), tiles(s)
                dve.wait_ge(evac, g_kt(s))
                f, d = tk[0:r, 0:m, T_F:T_Z], tk[0:r, 0:m, T_DT:TOKW]

                def rep(ap):
                    return ap[0:r, :].unsqueeze(1).broadcast_to([r, m, 6])
                ch.done(v.scalar_tensor_tensor(spy[0:r, 0:m, 0:6], f, -1.0, rep(bf), ALU.mult, ALU.subtract))
                ch.done(v.tensor_tensor(spy[0:r, 0:m, 6:12], d, rep(bdt), ALU.add))
                ch.wait()
                y = spy[0:r, 0:m, :]
                v.scalar_tensor_tensor(spa[0:r, 0:m, :], y, -1.0, y, ALU.mult, ALU.max).then_inc(sp_ready, 1)

            def gates_1(s):
                r, m = rows(s), tiles(s)
                dve.wait_ge(sp_exp, s + 1)
                v.tensor_scalar(spw[0:r, 0:m, :], spe[0:r, 0:m, :], 1.0, None, ALU.add).then_inc(sp_one, 1)

            def gates_2(s):
                r, m = rows(s), tiles(s)
                y, e, w, l, t = (a[0:r, 0:m, :] for a in (spy, spe, spw, spl, spr))
                dve.wait_ge(sp_one, s + 1)
                ch.step(v.scalar_tensor_tensor(t, w, -1.0, e, ALU.add, ALU.subtract))
                ch.done(v.reciprocal(e, w))
                ch.wait()
                ch.step(v.tensor_tensor(t, t, e, ALU.mult))
                dve.wait_ge(sp_ln, s + 1)
                ch.step(v.tensor_tensor(l, l, t, ALU.subtract))
                ch.step(v.scalar_tensor_tensor(l, y, 0.0, l, ALU.max, ALU.add))
                if not (isinstance(s, int) and s == 0):
                    dve.wait_ge(small_out, 16 * 2 * s)
                ch.step(v.tensor_scalar(logf[0:r, 0:m, :], l[:, :, 0:6], -1.0, None, ALU.mult))
                v.tensor_tensor(dta[0:r, 0:m, :], l[:, :, 6:12],
                                a_neg[0:r, :].unsqueeze(1).broadcast_to([r, m, 6]), ALU.mult).then_inc(dt_done, 1)

            v.memset(poolw[:, :, :], 0.0)
            v.memset(uT[:, :, 0:PHIST], 0.0)
            v.memset(xr[:, :, 0:CHIST], 0.0).then_inc(init_done, 1)
            v.memset(state[0][:, :], 0.0).then_inc(init_done, 1)
            dve.wait_ge(first_in, 16 * 3)
            for j in range(2):
                norm(0, j)
            dve.wait_ge(consts_in, 16 * N_CONST)
            dve.wait_ge(a_exp, 1)
            ch.step(v.tensor_scalar(a_neg[:, :], a_neg[:, :], -1.0, None, ALU.mult))
            dve.wait_ge(st_t, 1)
            v.tensor_copy(state[1][:, :], psT[:, 0, 0:384]).then_inc(init_done, 1)

            def slab(s):
                first = isinstance(s, int) and s == 0
                last = isinstance(s, int) and s == LAST
                if first:
                    for j in range(2):
                        norm(1, j)
                else:
                    for c in range(tiles(s - 1)):
                        scan_0(s - 1, c)
                        scan_b(s - 1, c)
                        scan_c(s - 1, c)
                        if not last and c < tiles(s + 1):
                            norm(s + 1, c)
                convolve(s)
                pool_mix(s)
                pool_take(s)
                gates_0(s)
                gates_1(s)
                gates_2(s)

            program(slab, dve, ch, STEPS_1)
            scan_0(LAST, 0)
            scan_b(LAST, 0)
            scan_c(LAST, 0)


STEPS_1 = 84


KEYS_S = PAST + DEC
QG = 4
GROUPS = SEQ // (QG * P)
KA = HD + 2
CT = SEQ // P + PAST // P + 1


def attention_constants():
    q, s = np.arange(P)[:, None], np.arange(P)[None, :]
    future = np.where(s > q, np.float32(-1e30), np.float32(0)).astype(np.float32)
    return {"c_future": future}


def attend(nc, sem, cache_k, cache_v, cache_logf, p_logf, s_logf, p_v, s_v, q_ch, k_ch, kc_ch, c_rows, cn_rows,
           c_square, c_future, mixed):
    NPAIR = FH // 2
    first_chunk = [sum(2 * NPAIR * QG * (g + 1) for g in range(G)) for G in range(GROUPS + 1)]
    UNITS = GROUPS * FH * QG

    with ExitStack() as ctx:
        def sb(name, shape, dt=F32):
            return ctx.enter_context(nc.sbuf_tensor(name, shape, dt))

        def ps(name, banks):
            return ctx.enter_context(nc.psum_tensor(name, [P, banks, 512], F32))

        square, future = sb("square2", [P, 4, P]), sb("future", [P, P])
        ident, upto, ones = square[:, 0, :], square[:, 1, :], square[:, 3, :]
        ident_h, future_h = sb("ident_h", [P, P], BF16), sb("future_h", [P, P], BF16)
        lf, carry, cc = sb("lf", [P, CT, FH]), sb("carry", [P, CT, FH]), sb("cc", [P, CT * FH])
        cT, cTn = sb("cT", [P, P]), sb("cTn", [P, P])
        ck, ckT = sb("ck", [P, 2, FOX_W]), sb("ckT", [P, 3, PAST])
        kx = sb("kx", [KA, FH, SEQ])
        kxs = sb("kxs", [KA, FH, KEYS_S])
        vx = sb("vx", [P, SEQ // P, FOX_W])
        vxs = sb("vxs", [P, 3, FOX_W])
        qa = [sb(f"qa{i}", [KA, QG * P]) for i in range(2)]
        qas = sb("qas", [KA, FH, DEC])
        prob = sb("prob", [P, 2, SEQ])
        pT = sb("pT", [P, 2, 512])
        ob = sb("ob", [P, 2, QG, FOX_W])
        mx, nmax = sb("mx", [P, 2, 4]), sb("nmax", [P, 2])
        rs, rsum, rinv = sb("rs", [P, 2, 4]), sb("rsum", [P, 2]), sb("rinv", [P, 2])
        S, T, O = ps("S", 4), ps("T", 2), ps("O", 2)

        const2, lf_in, ck_in = sem("const2_in"), sem("logf_in"), sem("cache_k_in")
        cleared, lf_clear = sem("rows_cleared"), sem("logf_cleared")
        c_mm, c_sum, c_tr, c_row, c_out = sem("c_mm"), sem("c_sum"), sem("c_transposed"), sem("c_rows"), sem("c_out")
        ck_tr, ck_ev, ck_out = sem("ck_tr"), sem("ck_ev"), sem("ck_out")
        kv_in = [sem(f"kv_group{g}_in") for g in range(GROUPS)]
        s_in = sem("sample_in")
        q_in = [sem(f"q{i}_in") for i in range(2)]
        qk, nm_done, exp_done = sem("qk_done"), sem("max_done"), sem("exp2_done")
        t_done, pv = sem("t_done"), sem("pv_done")
        t_taken = [sem(f"t{i}_taken") for i in range(2)]
        o_taken, o_out = sem("o_taken"), sem("o_stored")
        dve_chain, act_chain = sem("dve2_chain"), sem("act2_chain")
        block = ctx.enter_context(nc.Block())

        C_S, C_T, C_PV, C_O = 4, 1, 2, 2

        def unit(G, p, lu):
            return (G * NPAIR + p) * 2 * QG + lu

        def chunk(G, p, lu, c):
            return first_chunk[G] + p * (2 * QG * (G + 1)) + lu * (G + 1) + c

        def half_chunk(G, p, lu, c):
            return first_chunk[G] // 2 + p * (QG * (G + 1)) + (lu * (G + 1) + c) // 2

        def blocks(G, j, c):
            return QG if c < G else j + 1

        class U:

            def __init__(self, G, p, lu):
                self.prompt = True
                self.G, self.p, self.lu, self.j, self.hh = G, p, lu, lu % QG, lu // QG
                self.h = p * 2 + self.hh
                self.n, self.par, self.chunks, self.rows = unit(G, p, lu), lu % 2, G + 1, P
                self.ring = 4

            def X(self, c):
                return chunk(self.G, self.p, self.lu, c)

            def half(self, c):
                return half_chunk(self.G, self.p, self.lu, c)

            def bank(self, c):
                return (self.lu * (self.G + 1) + c) % 4

            def slot(self, c):
                return (self.lu * (self.G + 1) + c) % 2

            def keys(self, c):
                return P * blocks(self.G, self.j, c)

            def parts(self, c):
                return [(b, P) for b in range(blocks(self.G, self.j, c))]

        class US:

            def __init__(self, h):
                self.prompt = False
                self.h, self.n, self.par, self.chunks, self.rows = h, UNITS + h, h % 2, 1, DEC
                self.ring = 4

            def X(self, c):
                return first_chunk[GROUPS] + self.h

            def half(self, c):
                return (first_chunk[GROUPS] + self.h) // 2

            def bank(self, c):
                return self.h % 4

            def slot(self, c):
                return self.h % 2

            def keys(self, c):
                return KEYS_S

            def parts(self, c):
                return [(0, P), (1, P), (2, DEC)]

        def turns(eng, turn):
            for G in range(GROUPS):
                with eng.Fori(0, NPAIR) as p:
                    turn([U(G, p, lu) for lu in range(2 * QG)])
            turn([US(h) for h in range(FH)])

        def q_load(sp, G, p, hh):
            h = p * 2 + hh
            cview = c_rows.rearrange("(i h) t -> h i t", h=FH)
            sp.dma_start(qa[hh][0:HD, :], q_ch[bass.ds(h * HD, HD), G * 512:(G + 1) * 512]).then_inc(q_in[hh], 16)
            sp.dma_start(qa[hh][HD:HD + 1, :].rearrange("o (i t) -> o i t", t=P),
                         cview[bass.ds(h, 1), 4 * G:4 * G + 4, :]).then_inc(q_in[hh], 16)

        def take_chunk(eng, copy, u, c):
            slot, r = u.slot(c), u.rows
            eng.wait_ge(t_done, u.X(c) + 1)
            eng.wait_ge(pv, C_PV + u.X(c) - 2 + 1)
            parts = u.parts(c)
            if u.prompt:
                w = P * len(parts)
                copy(pT[:, slot, 0:w], T[:, slot, 0:w]).then_inc(t_taken[slot], 1)
            else:
                copy(pT[:, slot, 0:256].rearrange("p (b r) -> p b r", b=2)[:, :, 0:r],
                     T[:, slot, 0:256].rearrange("p (b r) -> p b r", b=2)[:, :, 0:r])
                copy(pT[0:DEC, slot, 256:256 + r], T[0:DEC, slot, 256:256 + r]).then_inc(t_taken[slot], 1)

        @block.sync
        def _(sp):
            sp.dma_start(square[:, :, :], c_square).then_inc(const2, 16)
            sp.dma_start(future[:, :], c_future).then_inc(const2, 16)
            sp.wait_ge(lf_clear, 1)
            sp.dma_start(lf[:, 0:16, :], p_logf.rearrange("(i p) h -> p i h", p=P)).then_inc(lf_in, 16)
            sp.dma_start(lf[:, 16:18, :], cache_logf.rearrange("(i p) h -> p i h", p=P)).then_inc(lf_in, 16)
            sp.dma_start(lf[0:DEC, 18, :], s_logf).then_inc(lf_in, 16)
            sp.dma_start(ck[:, :, :], cache_k.rearrange("(i p) c -> p i c", p=P)).then_inc(ck_in, 16)
            kview = k_ch.rearrange("(h d) t -> d h t", d=HD)
            cview, nview = (a.rearrange("(i h) t -> h i t", h=FH) for a in (c_rows, cn_rows))

            def kv(G):
                t = slice(G * 512, (G + 1) * 512)
                sp.dma_start(kx[0:HD, :, t], kview[:, :, t]).then_inc(kv_in[G], 16)
                sp.dma_start(vx[:, 4 * G:4 * G + 4, :],
                             p_v[t, :].rearrange("(i p) c -> p i c", p=P)).then_inc(kv_in[G], 16)

            kv(0)
            sp.wait_ge(c_row, 2)
            sp.dma_start(c_rows, cT[0:CT * FH, :]).then_inc(c_out, 16)
            sp.dma_start(cn_rows, cTn[0:CT * FH, :]).then_inc(c_out, 16)
            sp.wait_ge(c_out, 32)
            sp.wait_ge(cleared, 2)
            for G in range(GROUPS):
                if G:
                    kv(G)
                for h in range(FH):
                    sp.dma_start(kx[HD + 1:KA, h, G * 512:(G + 1) * 512].rearrange("o (i t) -> o i t", t=P),
                                 nview[h:h + 1, 4 * G:4 * G + 4, :]).then_inc(kv_in[G], 16)
                if G == 0:
                    for hh in range(2):
                        q_load(sp, 0, 0, hh)
            sp.wait_ge(ck_ev, 1)
            sp.dma_start(kc_ch.rearrange("(b p) t -> p b t", p=P), ckT[:, :, :]).then_inc(ck_out, 16)
            sp.wait_ge(ck_out, 16)
            sp.dma_start(kxs[0:HD, :, 0:PAST], kc_ch.rearrange("(h d) t -> d h t", d=HD)).then_inc(s_in, 16)
            sp.dma_start(kxs[0:HD, :, PAST:], kview[:, :, SEQ:TOKENS]).then_inc(s_in, 16)
            for h in range(FH):
                sp.dma_start(kxs[HD + 1:KA, h, 0:PAST].rearrange("o (i t) -> o i t", t=P),
                             nview[h:h + 1, 16:18, :]).then_inc(s_in, 16)
                sp.dma_start(kxs[HD + 1:KA, h, PAST:], nview[h:h + 1, 18, 0:DEC]).then_inc(s_in, 16)
                sp.dma_start(qas[HD:HD + 1, h, :], cview[h:h + 1, 18, 0:DEC]).then_inc(s_in, 16)
            sp.dma_start(qas[0:HD, :, :],
                         q_ch.rearrange("(h d) t -> d h t", d=HD)[:, :, SEQ:TOKENS]).then_inc(s_in, 16)
            sp.dma_start(vxs[:, 0:2, :], cache_v.rearrange("(i p) c -> p i c", p=P)).then_inc(s_in, 16)
            sp.dma_start(vxs[0:DEC, 2, :], s_v).then_inc(s_in, 16)

            for G in range(GROUPS):
                if G:
                    for hh in range(2):
                        sp.wait_ge(qk, first_chunk[G] - (1 - hh) * QG * G)
                        q_load(sp, G, 0, hh)
                with sp.Fori(1, NPAIR) as p:
                    for hh in range(2):
                        sp.wait_ge(qk, chunk(G, p, 0, 0) - (1 - hh) * QG * (G + 1))
                        q_load(sp, G, p, hh)
                sp.wait_ge(o_taken, C_O + unit(G + 1, 0, 0))
                sp.dma_start(mixed[G * 512:(G + 1) * 512, MIX_FOX:MIX_SSD].rearrange("(i p) c -> p i c", p=P),
                             ob[:, G % 2, :, :]).then_inc(o_out, 16)
            sp.wait_ge(o_taken, C_O + UNITS + FH)
            sp.dma_start(mixed[SEQ:TOKENS, MIX_FOX:MIX_SSD], ob[0:DEC, 0, 0, :]).then_inc(o_out, 16)
            sp.wait_ge(o_out, 16 * (GROUPS + 1))

        @block.gpsimd
        def _(pool):
            nc.gpsimd.memset(kx[HD:KA, :, :], 1.0).then_inc(cleared, 1)

        @block.tensor
        def _(pe):
            pe.sem_inc(pv, C_PV)
            pe.wait_ge(const2, 32)
            pe.wait_ge(lf_in, 48)
            lff = lf[:, :, :].rearrange("p i h -> p (i h)")
            pe.matmul(S[:, 0, 0:CT * FH], upto, lff, start=True, stop=True)
            pe.matmul(S[:, 1, 0:CT * FH], ones, lff, start=True, stop=True).then_inc(c_mm, 1)
            pe.wait_ge(ck_in, 16)
            for i in range(2):
                for b in range(3):
                    mm = pe.transpose(T[:, i, b * P:(b + 1) * P], ck[:, i, b * P:(b + 1) * P], ident)
            mm.then_inc(ck_tr, 1)
            pe.wait_ge(c_sum, 1)
            pe.transpose(S[0:CT * FH, 2, 0:P], cc[:, :], ident).then_inc(c_tr, 1)
            pe.wait_ge(ck_ev, 1)
            pe.wait_ge(c_row, 2)
            pe.wait_ge(cleared, 2)

            def scores(u):
                if u.prompt:
                    if u.j == 0:
                        pe.wait_ge(q_in[u.hh], 32 * (u.G * NPAIR + u.p + 1))
                    if u.lu == 0:
                        pe.wait_ge(kv_in[u.G], 16 * (2 + FH))
                elif u.h == 0:
                    pe.wait_ge(s_in, 16 * (2 + 3 * FH + 3))
                r = u.rows
                for c in range(u.chunks):
                    pe.wait_ge(exp_done, C_S + u.X(c) - u.ring + 1)
                    w = u.keys(c)
                    out = S[0:r, u.bank(c), :]
                    if u.prompt:
                        lhs = qa[u.hh][:, u.j * P:(u.j + 1) * P]

                        def keys(a, b):
                            return kx[:, u.h, c * 512 + a:c * 512 + b]
                    else:
                        lhs = qas[:, u.h, :]

                        def keys(a, b):
                            return kxs[:, u.h, a:b]
                    if c < u.chunks - 1:
                        mm = pe.matmul(out[:, 0:w], lhs, keys(0, w), start=True, stop=True)
                    else:
                        d = w - r
                        if d:
                            pe.matmul(out[:, 0:d], lhs, keys(0, d), start=True, stop=True)
                        pe.matmul(out[:, d:w], lhs, keys(d, w), start=True, stop=False)
                        mm = pe.matmul(out[:, d:w], ident_h[0:r, 0:r], future_h[0:r, 0:r], start=False, stop=True)
                    mm.then_inc(qk, 1)

            def turn_over(u, c):
                pe.wait_ge(t_taken[u.slot(c)], C_T + u.half(c))
                pe.wait_ge(exp_done, C_S + u.X(c) + 1)
                r = u.rows
                for b, w in u.parts(c):
                    mm = pe.transpose(T[0:w, u.slot(c), b * P:b * P + r],
                                      prob[0:r, u.par, c * 512 + b * P:c * 512 + b * P + w], ident[0:r, 0:r])
                mm.then_inc(t_done, 1)

            def weigh(u, c):
                if c == 0:
                    pe.wait_ge(o_taken, C_O + u.n - 2 + 1)
                pe.wait_ge(t_taken[u.slot(c)], C_T + u.half(c) + 1)
                parts = u.parts(c)
                r = u.rows
                for b, w in parts:
                    v = vx[:, 4 * c + b, bass.ds(u.h * HD, HD)] if u.prompt else vxs[0:w, b, u.h * HD:(u.h + 1) * HD]
                    mm = pe.matmul(O[0:r, u.par, 0:HD], pT[0:w, u.slot(c), b * P:b * P + r], v,
                                   start=(c == 0 and b == 0), stop=(c == u.chunks - 1 and b == parts[-1][0]))
                mm.then_inc(pv, 1)

            def values(u):
                turn_over(u, 0)
                for c in range(u.chunks):
                    if c + 1 < u.chunks:
                        turn_over(u, c + 1)
                    weigh(u, c)

            def turn(us):
                scores(us[0])
                for a, b in zip(us, us[1:] + [None]):
                    if b:
                        scores(b)
                    values(a)

            turns(pe, turn)

        @block.scalar
        def _(act):
            act.sem_inc(exp_done, C_S)
            act.sem_inc(t_taken[1], C_T)
            act.wait_ge(ck_tr, 1)
            nc.scalar.activation(ckT[:, :, :].rearrange("p b (i t) -> p i b t", i=2),
                                 T[:, :, 0:384].rearrange("p i (b t) -> p i b t", b=3), ACT.Copy).then_inc(ck_ev, 1)
            act.wait_ge(c_tr, 1)
            nc.scalar.activation(cT[0:CT * FH, :], S[0:CT * FH, 2, 0:P], ACT.Copy).then_inc(c_row, 1)
            nc.scalar.activation(cTn[0:CT * FH, :], S[0:CT * FH, 2, 0:P], ACT.Copy, scale=-1.0).then_inc(c_row, 1)

            def exps(u):
                act.wait_ge(nm_done, u.n + 1)
                act.wait_ge(o_taken, C_O + u.n - 2 + 1)
                r = u.rows
                for c in range(u.chunks):
                    w = u.keys(c)
                    nc.scalar.activation(prob[0:r, u.par, c * 512:c * 512 + w], S[0:r, u.bank(c), 0:w], ACT.Exp,
                                         bias=nmax[0:r, u.par:u.par + 1],
                                         accum_out=rs[0:r, u.par, c:c + 1]).then_inc(exp_done, 1)

            def takes(u):
                for c in range(u.chunks):
                    if u.slot(c) == 1:
                        take_chunk(act, nc.scalar.copy, u, c)

            def turn(us):
                exps(us[0])
                for a, b in zip(us, us[1:] + [None]):
                    takes(a)
                    if b:
                        exps(b)

            turns(act, turn)

        @block.vector
        def _(dve):
            ch = Chain(dve, dve_chain)
            v = nc.vector
            dve.sem_inc(t_taken[0], C_T)
            dve.sem_inc(o_taken, C_O)
            v.memset(lf[:, :, :], 0.0).then_inc(lf_clear, 1)
            ch.done(v.memset(carry[:, :, :], 0.0))
            for i in range(2):
                v.memset(qa[i][HD:KA, :], 1.0)
            v.memset(qas[HD:KA, :, :], 1.0)
            v.memset(kxs[HD:KA, :, :], 1.0)
            dve.wait_ge(const2, 32)
            v.tensor_copy(ident_h[:, :], ident)
            v.tensor_copy(future_h[:, :], future[:, :]).then_inc(cleared, 1)
            dve.wait_ge(c_mm, 1)
            ch.wait()
            tot = S[:, 1, 0:CT * FH].rearrange("p (i h) -> p i h", h=FH)
            for i in range(1, CT):
                if i != SEQ // P:
                    ch.step(v.tensor_tensor(carry[:, i, :], carry[:, i - 1, :], tot[:, i - 1, :], ALU.add))
            v.tensor_tensor(cc[:, :], S[:, 0, 0:CT * FH], carry[:, :, :].rearrange("p i h -> p (i h)"),
                            ALU.add).then_inc(c_sum, 1)

            def maxima(u):
                r = u.rows
                for c in range(u.chunks):
                    dve.wait_ge(qk, u.X(c) + 1)
                    src = S[0:r, u.bank(c), 0:u.keys(c)]
                    if u.chunks == 1:
                        v.tensor_reduce(nmax[0:r, u.par:u.par + 1], src, AX.X, ALU.max,
                                        negate=True).then_inc(nm_done, 1)
                    else:
                        ch.done(v.tensor_reduce(mx[0:r, u.par, c:c + 1], src, AX.X, ALU.max))
                if u.chunks > 1:
                    ch.wait()
                    v.tensor_reduce(nmax[0:r, u.par:u.par + 1], mx[0:r, u.par, 0:u.chunks], AX.X, ALU.max,
                                    negate=True).then_inc(nm_done, 1)

            def takes(u):
                for c in range(u.chunks):
                    if u.slot(c) == 0:
                        take_chunk(dve, v.tensor_copy, u, c)

            def output(u):
                r, k = u.rows, u.par
                dve.wait_ge(pv, C_PV + u.X(u.chunks - 1) + 1)
                if u.chunks > 1:
                    ch.step(v.tensor_reduce(rsum[0:r, k:k + 1], rs[0:r, k, 0:u.chunks], AX.X, ALU.add))
                    total = rsum[0:r, k:k + 1]
                else:
                    total = rs[0:r, k, 0:1]
                ch.step(v.reciprocal(rinv[0:r, k:k + 1], total))
                if u.prompt:
                    dst = ob[:, u.G % 2, u.j, bass.ds(u.h * HD, HD)]
                else:
                    dst = ob[0:r, 0, 0, u.h * HD:(u.h + 1) * HD]
                v.tensor_scalar(dst, O[0:r, k, 0:HD], rinv[0:r, k:k + 1], None, ALU.mult).then_inc(o_taken, 1)

            def turn(us):
                if us[0].prompt and us[0].G >= 2:
                    dve.wait_ge(o_out, 16 * (us[0].G - 1))
                if not us[0].prompt:
                    dve.wait_ge(o_out, 16 * (GROUPS - 1))
                maxima(us[0])
                for i, u in enumerate(us):
                    if i + 1 < len(us):
                        maxima(us[i + 1])
                    takes(u)
                    if i:
                        output(us[i - 1])
                output(us[-1])

            for G in range(GROUPS):
                with dve.Fori(0, NPAIR) as p:
                    ch.enter(p, 0, STEPS_2[G])
                    turn([U(G, p, lu) for lu in range(2 * QG)])
                ch.leave(NPAIR)
            turn([US(h) for h in range(FH)])


STEPS_2 = [8, 32, 40, 48]


def split_view(t):
    return t.bitcast(F32)


class Twice:

    def __init__(self, r, c=None):
        self.r, self.c = (0, r) if c is None else (r, c)
        self.n = self.r * 2 + self.c
        self.half = self.r + self.c // 2
        self.odd = self.c % 2

    def __add__(self, d):
        return Twice(self.r, self.c + d)

    def under(self, n):
        return isinstance(self.r, int) and self.n < n

    def over(self, n):
        return isinstance(self.r, int) and self.n >= n


def mix_out(nc, sem, w_out, ln_g, ln_b, mixed, h_rows, c_square, h2_ch):
    TILES = SEQ // P + 1
    LAST = TILES - 1

    def rows(i):
        return DEC if i.over(LAST) else P

    with ExitStack() as ctx:
        def sb(name, shape, dt=F32):
            return ctx.enter_context(nc.sbuf_tensor(name, shape, dt))

        def ps(name):
            return ctx.enter_context(nc.psum_tensor(name, [P, 2, 512], F32))

        ident = sb("ident3", [P, P])
        lng, lnb = sb("lng3", [P, D]), sb("lnb3", [P, D])
        w_raw = sb("wo_raw", [P, KT, D])
        w_hi, w_lo = sb("wo_hi", [P, KT, D], F32R), sb("wo_lo", [P, KT, D], F32R)
        half, idle = sb("half3", [P, 1]), sb("idle3", [1, 1])
        mrow = [sb(f"mrow{i}", [P, D]) for i in range(2)]
        hrow = [sb(f"hrow{i}", [P, D]) for i in range(2)]
        m_hi = [sb(f"m_hi{i}", [P, KT, P], F32R) for i in range(2)]
        m_lo = [sb(f"m_lo{i}", [P, KT, P], F32R) for i in range(2)]
        stats, mv, rstd = sb("stats3", [P, 2, 6]), sb("mv3", [P, 2]), sb("rstd3", [P, 1])
        hT = [sb(f"h2T{i}", [P, KT, P]) for i in range(2)]
        A, B = ps("A"), ps("B")
        Y = [ps(f"Y{i}") for i in range(2)]

        const_in, w_in = sem("const3_in"), [sem(f"wo{i}_in") for i in range(KT // 2)]
        w_hi_done, w_lo_done, half_done = sem("wo_hi_done"), sem("wo_lo_done"), sem("half3_done")
        m_in, h_in = [sem(f"mixed{i}_in") for i in range(2)], [sem(f"h{i}_in") for i in range(2)]
        a_tr, a_hi, a_lo = sem("mixed_transposed"), sem("mixed_hi"), sem("mixed_lo")
        y_mm, y_sum = sem("y_mm"), sem("y_summed")
        moments, rstd_done, h2_done = sem("moments3"), sem("rstd3_done"), sem("h2_done")
        b_tr, b_take, h2_out = sem("h2_transposed"), sem("h2_taken"), [sem(f"h2_stored{i}") for i in range(2)]
        dve_chain = sem("dve3_chain")
        block = ctx.enter_context(nc.Block())

        def program(body, eng, chain=None, steps=0):
            body(Twice(0))
            with eng.Fori(0, (TILES - 5) // 2) as t:
                if chain:
                    chain.enter(t, 0, steps)
                for u in range(2):
                    body(Twice(t, 1 + u))
            if chain:
                chain.leave((TILES - 5) // 2)
            for i in range(TILES - 4, TILES):
                body(Twice(i))

        @block.sync
        def _(sp):
            sp.dma_start(ident[:, :], c_square[:, 0, :]).then_inc(const_in, 16)

            def m_load(i):
                r = rows(i)
                if not i.under(2):
                    sp.wait_ge(a_tr, i.n - 1)
                sp.dma_start(mrow[i.odd][0:r, :], mixed[bass.ds(i.n * P, r), :]).then_inc(m_in[i.odd], 16)

            def h_load(i):
                r = rows(i)
                if not i.under(2):
                    sp.wait_ge(b_tr, i.n - 1)
                sp.dma_start(hrow[i.odd][0:r, :], h_rows[bass.ds(i.n * P, r), :]).then_inc(h_in[i.odd], 16)

            m_load(Twice(0))
            for k in range(KT // 2):
                sp.dma_start(w_raw[:, 2 * k:2 * k + 2, :], w_out.rearrange("(k p) n -> p k n", p=P)[:, 2 * k:2 * k + 2, :]
                             ).then_inc(w_in[k], 16)
                if k == 0:
                    m_load(Twice(1))
                    h_load(Twice(0))
            sp.dma_start(lng[:, :], load_rows(ln_g)).then_inc(const_in, 16)
            sp.dma_start(lnb[:, :], load_rows(ln_b)).then_inc(const_in, 16)

            def body(i):
                if not i.over(LAST - 1):
                    m_load(i + 2)
                if not i.over(LAST):
                    h_load(i + 1)

            program(body, sp)

        @block.gpsimd
        def _(pool):
            nc.gpsimd.memset(half[:, :], -0.5).then_inc(half_done, 1)
            pool.wait_ge(half_done, 1)

            def body(i):
                pool.wait_ge(moments, i.n + 1)
                nc.gpsimd.tensor_tensor(rstd[0:rows(i), :], mv[0:rows(i), 1:2], half[0:rows(i), :],
                                        ALU.pow).then_inc(rstd_done, 1)

            program(body, pool)

        @block.tensor
        def _(pe):
            pe.wait_ge(const_in, 16)

            def over(dst, src, r):
                for b in range(KT):
                    mm = pe.transpose(dst[:, b // 4, (b % 4) * P:(b % 4) * P + r], src[0:r, b * P:(b + 1) * P],
                                      ident[0:r, 0:r])
                return mm

            def mixed_over(i):
                pe.wait_ge(m_in[i.odd], 16 * (i.half + 1))
                if not i.under(1):
                    pe.wait_ge(a_lo, i.n)
                over(A, mrow[i.odd], rows(i)).then_inc(a_tr, 1)

            def h2_over(i):
                pe.wait_ge(h2_done, i.n + 1)
                if not i.under(1):
                    pe.wait_ge(b_take, i.n)
                over(B, hrow[i.odd], rows(i)).then_inc(b_tr, 1)

            def body(i):
                k = i.odd
                if not i.over(LAST):
                    mixed_over(i + 1)
                pe.wait_ge(a_lo, i.n + 1)
                if not i.under(2):
                    pe.wait_ge(y_sum, i.n - 1)
                for n in range(2):
                    for b in range(KT):
                        if i.under(1) and n == 0:
                            pe.wait_ge(w_lo_done, b + 1)
                        for m, (x, w) in enumerate(((m_hi, w_hi), (m_hi, w_lo), (m_lo, w_hi))):
                            mm = pe.matmul(Y[k][:, n, :], x[k][:, b, :], w[:, b, n * 512:(n + 1) * 512],
                                           start=(b == 0 and m == 0), stop=(b == KT - 1 and m == 2))
                mm.then_inc(y_mm, 1)
                if not i.under(1):
                    h2_over(i + -1)

            mixed_over(Twice(0))
            program(body, pe)
            h2_over(Twice(LAST))

        @block.scalar
        def _(act):
            def tiled(ap, r):
                return ap[:, :, :].rearrange("p n (b c) -> p (n b) c", c=P)[:, :, 0:r]

            def hi(i):
                r = rows(i)
                act.wait_ge(a_tr, i.n + 1)
                if not i.under(2):
                    act.wait_ge(y_mm, i.n - 1)
                nc.scalar.activation(m_hi[i.odd][:, :, 0:r], tiled(A, r), ACT.Copy).then_inc(a_hi, 1)

            def take(i):
                r = rows(i)
                act.wait_ge(b_tr, i.n + 1)
                if not i.under(2):
                    act.wait_ge(h2_out[i.odd], 16 * i.half)
                nc.scalar.activation(hT[i.odd][:, :, 0:r], tiled(B, r), ACT.Copy).then_inc(b_take, 1)
                act.wait_ge(b_take, i.n + 1)
                act.dma_start(h2_ch.rearrange("(k p) t -> p k t", p=P)[:, :, bass.ds(i.n * P, r)],
                              hT[i.odd][:, :, 0:r]).then_inc(h2_out[i.odd], 16)

            def body(i):
                if not i.over(LAST):
                    hi(i + 1)
                if not i.under(1):
                    take(i + -1)

            hi(Twice(0))
            for k in range(KT):
                if k % 2 == 0:
                    act.wait_ge(w_in[k // 2], 16)
                nc.scalar.activation(w_hi[:, k, :], w_raw[:, k, :], ACT.Copy).then_inc(w_hi_done, 1)
            program(body, act)
            take(Twice(LAST))
            act.wait_ge(h2_out[0], 16 * ((TILES + 1) // 2))
            act.wait_ge(h2_out[1], 16 * (TILES // 2))

        @block.vector
        def _(dve):
            ch = Chain(dve, dve_chain)
            v = nc.vector

            def lo(i):
                r, k = rows(i), i.odd
                dve.wait_ge(a_hi, i.n + 1)
                v.tensor_tensor(m_lo[k][:, :, 0:r], A[:, :, :].rearrange("p n (b c) -> p (n b) c", c=P)[:, :, 0:r],
                                split_view(m_hi[k][:, :, 0:r]), ALU.subtract).then_inc(a_lo, 1)

            def norm(i):
                r, k = rows(i), i.odd
                x = hrow[k][0:r, :]
                dve.wait_ge(h_in[k], 16 * (i.half + 1))
                dve.wait_ge(y_mm, i.n + 1)
                v.scalar_tensor_tensor(x, x, ALPHA, Y[k][0:r, :, :].rearrange("p n c -> p (n c)"),
                                       ALU.mult, ALU.add).then_inc(y_sum, 1)
                dve.wait_ge(y_sum, i.n + 1)
                for u in range(2):
                    ch.done(v.bn_stats(stats[0:r, u, :], x[:, u * 512:(u + 1) * 512]))
                ch.wait()
                v.memset(idle[:, :], 0.0)
                ch.step(v.bn_aggr(mv[0:r, :], stats[0:r, :, :]))
                v.tensor_scalar(mv[0:r, 1:2], mv[0:r, 1:2], EPS, None, ALU.add).then_inc(moments, 1)
                dve.wait_ge(rstd_done, i.n + 1)
                ch.step(v.tensor_scalar(x, x, mv[0:r, 0:1], rstd[0:r, 0:1], ALU.subtract, ALU.mult))
                ch.step(v.tensor_tensor(x, x, lng[0:r, :], ALU.mult))
                v.tensor_tensor(x, x, lnb[0:r, :], ALU.add).then_inc(h2_done, 1)

            def body(i):
                if not i.over(LAST):
                    lo(i + 1)
                norm(i)

            lo(Twice(0))
            for k in range(KT):
                dve.wait_ge(w_hi_done, k + 1)
                v.tensor_tensor(w_lo[:, k, :], w_raw[:, k, :], split_view(w_hi[:, k, :]),
                                ALU.subtract).then_inc(w_lo_done, 1)
            dve.wait_ge(const_in, 48)
            program(body, dve, ch, STEPS_3)


STEPS_3 = 10


def feed_forward(nc, sem, w_gate, w_up, w_down, ln_g, ln_b, h2_ch, c_square, y_prompt, y_sample):
    NB = 4
    W = TOKENS // NB
    H = W // 2
    FS = FT // 2
    UNITS = 2 * (FS + KT)
    NO = 5

    def row_tile(t, r):
        if isinstance(t, int) and t == NB - 1:
            return ((W - DEC) // 4 * r, (W - DEC) // 4) if r < NO - 1 else (W - DEC, DEC)
        a = -(-W // NO)
        return a * r, min(a, W - a * r)

    with ExitStack() as ctx:
        def sb(name, shape, dt=F32):
            return ctx.enter_context(nc.sbuf_tensor(name, shape, dt))

        ident = sb("ident4", [P, P])
        lng, lnb = sb("lng4", [P, D]), sb("lnb4", [P, D])
        half, idle = sb("half4", [P, 1]), sb("idle4", [1, 1])
        x_hi, x_lo = sb("x_hi", [P, KT, W], F32R), sb("x_lo", [P, KT, W], F32R)
        a_hi, a_lo = sb("act_hi", [P, FS, W], F32R), sb("act_lo", [P, FS, W], F32R)
        raw = [sb(f"w_raw{i}", [P, 2 * KT, P]) for i in range(2)]
        whi = [sb(f"w_hi{i}", [P, 2 * KT, P], F32R) for i in range(2)]
        wlo = [sb(f"w_lo{i}", [P, 2 * KT, P], F32R) for i in range(2)]
        sl = [sb(f"slice{i}", [P, W]) for i in range(2)]
        act_t = [sb(f"silu{i}", [P, H]) for i in range(2)]
        yT = sb("yT", [P, KT, W])
        ob = [sb(f"y_rows{i}", [P, D]) for i in range(2)]
        stats, mv, rstd = sb("stats4", [P, 2, 6]), sb("mv4", [P, 2]), sb("rstd4", [P, 1])
        G = [ctx.enter_context(nc.psum_tensor(f"G{i}", [P, 2, 512], F32)) for i in range(2)]
        Y = [ctx.enter_context(nc.psum_tensor(f"Yd{i}", [P, 2, 512], F32)) for i in range(2)]

        const_in = sem("const4_in")
        w_in, s_in = [sem(f"w{i}_in") for i in range(2)], [sem(f"slice{i}_in") for i in range(2)]
        hi_done, lo_done, d_done = sem("w_hi_done"), sem("w_lo_done"), sem("down_done")
        s_hi, s_used = sem("slice_hi"), sem("slice_used")
        x0_in, x0_done = [sem(f"x0_part{i}_in") for i in range(KT // 2)], sem("x0_done")
        g_done, silu_done, gated = sem("gate_up_done"), sem("silu4_done"), sem("gated")
        act_hi, act_done = sem("act_hi_done"), sem("act_done")
        y_taken, tr_done, ln_taken = sem("y_taken"), sem("y_transposed"), sem("ln_taken")
        moments, rstd_done, half_done = sem("moments4"), sem("rstd4_done"), sem("half4_done")
        rows_done, y_out = sem("y_rows_done"), [sem(f"y_rows{i}_stored") for i in range(2)]
        dve_chain = sem("dve4_chain")
        C = 2
        block = ctx.enter_context(nc.Block())

        def wn(t, sec, m):
            return t * UNITS + (m.n + sec * (FS + KT))

        def wn_half(t, sec, m):
            return t * (UNITS // 2) + (m + sec * (FS + KT)).half

        def slot(sec, m):
            return (m + sec * (FS + KT)).odd

        def gh(t, sec, f, h):
            return (t * 2 + sec) * (2 * FS) + f.n * 2 + h

        def dn(t, sec, b):
            return (t * 2 + sec) * KT + b.n

        def sn(t, sec, b):
            return t * 2 * KT + sec * KT + b.n

        def sections(eng, gate, down, has_next, t, after=None):
            for sec in range(2):
                tail = sec == 0 and not (isinstance(t, int) and t == 0)
                first = NO + 4 if tail else 3
                for f in range(first):
                    gate(t, sec, Twice(f))
                    if tail and after and 1 <= f <= NO + 2:
                        after(t - 1, f - 1)
                with eng.Fori(0, (FS - first) // 2) as r:
                    for u in range(2):
                        gate(t, sec, Twice(r, first + u))
                for b in range(2):
                    down(t, sec, Twice(b), has_next)
                with eng.Fori(0, (KT - 2) // 2) as r:
                    for u in range(2):
                        down(t, sec, Twice(r, 2 + u), has_next)

        def program(eng, gate, down, after=None, chain=None, steps=0):
            sections(eng, gate, down, True, 0)
            with eng.Fori(1, NB - 1) as t:
                if chain:
                    chain.enter(t, 1, steps)
                sections(eng, gate, down, True, t, after)
            if chain:
                chain.leave(NB - 2)
            sections(eng, gate, down, False, NB - 1, after)

        @block.sync
        def _(sp):
            def slice_in(n, k, src):
                sp.wait_ge(s_used, C + n - 2 + 1)
                sp.dma_start(sl[k][:, :], src).then_inc(s_in[k], 16)

            def gate(t, sec, f):
                if not (isinstance(t, int) and t == 0 and sec == 0 and f.under(1)):
                    gate_load(t, sec, f)

            def gate_load(t, sec, f):
                k = slot(sec, f)
                sp.wait_ge(lo_done, C + wn(t, sec, f) - 2 + 1)
                for i, w in enumerate((w_gate, w_up)):
                    sp.dma_start(raw[k][:, i * KT:(i + 1) * KT, :],
                                 w.rearrange("(k p) n -> p k n", p=P)[:, :, bass.ds((f.n + sec * FS) * P, P)]
                                 ).then_inc(w_in[k], 16)

            def down(t, sec, b, has_next):
                m = b + FS
                k = slot(sec, m)
                sp.wait_ge(lo_done, C + wn(t, sec, m) - 2 + 1)
                for a, z in ((0, 6), (6, FS)):
                    sp.dma_start(raw[k][:, a:z, :],
                                 w_down[(sec * FS + a) * P:(sec * FS + z) * P, bass.ds(b.n * P, P)]
                                 .rearrange("(f p) n -> p f n", p=P)).then_inc(w_in[k], 16)
                if sec == 0:
                    slice_in(sn(t, 0, b), b.odd, h2_ch[bass.ds(b.n * P, P), bass.ds(t * W, W)])
                elif has_next:
                    slice_in(sn(t, 1, b), b.odd, h2_ch[bass.ds(b.n * P, P), bass.ds((t + 1) * W, W)])

            x0 = h2_ch.rearrange("(k p) t -> p k t", p=P)
            sp.dma_start(yT[:, 0:2, :], x0[:, 0:2, 0:W]).then_inc(x0_in[0], 16)
            gate_load(0, 0, Twice(0))
            for i in range(1, KT // 2):
                sp.dma_start(yT[:, 2 * i:2 * i + 2, :], x0[:, 2 * i:2 * i + 2, 0:W]).then_inc(x0_in[i], 16)
            sp.dma_start(ident[:, :], c_square[:, 0, :]).then_inc(const_in, 16)
            sp.dma_start(lng[:, :], load_rows(ln_g)).then_inc(const_in, 16)
            sp.dma_start(lnb[:, :], load_rows(ln_b)).then_inc(const_in, 16)
            program(sp, gate, down)

        @block.gpsimd
        def _(pool):
            nc.gpsimd.memset(half[:, :], -0.5).then_inc(half_done, 1)
            pool.wait_ge(half_done, 1)


            def power(t, r):
                n = row_tile(t, r)[1]
                pool.wait_ge(moments, t * NO + r + 1)
                nc.gpsimd.tensor_tensor(rstd[0:n, :], mv[0:n, 1:2], half[0:n, :], ALU.pow).then_inc(rstd_done, 1)

            with pool.Fori(0, NB - 1) as t:
                for r in range(NO):
                    power(t, r)
            for r in range(NO):
                power(NB - 1, r)

        @block.tensor
        def _(pe):
            def gate(t, sec, f):
                k = slot(sec, f)
                first = isinstance(t, int) and t == 0 and sec == 0 and f.under(1)
                if sec == 0 and f.under(1) and not first:
                    pe.wait_ge(s_used, C + t * 2 * KT)
                pe.wait_ge(lo_done, C + wn(t, sec, f) + 1)
                for h in range(2):
                    pe.wait_ge(gated, C + gh(t, sec, f, h) - 2 + 1)
                    for i in range(2):
                        for kk in range(KT):
                            if first and h == 0 and i == 0:
                                pe.wait_ge(x0_done, kk + 1)
                            for m, (w, x) in enumerate(((whi, x_hi), (whi, x_lo), (wlo, x_hi))):
                                mm = pe.matmul(G[h][:, i, 0:H], w[k][:, i * KT + kk, :], x[:, kk, h * H:(h + 1) * H],
                                               start=(kk == 0 and m == 0), stop=(kk == KT - 1 and m == 2))
                    mm.then_inc(g_done, 1)

            def down(t, sec, b, has_next):
                k, par = slot(sec, b + FS), b.odd
                if b.under(1):
                    pe.wait_ge(act_done, C + gh(t, sec, Twice(FS - 1), 1) + 1)
                    if sec == 0:
                        pe.wait_ge(ln_taken, C + t * NO)
                pe.wait_ge(lo_done, C + wn(t, sec, b + FS) + 1)
                pe.wait_ge(y_taken, C + dn(t, sec, b) - 2 + 1)
                for h in range(2):
                    for f in range(FS):
                        for m, (w, x) in enumerate(((whi, a_hi), (whi, a_lo), (wlo, a_hi))):
                            mm = pe.matmul(Y[par][:, h, 0:H], w[k][:, f, :], x[:, f, h * H:(h + 1) * H],
                                           start=(f == 0 and m == 0), stop=(f == FS - 1 and m == 2))
                mm.then_inc(d_done, 1)

            def rows_of(t, r):
                a, n = row_tile(t, r)
                if r == 0:
                    pe.wait_ge(const_in, 48)
                    pe.wait_ge(y_taken, C + (t + 1) * 2 * KT)
                pe.wait_ge(ln_taken, C + t * NO + r - 2 + 1)
                for b in range(KT):
                    mm = pe.transpose(Y[r % 2][0:n, b // 4, (b % 4) * P:(b % 4 + 1) * P], yT[:, b, a:a + n], ident[:, :])
                mm.then_inc(tr_done, 1)

            program(pe, gate, down, lambda t, r: rows_of(t, r) if r < NO else None)
            for r in range(NO):
                rows_of(NB - 1, r)

        @block.scalar
        def _(act):
            def gate_used(t, sec, f):
                act.wait_ge(g_done, gh(t, sec, f, 1) + 1)

            def down_used(t, sec, b):
                act.wait_ge(d_done, dn(t, sec, b) + 1)

            def hi(t, sec, m, n):
                k = slot(sec, m)
                act.wait_ge(w_in[k], 32 * (wn_half(t, sec, m) + 1))
                nc.scalar.activation(whi[k][:, 0:n, :], raw[k][:, 0:n, :], ACT.Copy).then_inc(hi_done, 1)

            def slice_hi(n_half, b):
                act.wait_ge(s_in[b.odd], 16 * (n_half + 1))
                nc.scalar.activation(x_hi[:, b.n, :], sl[b.odd][:, :], ACT.Copy).then_inc(s_hi, 1)

            def tail(t, sec, f):
                for h in range(2):
                    act.wait_ge(g_done, gh(t, sec, f, h) + 1)
                    act.wait_ge(act_done, C + gh(t, sec, f, h) - 2 + 1)
                    nc.scalar.activation(act_t[h][:, :], G[h][:, 0, 0:H], ACT.Silu).then_inc(silu_done, 1)

            def gate(t, sec, f):
                if not f.under(2):
                    gate_used(t, sec, f + -2)
                elif sec:
                    down_used(t, 0, f + (KT - 2))
                elif not (isinstance(t, int) and t == 0):
                    down_used(t - 1, 1, f + (KT - 2))
                hi(t, sec, f, 2 * KT)
                if not f.under(1):
                    tail(t, sec, f + -1)

            def down(t, sec, b, has_next):
                if b.under(2):
                    gate_used(t, sec, b + (FS - 2))
                else:
                    down_used(t, sec, b + -2)
                hi(t, sec, b + FS, FS)
                if b.under(1):
                    tail(t, sec, Twice(FS - 1))
                if sec == 1 and has_next:
                    if b.under(1):
                        gate_used(t, 1, Twice(FS - 1))
                    slice_hi(t * KT + (b + KT).half, b)

            def store(t, r):
                a, n = row_tile(t, r)
                if isinstance(t, int) and t == NB - 1 and r == NO - 1:
                    dst = y_sample
                else:
                    dst = y_prompt[bass.ds(t * W + a, n), :]
                act.wait_ge(rows_done, t * NO + r + 1)
                act.dma_start(dst, ob[r % 2][0:n, :]).then_inc(y_out[r % 2], 16)

            for k in range(2):
                act.sem_inc(y_out[k], 16)
            for b in range(KT):
                if b % 2 == 0:
                    act.wait_ge(x0_in[b // 2], 16)
                nc.scalar.activation(x_hi[:, b, :], yT[:, b, :], ACT.Copy).then_inc(s_hi, 1)
            program(act, gate, down, lambda t, r: store(t, r - 2) if r >= 2 else None)
            for r in range(NO):
                store(NB - 1, r)
            act.wait_ge(y_out[0], 16 * (NB * 3 + 1))
            act.wait_ge(y_out[1], 16 * (NB * 2 + 1))

        @block.vector
        def _(dve):
            ch = Chain(dve, dve_chain)
            v = nc.vector
            for s in (lo_done, s_used, gated, act_done, y_taken, ln_taken):
                dve.sem_inc(s, C)

            def lo(t, sec, m, n):
                k = slot(sec, m)
                dve.wait_ge(hi_done, wn(t, sec, m) + 1)
                v.tensor_tensor(wlo[k][:, 0:n, :], raw[k][:, 0:n, :], split_view(whi[k][:, 0:n, :]),
                                ALU.subtract).then_inc(lo_done, 1)

            def slice_lo(n, b):
                dve.wait_ge(s_hi, n + 1)
                v.tensor_tensor(x_lo[:, b.n, :], sl[b.odd][:, :], split_view(x_hi[:, b.n, :]),
                                ALU.subtract).then_inc(s_used, 1)

            def tail(t, sec, f):
                for h in range(2):
                    n = gh(t, sec, f, h)
                    to = a_hi[:, f.n, h * H:(h + 1) * H]
                    dve.wait_ge(silu_done, n + 1)
                    v.tensor_tensor(act_t[h][:, :], act_t[h][:, :], G[h][:, 1, 0:H], ALU.mult).then_inc(gated, 1)
                    dve.wait_ge(gated, C + n + 1)
                    v.tensor_copy(to, act_t[h][:, :]).then_inc(act_hi, 1)
                    dve.wait_ge(act_hi, n + 1)
                    v.tensor_tensor(a_lo[:, f.n, h * H:(h + 1) * H], act_t[h][:, :], split_view(to),
                                    ALU.subtract).then_inc(act_done, 1)

            def y_take(t, sec, b):
                k = b.odd
                dve.wait_ge(d_done, dn(t, sec, b) + 1)
                src = Y[k][:, :, 0:H]
                dst = yT[:, b.n, :].rearrange("p (h c) -> p h c", h=2)
                if sec == 0:
                    dve.wait_ge(s_in[k], 16 * (t * KT + b.half + 1))
                    if b.under(1) and not (isinstance(t, int) and t == 0):
                        dve.wait_ge(tr_done, t * NO)
                    v.scalar_tensor_tensor(dst, sl[k][:, :].rearrange("p (h c) -> p h c", h=2), ALPHA, src,
                                           ALU.mult, ALU.add).then_inc(y_taken, 1)
                    dve.wait_ge(y_taken, C + dn(t, 0, b) + 1)
                    dve.sem_inc(s_used, 1)
                else:
                    dve.wait_ge(y_taken, C + dn(t, 0, b) + 1)
                    v.tensor_tensor(dst, dst, src, ALU.add).then_inc(y_taken, 1)

            def gate(t, sec, f):
                lo(t, sec, f, 2 * KT)
                if not f.under(1):
                    tail(t, sec, f + -1)
                elif sec == 1:
                    y_take(t, 0, Twice(KT - 1))
                elif not (isinstance(t, int) and t == 0):
                    y_take(t - 1, 1, Twice(KT - 1))

            def down(t, sec, b, has_next):
                lo(t, sec, b + FS, FS)
                if b.under(1):
                    tail(t, sec, Twice(FS - 1))
                else:
                    y_take(t, sec, b + -1)
                if sec == 1 and has_next:
                    slice_lo((t + 1) * KT + b.n, b)

            def norm(t, r):
                a, n = row_tile(t, r)
                k = r % 2
                dve.wait_ge(tr_done, t * NO + r + 1)
                dve.wait_ge(y_out[k], 16 * (t * (3 - k) + r // 2 + 1))
                for u in range(2):
                    ch.done(v.bn_stats(stats[0:n, u, :], Y[k][0:n, u, :]))
                ch.wait()
                v.memset(idle[:, :], 0.0)
                ch.step(v.bn_aggr(mv[0:n, :], stats[0:n, :, :]))
                v.tensor_scalar(mv[0:n, 1:2], mv[0:n, 1:2], EPS, None, ALU.add).then_inc(moments, 1)
                dve.wait_ge(rstd_done, t * NO + r + 1)
                x = ob[k][0:n, :]
                v.tensor_scalar(x, Y[k][0:n, :, :].rearrange("p n c -> p (n c)"), mv[0:n, 0:1], rstd[0:n, 0:1],
                                ALU.subtract, ALU.mult).then_inc(ln_taken, 1)
                dve.wait_ge(ln_taken, C + t * NO + r + 1)
                ch.step(v.tensor_tensor(x, x, lng[0:n, :], ALU.mult))
                v.tensor_tensor(x, x, lnb[0:n, :], ALU.add).then_inc(rows_done, 1)

            for b in range(KT):
                dve.wait_ge(s_hi, b + 1)
                v.tensor_tensor(x_lo[:, b, :], yT[:, b, :], split_view(x_hi[:, b, :]), ALU.subtract).then_inc(x0_done, 1)
            program(dve, gate, down, lambda t, r: norm(t, r - 1) if 1 <= r <= NO else None, ch, STEPS_4)
            y_take(NB - 1, 1, Twice(KT - 1))
            for r in range(NO):
                norm(NB - 1, r)


STEPS_4 = 20


def build(nc, x_prompt, x_sample, cache_k, cache_v, cache_logf, state_pool, state_conv, state_ssm, ln_in_g, ln_in_b,
          w_in, pool_w, pool_scale, fox_b_f, conv_w, conv_b, dt_bias, a_log, d_skip, ssm_norm_g, w_out,
          ln_mix_g, ln_mix_b, w_gate, w_up, w_down, ln_ffn_g, ln_ffn_b, c_square, c_inv, c_future,
          y_prompt, y_sample, p_k, p_v, p_logf, p_pool, p_conv, p_ssm, s_k, s_v, s_logf, s_pool, s_conv, s_ssm):
    def scratch(name, shape):
        return nc.dram_tensor(name, shape, F32).ap()

    def rows(a):
        return a[0, 0].rearrange("t h d -> t (h d)")

    def states(a):
        return a[0, 0].rearrange("h p n -> (h p) n")

    h_rows, mixed = scratch("h_rows", [TOKENS, D]), scratch("mixed", [TOKENS, D])
    q_ch, k_ch = scratch("q_ch", [FOX_W, TOKENS]), scratch("k_ch", [FOX_W, TOKENS])
    kc_ch = scratch("kc_ch", [FOX_W, PAST])
    c_rows, cn_rows = scratch("c_rows", [CT * FH, P]), scratch("cn_rows", [CT * FH, P])
    h2_ch = scratch("h2_ch", [D, TOKENS])
    outs = (rows(p_k), rows(p_v), p_logf[0, 0], p_pool[0, 0], p_conv[0, 0], states(p_ssm),
            rows(s_k), rows(s_v), s_logf[0, 0], s_pool[0, 0], s_conv[0, 0], states(s_ssm))

    with ExitStack() as ctx:
        def sem(name):
            return ctx.enter_context(nc.semaphore(name))

        project_mix_scan(nc, sem, x_prompt[0], x_sample[0], state_pool[0, 0], state_conv[0, 0], states(state_ssm),
                         ln_in_g, ln_in_b, w_in[0], pool_w[0], pool_scale[0], fox_b_f[0], conv_w[0], conv_b[0],
                         dt_bias[0], a_log[0], d_skip[0], ssm_norm_g[0], c_square, c_inv, h_rows, q_ch, k_ch,
                         mixed, outs)
        attend(nc, sem, rows(cache_k), rows(cache_v), cache_logf[0, 0], p_logf[0, 0], s_logf[0, 0], rows(p_v),
               rows(s_v), q_ch, k_ch, kc_ch, c_rows, cn_rows, c_square, c_future, mixed)
        mix_out(nc, sem, w_out[0], ln_mix_g[0], ln_mix_b[0], mixed, h_rows, c_square, h2_ch)
        feed_forward(nc, sem, w_gate[0], w_up[0], w_down[0], ln_ffn_g[0], ln_ffn_b[0], h2_ch, c_square,
                     y_prompt[0], y_sample[0])


_INS = ["x_prompt", "x_sample", "cache_fox_k", "cache_fox_v", "cache_fox_logf", "state_pool", "state_conv",
        "state_ssm", "ln_in_g", "ln_in_b", "w_in", "pool_w", "pool_scale", "fox_b_f", "conv_w", "conv_b",
        "dt_bias", "a_log", "d_skip", "ssm_norm_g", "w_out", "ln_mix_g", "ln_mix_b", "w_gate", "w_up",
        "w_down", "ln_ffn_g", "ln_ffn_b"]


def _out_shapes():
    def group(t):
        return [(1, 1, t, FH, HD), (1, 1, t, FH, HD), (1, 1, t, FH), (1, 1, PHIST, POOL_W), (1, 1, CHIST, CONV),
                (1, 1, SH, HD, NST)]

    return [(1, SEQ, D), (1, DEC, D)] + group(SEQ) + group(DEC)


def kernel(**inputs):
    import numpy as _np
    import concourse.bacc as _bacc
    from concourse.bass_utils import run_bass_kernel_spmd as _run

    nc = _bacc.Bacc("TRN2", target_bir_lowering=False, num_devices=1)
    given = {name: _np.ascontiguousarray(inputs[name]) for name in _INS}
    given.update(host_constants())
    given.update(attention_constants())
    arrays, args = {}, []
    for name, a in given.items():
        arrays[f"in_{name}"] = a
        args.append(nc.dram_tensor(f"in_{name}", a.shape, F32, kind="ExternalInput").ap())
    for i, shape in enumerate(_out_shapes()):
        args.append(nc.dram_tensor(f"out_{i}", shape, F32, kind="ExternalOutput").ap())
    build(nc, *args)
    r = _run(nc, [arrays], core_ids=[0])
    return tuple(r.results[0][f"out_{i}"] for i in range(len(_out_shapes())))
```

```python
from contextlib import ExitStack

import numpy as np

import concourse.bass as bass
from concourse import mybir

F32 = mybir.dt.float32
F32R = mybir.dt.float32r
BF16 = mybir.dt.bfloat16
ALU = mybir.AluOpType
ACT = mybir.ActivationFunctionType
AX = mybir.AxisListType

P = 128
D = 1024
KT = D // P
SEQ, DEC, PAST = 2048, 64, 256
TOKENS = SEQ + DEC
HD = 64
POOL_W, FOX_W, SSD_W = 256, 384, 384
FH, SH, SG, SR = 6, 6, 2, 3
WINDOWS = (2, 4, 8, 16)
PHIST, CHIST = 15, 3
NST = 128
CONV = 896
CB_ = CONV // P
DFF = 2816
FT = DFF // P
ALPHA = 2.0 ** 0.25
EPS = 1e-5
C_U, C_Q, C_K, C_X, C_DT = 0, 256, 640, 1798, 2694
NCH = (POOL_W + FOX_W + CONV) // P
TOKW = C_X - C_K + SH
T_V, T_F, T_Z, T_DT = 384, 768, 774, 1158
TG = 3
TGW = TOKW // TG
MIX_FOX, MIX_SSD = POOL_W, POOL_W + FOX_W
SLAB = 256
SLABS = SEQ // SLAB


def host_constants():
    k, t = np.arange(P)[:, None], np.arange(P)[None, :]
    upto = (k <= t).astype(np.float32)
    after = (k > t).astype(np.float32)
    ident = np.eye(P, dtype=np.float32)
    ones = np.ones((P, P), np.float32)
    square = np.stack([ident, upto, after, ones], 1).copy()
    inv = np.zeros((P, 2, 16), np.float32)
    for g, w in enumerate(WINDOWS):
        rows = slice(64 * (g % 2), 64 * (g % 2) + 64)
        inv[rows, g // 2] = 1.0 / np.minimum(np.arange(16) + 1, w)
    return {"c_square": square, "c_inv": inv}


class Chain:

    def __init__(self, eng, sem):
        self.eng, self.sem, self.n, self.base = eng, sem, 0, 0

    def done(self, ins):
        ins.then_inc(self.sem, 1)
        self.n += 1

    def wait(self):
        if self.n or not isinstance(self.base, int) or self.base:
            self.eng.wait_ge(self.sem, self.base + self.n)

    def step(self, ins):
        self.done(ins)
        self.wait()

    def enter(self, turn, first, steps):
        self.before, self.steps = self.n, steps
        self.base, self.n = turn * steps + (self.before - first * steps), 0

    def leave(self, turns):
        assert self.n == self.steps, (self.n, self.steps)
        self.base, self.n = 0, self.before + turns * self.steps


def split_view(t):
    return t.bitcast(F32)


def load_rows(ap, n=P):
    return ap.partition_broadcast(n)


def project_mix_scan(nc, sem, x_prompt, x_sample, state_pool, state_conv, state_ssm, ln_g, ln_b, w_in,
                     pool_w, pool_scale, fox_b_f, conv_w, conv_b, dt_bias, a_log, d_skip, norm_g,
                     c_square, c_inv, h_rows, q_ch, k_ch, mixed, outs):
    (p_k, p_v, p_logf, p_pool, p_conv, p_ssm, s_k, s_v, s_logf, s_pool, s_conv, s_ssm) = outs
    LAST = SLABS

    def width(s):
        return DEC if isinstance(s, int) and s == LAST else SLAB

    def tiles(s):
        return 1 if isinstance(s, int) and s == LAST else SLAB // P

    def rows(s):
        return DEC if isinstance(s, int) and s == LAST else P

    FIRST = 2 * (SLAB // P)
    TURN = NCH + (TG + 1 + 2) * (SLAB // P)

    def group0(s):
        return FIRST + s * TURN - (2 if isinstance(s, int) and s == LAST else 0)

    def g_tok(s):
        return group0(s) + NCH

    def g_kt(s):
        return g_tok(s) + TG * tiles(s)

    def g_next(s):
        return g_kt(s) + tiles(s)

    RAW, RING = 3, 3

    def later(s):
        return not (isinstance(s, int) and s == 0)

    def wn(s, i):
        return s * NCH + i

    def w_loaded(s, i):
        return s * (16 * NCH // RAW) + 16 * (i // RAW + 1)

    def chunk_no(q, c):
        return q * (SLAB // P) + c

    with ExitStack() as ctx:
        def sb(name, shape, dt=F32):
            return ctx.enter_context(nc.sbuf_tensor(name, shape, dt))

        def ps(name):
            return ctx.enter_context(nc.psum_tensor(name, [P, 2, 512], F32))

        w_raw = [sb(f"w_in_raw{i}", [P, KT, P]) for i in range(RAW)]
        w_chi = [sb(f"w_in_hi{i}", [P, KT, P], F32R) for i in range(RING)]
        w_clo = [sb(f"w_in_lo{i}", [P, KT, P], F32R) for i in range(RING)]
        w_thi, w_tlo = sb("w_tok_hi", [P, KT, TOKW], F32R), sb("w_tok_lo", [P, KT, TOKW], F32R)
        lng, lnb = sb("lng", [P, D]), sb("lnb", [P, D])
        square = sb("square", [P, 4, P])
        ident, upto, after, ones = (square[:, i, :] for i in range(4))
        inv = sb("inv", [P, 2, 16])
        poolw = sb("poolw", [P, 2, P])
        pscale, gnorm = sb("pscale", [P, POOL_W]), sb("gnorm", [P, SSD_W])
        cw, cbias = sb("cw", [P, 4, CB_]), sb("cbias", [P, CB_])
        bf, bdt, a_neg, dsk = sb("bf", [P, FH]), sb("bdt", [P, SH]), sb("a_neg", [P, SH]), sb("dsk", [P, SH])
        half = sb("half", [P, 2])
        xb = sb("xb", [P, 2, D])
        stats, mv = sb("stats", [P, 2, 6]), sb("mv", [P, 2])
        rstd = sb("rstd", [P, 1])
        idle = sb("idle", [1, 1])
        h_hi, h_lo = sb("hT_hi", [P, KT, SLAB], F32R), sb("hT_lo", [P, KT, SLAB], F32R)
        qs = sb("qs", [P, 3, SLAB])
        uT = sb("uT", [P, 2, PHIST + SLAB])
        win = [sb(f"win{i}", [P, 2, PHIST + SLAB]) for i in range(2)]
        pd = sb("pd", [P, 2, SLAB])
        h_raw = pd[:, :, :].rearrange("p b t -> p (b t)").rearrange("p (k t) -> p k t", k=KT)
        pm = sb("pm", [P, 2, POOL_W])
        xr = sb("xr", [P, CB_, CHIST + SLAB])
        cv = sb("cv", [P, CB_, SLAB])
        tk = sb("tk", [P, 2, TOKW])
        ks = qs
        spy, spa, spe, spw, spl, spr = (sb(f"sp{n}", [P, 2, FH + SH]) for n in "yaewlr")
        logf = sb("logf", [P, 2, FH])
        dta = sb("dta", [P, 2, SH])
        amask = sb("amask", [P, SH, P])
        dec = sb("dec", [P, SH, P])
        ex = sb("ex", [P, 3 * SH])
        xt, xdt, xw = sb("xt", [P, SSD_W]), sb("xdt", [P, SSD_W]), sb("xw", [P, SSD_W])
        bt, cbm = sb("bt", [P, SG * NST]), sb("cbm", [P, SG, P])
        w6 = sb("w6", [P, SH])
        ya, yb, yo = sb("ya", [P, SSD_W]), sb("yb", [P, SSD_W]), sb("yo", [P, SSD_W])
        ssum, rr = sb("ssum", [P, SG]), sb("rr", [P, SG])
        state = {0: sb("state_p", [NST, SSD_W]), 1: sb("state_s", [NST, SSD_W])}
        stin = sb("stin", [P, 3, NST])
        pp, psT, psG = ps("pp"), ps("psT"), ps("psG")
        psC = ctx.enter_context(nc.psum_tensor("psC", [P, 512], F32))
        psY = ctx.enter_context(nc.psum_tensor("psY", [P, 512], F32))

        first_in, hist_in = sem("norm_consts_in"), sem("histories_in")
        consts_in, w_loads = sem("consts_in"), [sem(f"w_in{i}_loaded") for i in range(RAW)]
        w_tok_in = [sem(f"w_tok{i}_in") for i in range(3)]
        wi_hi, wi_lo, h_hi_done = sem("w_in_hi_done"), sem("w_in_lo_done"), sem("hT_hi_done")
        h_raw_done = sem("hT_raw_done")
        wt_hi, wt_lo = sem("w_tok_hi_done"), sem("w_tok_lo_done")
        x_in, h_done = [sem(f"x_tile{j}_in") for j in range(2)], sem("h_done")
        moments, rstd_done = sem("moments"), sem("rstd_done")
        full, evac = sem("group_full"), sem("group_evacuated")
        h_out, q_out, kv_out, kt_out, small_out, y_out, m_out = (
            sem("h_stored"), sem("q_stored"), sem("kv_stored"), sem("kt_stored"),
            sem("logf_stored"), sem("y_stored"), sem("pool_stored"))
        end_out = sem("states_stored")
        conv_done, pool_done, pool_mm, pm_done = sem("conv_done"), sem("pool_done"), sem("pool_mm"), sem("pm_done")
        silu_done = sem("silu_done")
        sp_ready, sp_exp, sp_one, sp_ln, dt_done = (
            sem("sp_ready"), sem("sp_exp"), sem("sp_one"), sem("sp_ln"), sem("dt_done"))
        amask_done, seg_done, sums_done, exp_done, mix_ready, mix_done, chunk_done = (
            sem("amask_done"), sem("seg_done"), sem("sums_done"), sem("exp_done"), sem("mix_ready"),
            sem("mix_done"), sem("chunk_done"))
        ss_done, rr_done, y_done = sem("ss_done"), sem("rr_done"), sem("y_done")
        a_exp, init_done = sem("a_exp"), sem("init_done")
        st_t, st_rows = sem("state_transposed"), sem("state_rows")
        dve_chain = sem("dve_chain")
        N_CONST = 1 + 4 + 6 + 4 + 1 + 3

        block = ctx.enter_context(nc.Block())

        def token0(s):
            return s * SLAB

        def tile_rows(s, j):
            return bass.ds(token0(s) + j * P, rows(s))

        def out_rows(s, j, prompt, sample):
            if isinstance(s, int) and s == LAST:
                return sample[bass.ds(j * P, DEC)]
            return prompt[tile_rows(s, j)]

        def program(s_body, eng, chain=None, steps=0):
            s_body(0)
            with eng.Fori(1, SLABS - 1) as s:
                if chain:
                    chain.enter(s, 1, steps)
                s_body(s)
            if chain:
                chain.leave(SLABS - 2)
            s_body(SLABS - 1)
            s_body(SLABS)

        w_tok_raw = [tk[:, 0, :], tk[:, 1, :], cv[:, :, :].rearrange("p b t -> p (b t)")[:, 0:TOKW]]

        def w_tok_load(eng, k):
            to, rows_k = w_tok_raw[k % 3], w_in[k * P:(k + 1) * P, :]
            eng.dma_start(to[:, 0:T_DT], rows_k[:, C_K:C_X]).then_inc(w_tok_in[k % 3], 16)
            eng.dma_start(to[:, T_DT:TOKW], rows_k[:, C_DT:C_DT + SH]).then_inc(w_tok_in[k % 3], 16)

        @block.gpsimd
        def _(pool):
            nc.gpsimd.memset(half[:, :], -0.5).then_inc(init_done, 1)
            pool.wait_ge(init_done, 3)

            def w_low(s, i):
                if isinstance(s, int) and s == LAST:
                    return
                pool.wait_ge(wi_hi, wn(s, i) + 1)
                nc.gpsimd.tensor_tensor(w_clo[i % RING][:, :, :], w_raw[i % RAW][:, :, :],
                                        split_view(w_chi[i % RING][:, :, :]), ALU.subtract).then_inc(wi_lo, 1)

            def norm(s, j):
                r = rows(s)
                pool.wait_ge(moments, s * 2 + j + 1)
                nc.gpsimd.tensor_tensor(rstd[0:r, :], mv[0:r, 1:2], half[0:r, 0:1], ALU.pow).then_inc(rstd_done, 1)

            def scan(q, c):
                r = rows(q)
                pool.wait_ge(ss_done, chunk_no(q, c) + 1)
                nc.gpsimd.tensor_tensor(rr[0:r, :], ssum[0:r, :], half[0:r, :], ALU.pow).then_inc(rr_done, 1)

            def slab(s):
                first = isinstance(s, int) and s == 0
                last = isinstance(s, int) and s == LAST
                for i in range(RING, NCH):
                    w_low(s, i)
                    if i == RING + 3 and not first:
                        scan(s - 1, 0)
                        if not last:
                            norm(s + 1, 0)
                    if i in (RING, RING + 3) and first:
                        norm(1, (i - RING) // 3)
                if not last:
                    w_low(s + 1, 0)
                if not first:
                    scan(s - 1, 1)
                    if not last and tiles(s + 1) > 1:
                        norm(s + 1, 1)
                if not last:
                    for i in range(1, RING):
                        w_low(s + 1, i)

            for j in range(2):
                norm(0, j)
            for i in range(RING):
                w_low(0, i)
            program(slab, pool)
            scan(LAST, 0)

        @block.sync
        def _(sp):
            def x_load(s):
                for j in range(tiles(s)):
                    if not (isinstance(s, int) and s == 0):
                        sp.wait_ge(h_out, 16 * (s * 2 - 2 + 2))
                        sp.wait_ge(full, group0(s - 1))
                    sp.dma_start(xb[0:rows(s), j, :], out_rows(s, j, x_prompt, x_sample)).then_inc(x_in[j], 16)

            def h_store(s):
                for j in range(tiles(s)):
                    sp.wait_ge(h_done, s * 2 + j + 1)
                    sp.dma_start(h_rows[tile_rows(s, j), :], xb[0:rows(s), j, :]).then_inc(h_out, 16)

            def const(dst, src, **kw):
                sp.dma_start(dst, src, **kw).then_inc(consts_in, 16)

            x_load(0)
            sp.dma_start(lng[:, :], load_rows(ln_g)).then_inc(first_in, 16)
            sp.dma_start(lnb[:, :], load_rows(ln_b)).then_inc(first_in, 16)
            sp.dma_start(square[:, :, :], c_square).then_inc(first_in, 16)
            const(inv[:, :, :], c_inv)
            sp.wait_ge(init_done, 3)
            for g in range(4):
                a = 64 * (g % 2)
                const(poolw[a:a + 64, g // 2, a:a + 64], pool_w[g])
            const(pscale[:, :], load_rows(pool_scale))
            const(gnorm[:, :], load_rows(norm_g))
            const(bf[:, :], load_rows(fox_b_f))
            const(bdt[:, :], load_rows(dt_bias))
            const(a_neg[:, :], load_rows(a_log))
            const(dsk[:, :], load_rows(d_skip))
            for t in range(4):
                const(cw[:, t, :], conv_w[t].rearrange("(b p) -> p b", p=P), allow_slow_non_contiguous=True)
            const(cbias[:, :], conv_b.rearrange("(b p) -> p b", p=P), allow_slow_non_contiguous=True)
            for b in range(3):
                const(stin[:, b, :], state_ssm[b * P:(b + 1) * P, :])
            for k in range(3):
                w_tok_load(sp, k)
            h_store(0)

            def y_store(q, c):
                sp.wait_ge(y_done, chunk_no(q, c) + 1)
                sp.dma_start(mixed[tile_rows(q, c), MIX_SSD:D], yo[0:rows(q), :]).then_inc(y_out, 16)

            def slab(s):
                first = isinstance(s, int) and s == 0
                last = isinstance(s, int) and s == LAST
                w = width(s)
                if not last:
                    x_load(s + 1)
                if last:
                    sp.wait_ge(pool_done, LAST)
                    sp.wait_ge(conv_done, LAST)
                    for b in range(2):
                        sp.dma_start(uT[:, b, 0:PHIST],
                                     state_pool[:, b * P:(b + 1) * P].rearrange("t p -> p t"),
                                     allow_slow_non_contiguous=True).then_inc(hist_in, 16)
                    for b in range(CB_):
                        sp.dma_start(xr[:, b, 0:CHIST],
                                     state_conv[:, b * P:(b + 1) * P].rearrange("t p -> p t"),
                                     allow_slow_non_contiguous=True).then_inc(hist_in, 16)
                if first:
                    h_store(s + 1)
                sp.wait_ge(evac, group0(s) + 5)
                for b in range(3):
                    sp.dma_start(q_ch[b * P:(b + 1) * P, bass.ds(token0(s), w)], qs[:, b, 0:w]).then_inc(q_out, 16)
                if not first:
                    for c in range(tiles(s - 1)):
                        y_store(s - 1, c)
                        if not last and c < tiles(s + 1):
                            j, n = c, s + 1
                            sp.wait_ge(h_done, n * 2 + j + 1)
                            sp.dma_start(h_rows[tile_rows(n, j), :], xb[0:rows(n), j, :]).then_inc(h_out, 16)
                for j in range(tiles(s)):
                    sp.wait_ge(evac, g_tok(s) + TG * (j + 1))
                    sp.dma_start(out_rows(s, j, p_k, s_k), tk[0:rows(s), j, 0:T_V]).then_inc(kv_out, 16)
                    sp.dma_start(out_rows(s, j, p_v, s_v), tk[0:rows(s), j, T_V:T_F]).then_inc(kv_out, 16)
                sp.wait_ge(evac, g_kt(s) + tiles(s))
                for b in range(3):
                    sp.dma_start(k_ch[b * P:(b + 1) * P, bass.ds(token0(s), w)], ks[:, b, 0:w]).then_inc(kt_out, 16)
                sp.wait_ge(dt_done, s + 1)
                for j in range(tiles(s)):
                    sp.dma_start(out_rows(s, j, p_logf, s_logf), logf[0:rows(s), j, :]).then_inc(small_out, 16)
                sp.wait_ge(pm_done, s + 1)
                for j in range(tiles(s)):
                    sp.dma_start(mixed[tile_rows(s, j), 0:POOL_W], pm[0:rows(s), j, :]).then_inc(m_out, 16)
                if isinstance(s, int) and s >= LAST - 1:
                    u_out, x_out = (s_pool, s_conv) if last else (p_pool, p_conv)
                    for b in range(2):
                        sp.dma_start(u_out[:, b * P:(b + 1) * P].rearrange("t p -> p t"),
                                     uT[:, b, w:w + PHIST], allow_slow_non_contiguous=True).then_inc(end_out, 16)
                    for b in range(CB_):
                        sp.dma_start(x_out[:, b * P:(b + 1) * P].rearrange("t p -> p t"),
                                     xr[:, b, w:w + CHIST], allow_slow_non_contiguous=True).then_inc(end_out, 16)
                    if not last:
                        sp.wait_ge(end_out, 16 * (2 + CB_))

            program(slab, sp)
            y_store(LAST, 0)
            for i, dst in enumerate((p_ssm, s_ssm)):
                sp.wait_ge(st_rows, 1 + 2 * i)
                for b in range(3):
                    sp.dma_start(dst[b * P:(b + 1) * P, :], stin[:, b, :]).then_inc(end_out, 16)
                sp.wait_ge(end_out, 16 * (2 * (2 + CB_) + 3 * (i + 1)))
                if i == 0:
                    sp.sem_inc(st_rows, 1)
            n = 2 * SLABS + 1
            sp.wait_ge(h_out, 16 * n)
            sp.wait_ge(q_out, 16 * 3 * (SLABS + 1))
            sp.wait_ge(kv_out, 16 * 2 * n)
            sp.wait_ge(kt_out, 16 * 3 * (SLABS + 1))
            sp.wait_ge(small_out, 16 * n)
            sp.wait_ge(y_out, 16 * n)
            sp.wait_ge(m_out, 16 * n)

        @block.tensor
        def _(pe):
            def begin(n, ok):
                if ok:
                    pe.wait_ge(evac, n - 1)

            def transposes(s, n0):
                for j in range(tiles(s)):
                    pe.wait_ge(h_done, s * 2 + j + 1)
                    for u in range(2):
                        n = n0 + 2 * j + u
                        begin(n, not isinstance(n, int) or n >= 2)
                        for i in range(4):
                            k = 4 * u + i
                            mm = pe.transpose(pp[:, u, i * P:i * P + rows(s)], xb[0:rows(s), j, k * P:(k + 1) * P],
                                              ident[0:rows(s), 0:rows(s)])
                        mm.then_inc(full, 1)

            def scan_a(q, c):
                r, n = rows(q), chunk_no(q, c)
                st = state[1 if isinstance(q, int) and q == LAST else 0]
                a = c * P
                if not (isinstance(q, int) and q == 0 and c == 0):
                    pe.wait_ge(chunk_done, n)
                if c == 0:
                    pe.wait_ge(pm_done, q + 1)
                pe.wait_ge(silu_done, 2 * q + 2)
                for b in range(5):
                    dst = psT[0:r, 0, b * P:(b + 1) * P] if b < 3 else psT[0:r, 1, (b - 3) * P:(b - 2) * P]
                    pe.transpose(dst, cv[:, b, a:a + r], ident)
                pe.wait_ge(dt_done, q + 1)
                for i, m in enumerate((upto, after)):
                    pe.matmul(psC[0:r, 256 + 6 * i:262 + 6 * i], m[0:r, 0:r], dta[0:r, c, :], start=True, stop=True)
                pe.matmul(psC[:, 268:274], ones[0:r, :], dta[0:r, c, :], start=True, stop=True)
                for g in range(SG):
                    pe.matmul(psC[0:r, g * P:g * P + r], cv[:, 3 + g, a:a + r], cv[:, 5 + g, a:a + r],
                              start=True, stop=True)
                for g in range(SG):
                    mm = pe.matmul(psY[0:r, g * 192:(g + 1) * 192], cv[:, 5 + g, a:a + r],
                                   st[:, g * 192:(g + 1) * 192], start=True, stop=True)
                mm.then_inc(sums_done, 1)
                pe.wait_ge(amask_done, n + 1)
                for h in range(SH):
                    mm = pe.matmul(psG[0:r, h // 3, (h % 3) * P:(h % 3) * P + r], amask[0:r, h, 0:r],
                                   upto[0:r, 0:r], start=True, stop=True)
                mm.then_inc(seg_done, 1)

            def scan_c(q, c):
                r, n = rows(q), chunk_no(q, c)
                pe.wait_ge(mix_ready, n + 1)
                for g in range(SG):
                    pe.matmul(psT[:, 0, g * 192:(g + 1) * 192], bt[0:r, g * P:(g + 1) * P],
                              xw[0:r, g * 192:(g + 1) * 192], start=True, stop=True)
                for h in range(SH):
                    mm = pe.matmul(psY[0:r, h * HD:(h + 1) * HD], dec[0:r, h, 0:r], xdt[0:r, h * HD:(h + 1) * HD],
                                   start=True, stop=True)
                mm.then_inc(mix_done, 1)

            def scan(q, slot):
                for c in range(tiles(q)):
                    if slot == 5 * c:
                        scan_a(q, c)
                    if slot == 5 * c + 3:
                        scan_c(q, c)

            pe.wait_ge(first_in, 16 * 3)
            transposes(0, 0)
            pe.wait_ge(consts_in, 16 * N_CONST)
            for b in range(3):
                mm = pe.transpose(psT[:, 0, b * P:(b + 1) * P], stin[:, b, :], ident)
            mm.then_inc(st_t, 1)

            def slab(s):
                first = isinstance(s, int) and s == 0
                last = isinstance(s, int) and s == LAST
                w, r = width(s), rows(s)
                pe.wait_ge(evac, group0(s))
                for i in range(NCH):
                    n = group0(s) + i
                    if last:
                        pe.wait_ge(w_loads[i % RAW], w_loaded(s, i))
                        pe.wait_ge(h_raw_done, 2)
                        begin(n, True)
                        for k in range(KT):
                            mm = pe.matmul(pp[:, i % 2, 0:w], w_raw[i % RAW][:, k, :], h_raw[:, k, :],
                                           start=(k == 0), stop=(k == KT - 1))
                        mm.then_inc(full, 1)
                        scan(s - 1, i)
                        continue
                    pe.wait_ge(wi_lo, wn(s, i) + 1)
                    begin(n, True)
                    for k in range(KT):
                        for m, (wt, x) in enumerate(((w_chi, h_hi), (w_clo, h_hi), (w_chi, h_lo))):
                            mm = pe.matmul(pp[:, i % 2, 0:w], wt[i % RING][:, k, :], x[:, k, 0:w],
                                           start=(k == 0 and m == 0), stop=(k == KT - 1 and m == 2))
                    mm.then_inc(full, 1)
                    if not first:
                        scan(s - 1, i)
                for j in range(tiles(s)):
                    for u in range(TG):
                        i = j * TG + u
                        begin(g_tok(s) + i, True)
                        for k in range(KT):
                            if first and i == 0:
                                pe.wait_ge(wt_lo, k + 1)
                            for m, (x, wt) in enumerate(((h_hi, w_thi), (h_hi, w_tlo), (h_lo, w_thi))):
                                mm = pe.matmul(pp[:, i % 2, 0:TGW], x[:, k, j * P:(j + 1) * P],
                                               wt[:, k, u * TGW:(u + 1) * TGW],
                                               start=(k == 0 and m == 0), stop=(k == KT - 1 and m == 2))
                        mm.then_inc(full, 1)
                pe.wait_ge(pool_done, s + 1)
                if not first:
                    pe.wait_ge(chunk_done, chunk_no(s, 0))
                else:
                    pe.wait_ge(init_done, 4)
                for j in range(tiles(s)):
                    for b in range(2):
                        mm = pe.matmul(psT[0:r, j, b * P:(b + 1) * P], pd[:, b, j * P:j * P + r], poolw[:, b, :],
                                       start=True, stop=True)
                mm.then_inc(pool_mm, 1)
                for j in range(tiles(s)):
                    i = tiles(s) * TG + j
                    begin(g_kt(s) + j, True)
                    pe.wait_ge(evac, g_tok(s) + TG * j + 1)
                    for b in range(3):
                        mm = pe.transpose(pp[:, i % 2, b * P:b * P + r], tk[0:r, j, b * P:(b + 1) * P],
                                          ident[0:r, 0:r])
                    mm.then_inc(full, 1)
                if not last:
                    transposes(s + 1, g_next(s))

            program(slab, pe)
            scan_a(LAST, 0)
            scan_c(LAST, 0)
            for i in range(2):
                pe.wait_ge(chunk_done, chunk_no(LAST, 0) + 1)
                if i:
                    pe.wait_ge(st_rows, 3 - 1)
                for b in range(3):
                    mm = pe.transpose(psT[:, 0, b * P:(b + 1) * P], state[i][:, b * P:(b + 1) * P], ident)
                mm.then_inc(st_t, 1)

        @block.scalar
        def _(act):
            def take(n, out, src, scale=1.0):
                act.wait_ge(full, n + 1)
                nc.scalar.activation(out, src, ACT.Copy, scale=scale).then_inc(evac, 1)

            def h_take(s, n0):
                for j in range(tiles(s)):
                    for u in range(2):
                        act.wait_ge(full, n0 + 2 * j + u + 1)
                        nc.scalar.activation(h_hi[:, 4 * u:4 * u + 4, j * P:j * P + rows(s)],
                                             pp[:, u, :].rearrange("p (i c) -> p i c", c=P)[:, :, 0:rows(s)],
                                             ACT.Copy).then_inc(h_hi_done, 1)
                        if isinstance(s, int) and s == LAST:
                            nc.scalar.activation(h_raw[:, 4 * u:4 * u + 4, :],
                                                 pp[:, u, :].rearrange("p (i c) -> p i c", c=P)[:, :, 0:DEC],
                                                 ACT.Copy).then_inc(h_raw_done, 1)

            def scan(q, slot):
                for c in range(tiles(q)):
                    if slot != 5 * c:
                        continue
                    r, n = rows(q), chunk_no(q, c)
                    act.wait_ge(sums_done, n + 1)
                    nc.scalar.activation(ex[0:r, 0:12], psC[0:r, 256:268], ACT.Exp)
                    nc.scalar.activation(ex[:, 12:18], psC[:, 268:274], ACT.Exp)
                    act.wait_ge(seg_done, n + 1)
                    for b in range(2):
                        i = nc.scalar.activation(dec[0:r, 3 * b:3 * b + 3, 0:r],
                                                 psG[0:r, b, 0:384].rearrange("p (h c) -> p h c", c=P)[:, :, 0:r],
                                                 ACT.Exp)
                    i.then_inc(exp_done, 1)

            w3 = w_in.rearrange("(k p) n -> p k n", p=P)
            cols = [C_U, C_U + P] + [C_Q + i * P for i in range(3)] + [C_X + i * P for i in range(CB_)]

            def w_load(i):
                act.dma_start(w_raw[i % RAW][:, :, :], w3[:, :, cols[i]:cols[i] + P]).then_inc(w_loads[i % RAW], 16)

            def w_high(s, i):
                if isinstance(s, int) and s == LAST:
                    if i >= 1 and i + RAW - 1 < NCH:
                        act.wait_ge(full, group0(s) + i)
                        w_load(i + RAW - 1)
                    elif i == 0:
                        act.wait_ge(wi_lo, wn(s, 0))
                        w_load(RAW - 1)
                    return
                act.wait_ge(w_loads[i % RAW], w_loaded(s, i))
                nc.scalar.activation(w_chi[i % RING][:, :, :], w_raw[i % RAW][:, :, :], ACT.Copy).then_inc(wi_hi, 1)
                if later(s) or i:
                    act.wait_ge(wi_lo, wn(s, i))
                w_load((i + RAW - 1) % NCH)

            def w_tok_high(k):
                act.wait_ge(w_tok_in[k % 3], 32 * (k // 3 + 1))
                nc.scalar.activation(w_thi[:, k, :], w_tok_raw[k % 3], ACT.Copy).then_inc(wt_hi, 1)
                if k and k + 2 < KT:
                    act.wait_ge(wt_lo, k)
                    w_tok_load(act, k + 2)

            for i in range(RAW - 1):
                w_load(i)
            h_take(0, 0)
            for i in range(RING):
                w_high(0, i)
            act.wait_ge(consts_in, 16 * N_CONST)
            nc.scalar.activation(a_neg[:, :], a_neg[:, :], ACT.Exp).then_inc(a_exp, 1)

            def slab(s):
                first = isinstance(s, int) and s == 0
                last = isinstance(s, int) and s == LAST
                w, r = width(s), rows(s)
                for i in range(NCH):
                    n = group0(s) + i
                    src = pp[:, i % 2, 0:w]
                    if i < 2:
                        if i == 0 and not first:
                            act.wait_ge(pool_done, s)
                            if last:
                                act.wait_ge(end_out, 16 * (2 + CB_))
                        take(n, uT[:, i, PHIST:PHIST + w], src)
                    elif i < 5:
                        if i == 2 and not first:
                            act.wait_ge(kt_out, 16 * 3 * s)
                        take(n, qs[:, i - 2, 0:w], src, scale=HD ** -0.5)
                    else:
                        if i == 5 and not first:
                            act.wait_ge(conv_done, s)
                        take(n, xr[:, i - 5, CHIST:CHIST + w], src)
                    if last:
                        w_high(s, i + 1)
                    elif i + RING < NCH:
                        w_high(s, i + RING)
                    elif not (isinstance(s, int) and s == LAST - 1):
                        w_high(s + 1, i + RING - NCH)
                    elif i == NCH - 1:
                        w_high(s + 1, 0)
                    if first and i >= NCH - KT:
                        w_tok_high(i - (NCH - KT))
                    if not first:
                        scan(s - 1, i)
                if not first:
                    act.wait_ge(kv_out, 16 * 4 * s)
                    act.wait_ge(y_done, chunk_no(s, 0))
                for j in range(tiles(s)):
                    for u in range(TG):
                        i = j * TG + u
                        take(g_tok(s) + i, tk[0:r, j, u * TGW:(u + 1) * TGW], pp[0:r, i % 2, 0:TGW])
                act.wait_ge(q_out, 16 * 3 * (s + 1))
                for j in range(tiles(s)):
                    i = tiles(s) * TG + j
                    take(g_kt(s) + j, ks[:, :, j * P:j * P + r],
                         pp[:, i % 2, 0:384].rearrange("p (b c) -> p b c", c=P)[:, :, 0:r])
                if not last:
                    h_take(s + 1, g_next(s))
                act.wait_ge(sp_ready, s + 1)
                nc.scalar.activation(spe[0:r, 0:tiles(s), :], spa[0:r, 0:tiles(s), :], ACT.Exp,
                                     scale=-1.0).then_inc(sp_exp, 1)
                act.wait_ge(sp_one, s + 1)
                nc.scalar.activation(spl[0:r, 0:tiles(s), :], spw[0:r, 0:tiles(s), :], ACT.Ln).then_inc(sp_ln, 1)
                act.wait_ge(evac, g_tok(s) + TG * tiles(s))
                nc.scalar.activation(tk[0:r, 0:tiles(s), T_Z:T_DT], tk[0:r, 0:tiles(s), T_Z:T_DT],
                                     ACT.Silu).then_inc(silu_done, 1)
                act.wait_ge(conv_done, s + 1)
                nc.scalar.activation(cv[:, :, 0:w], cv[:, :, 0:w], ACT.Silu).then_inc(silu_done, 1)

            program(slab, act)
            scan(LAST, 0)
            for i in range(2):
                act.wait_ge(st_t, 2 + i)
                if i:
                    act.wait_ge(st_rows, 2)
                nc.scalar.activation(stin[:, :, :], psT[:, 0, 0:384].rearrange("p (b c) -> p b c", c=P),
                                     ACT.Copy).then_inc(st_rows, 1)

        @block.vector
        def _(dve):
            ch = Chain(dve, dve_chain)
            v = nc.vector

            def norm(s, j):
                r, n = rows(s), s * 2 + j
                dve.wait_ge(x_in[j], 16 * (s + 1))
                x = xb[0:r, j, :]
                for u in range(2):
                    ch.done(v.bn_stats(stats[0:r, u, :], x[:, u * 512:(u + 1) * 512]))
                ch.wait()
                v.memset(idle[:, :], 0.0)
                ch.step(v.bn_aggr(mv[0:r, :], stats[0:r, :, :]))
                v.tensor_scalar(mv[0:r, 1:2], mv[0:r, 1:2], EPS, None, ALU.add).then_inc(moments, 1)
                dve.wait_ge(rstd_done, n + 1)
                ch.step(v.tensor_scalar(x, x, mv[0:r, 0:1], rstd[0:r, 0:1], ALU.subtract, ALU.mult))
                ch.step(v.tensor_tensor(x, x, lng[0:r, :], ALU.mult))
                v.tensor_tensor(x, x, lnb[0:r, :], ALU.add).then_inc(h_done, 1)

            def h_low(s):
                for j in range(tiles(s)):
                    for u in range(2):
                        to = (slice(None), slice(4 * u, 4 * u + 4), slice(j * P, j * P + rows(s)))
                        dve.wait_ge(h_hi_done, s * 4 + 2 * j + u + 1)
                        if isinstance(s, int) and s == LAST:
                            dve.wait_ge(h_raw_done, u + 1)
                        v.tensor_tensor(h_lo[to], pp[:, u, :].rearrange("p (i c) -> p i c", c=P)[:, :, 0:rows(s)],
                                        split_view(h_hi[to]), ALU.subtract).then_inc(evac, 1)

            def scan_0(q, c):
                r = rows(q)
                dve.wait_ge(dt_done, q + 1)
                v.tensor_tensor(amask[0:r, :, 0:r], after[0:r, 0:r].unsqueeze(1).broadcast_to([r, SH, r]),
                                dta[0:r, c, :].unsqueeze(2).broadcast_to([r, SH, r]),
                                ALU.mult).then_inc(amask_done, 1)

            def heads(ap, r):
                return ap.unsqueeze(2).broadcast_to([r, SH, HD])

            def by_head(ap):
                return ap.rearrange("p (h c) -> p h c", c=HD)

            def scan_b(q, c):
                r, n = rows(q), chunk_no(q, c)
                dve.wait_ge(exp_done, n + 1)
                ch.done(v.tensor_copy(xt[0:r, :], psT[0:r, 0, 0:384]))
                ch.done(v.tensor_tensor(w6[0:r, :], ex[0:r, 6:12], spl[0:r, c, 6:12], ALU.mult))
                ch.done(v.tensor_tensor(cbm[0:r, :, 0:r], psC[0:r, 0:256].rearrange("p (g c) -> p g c", c=P)[:, :, 0:r],
                                        upto[0:r, 0:r].unsqueeze(1).broadcast_to([r, SG, r]), ALU.mult))
                ch.wait()
                ch.done(v.tensor_copy(bt[0:r, :], psT[0:r, 1, 0:256]))
                ch.done(v.tensor_tensor(by_head(xdt[0:r, :]), by_head(xt[0:r, :]), heads(spl[0:r, c, 6:12], r), ALU.mult))
                ch.done(v.tensor_tensor(by_head(xw[0:r, :]), by_head(xt[0:r, :]), heads(w6[0:r, :], r), ALU.mult))
                ch.done(v.tensor_tensor(by_head(ya[0:r, :]), by_head(psY[0:r, 0:384]), heads(ex[0:r, 0:6], r), ALU.mult))
                for g in range(SG):
                    e = dec[0:r, 3 * g:3 * g + 3, 0:r]
                    ch.done(v.tensor_tensor(e, e, cbm[0:r, g, 0:r].unsqueeze(1).broadcast_to([r, SR, r]), ALU.mult))
                ch.wait()
                v.tensor_tensor(by_head(yb[0:r, :]), by_head(xt[0:r, :]), heads(dsk[0:r, :], r),
                                ALU.mult).then_inc(mix_ready, 1)

            def scan_c(q, c):
                r, n = rows(q), chunk_no(q, c)
                sample = isinstance(q, int) and q == LAST
                st = state[1 if sample else 0]
                dve.wait_ge(mix_ready, n + 1)
                if not (isinstance(q, int) and q == 0 and c == 0):
                    dve.wait_ge(chunk_done, n)
                ch.done(v.tensor_tensor(ya[0:r, :], ya[0:r, :], yb[0:r, :], ALU.add))
                ch.done(v.tensor_tensor(by_head(st[:, :]), by_head(st[:, :]), heads(ex[:, 12:18], P), ALU.mult))
                dve.wait_ge(mix_done, n + 1)
                ch.wait()
                ch.done(v.tensor_tensor(ya[0:r, :], ya[0:r, :], psY[0:r, 0:384], ALU.add))
                v.tensor_tensor(st[:, :], st[:, :], psT[:, 0, 0:384], ALU.add).then_inc(chunk_done, 1)
                ch.wait()
                ch.step(v.tensor_tensor(ya[0:r, :], ya[0:r, :], tk[0:r, c, T_Z:T_DT], ALU.mult))
                for g in range(SG):
                    ch.done(v.tensor_tensor_reduce(yb[0:r, g * 192:(g + 1) * 192], ya[0:r, g * 192:(g + 1) * 192],
                                                   ya[0:r, g * 192:(g + 1) * 192], 1.0, 0.0, ALU.mult, ALU.add,
                                                   ssum[0:r, g:g + 1]))
                ch.wait()
                v.tensor_scalar(ssum[0:r, :], ssum[0:r, :], 1.0 / 192, EPS, ALU.mult, ALU.add).then_inc(ss_done, 1)
                dve.wait_ge(rr_done, n + 1)
                if not (isinstance(q, int) and q == 0 and c == 0):
                    dve.wait_ge(y_out, 16 * n)
                for g in range(SG):
                    a, b = g * 192, (g + 1) * 192
                    i = v.scalar_tensor_tensor(yo[0:r, a:b], ya[0:r, a:b], rr[0:r, g:g + 1], gnorm[0:r, a:b],
                                               ALU.mult, ALU.mult)
                i.then_inc(y_done, 1)

            def convolve(s):
                w = width(s)
                keep = not (isinstance(s, int) and s >= LAST - 1)
                dve.wait_ge(evac, g_tok(s))
                if not (isinstance(s, int) and s == 0):
                    dve.wait_ge(conv_done, s)
                if isinstance(s, int) and s == LAST:
                    dve.wait_ge(hist_in, 16 * (2 + CB_))
                for t in range(4):
                    for b in range(CB_):
                        x = xr[:, b, t:t + w]
                        if t == 0:
                            i = v.tensor_scalar(cv[:, b, 0:w], x, cw[:, 0, b:b + 1], cbias[:, b:b + 1],
                                                ALU.mult, ALU.add)
                        else:
                            i = v.scalar_tensor_tensor(cv[:, b, 0:w], x, cw[:, t, b:b + 1], cv[:, b, 0:w],
                                                       ALU.mult, ALU.add)
                        if t == 3 and b == CB_ - 1 and not keep:
                            i.then_inc(conv_done, 1)
                        else:
                            ch.done(i)
                    if t < 3:
                        ch.wait()
                if keep:
                    v.tensor_copy(xr[:, :, 0:CHIST], xr[:, :, w:w + CHIST]).then_inc(conv_done, 1)

            def pool_mix(s):
                w = width(s)
                keep = not (isinstance(s, int) and s >= LAST - 1)
                if not (isinstance(s, int) and s == 0):
                    dve.wait_ge(pool_done, s)
                n = PHIST + w
                lo = 1
                src = uT
                for g, wd in enumerate(WINDOWS):
                    step, to = wd // 2, win[g % 2]
                    ch.step(v.tensor_tensor(to[:, :, lo:n], src[:, :, lo:n], src[:, :, lo - step:n - step], ALU.add))
                    src, lo = to, lo + 2 * step
                    a, b = 64 * (g % 2), g // 2
                    i = v.scalar_tensor_tensor(pd[a:a + 64, b, 0:w], to[a:a + 64, b, PHIST:n], 1.0 / wd,
                                               uT[a:a + 64, b, PHIST:n], ALU.mult, ALU.subtract)
                    if g == 3 and not keep:
                        i.then_inc(pool_done, 1)
                    else:
                        ch.done(i)
                    if isinstance(s, int) and s == 0:
                        ch.wait()
                        ch.step(v.tensor_tensor(pd[a:a + 64, b, 0:16], to[a:a + 64, b, PHIST:PHIST + 16],
                                                inv[a:a + 64, b, :], ALU.mult))
                        ch.step(v.tensor_tensor(pd[a:a + 64, b, 0:16], pd[a:a + 64, b, 0:16],
                                                uT[a:a + 64, b, PHIST:PHIST + 16], ALU.subtract))
                if keep:
                    v.tensor_copy(uT[:, :, 0:PHIST], uT[:, :, w:n]).then_inc(pool_done, 1)

            def pool_take(s):
                r = rows(s)
                if not (isinstance(s, int) and s == 0):
                    dve.wait_ge(m_out, 16 * 2 * s)
                dve.wait_ge(pool_mm, s + 1)
                v.tensor_tensor(pm[0:r, 0:tiles(s), :], psT[0:r, 0:tiles(s), 0:256],
                                pscale[0:r, :].unsqueeze(1).broadcast_to([r, tiles(s), 256]),
                                ALU.mult).then_inc(pm_done, 1)

            def gates_0(s):
                r, m = rows(s), tiles(s)
                dve.wait_ge(evac, g_kt(s))
                f, d = tk[0:r, 0:m, T_F:T_Z], tk[0:r, 0:m, T_DT:TOKW]

                def rep(ap):
                    return ap[0:r, :].unsqueeze(1).broadcast_to([r, m, 6])
                ch.done(v.scalar_tensor_tensor(spy[0:r, 0:m, 0:6], f, -1.0, rep(bf), ALU.mult, ALU.subtract))
                ch.done(v.tensor_tensor(spy[0:r, 0:m, 6:12], d, rep(bdt), ALU.add))
                ch.wait()
                y = spy[0:r, 0:m, :]
                v.scalar_tensor_tensor(spa[0:r, 0:m, :], y, -1.0, y, ALU.mult, ALU.max).then_inc(sp_ready, 1)

            def gates_1(s):
                r, m = rows(s), tiles(s)
                dve.wait_ge(sp_exp, s + 1)
                v.tensor_scalar(spw[0:r, 0:m, :], spe[0:r, 0:m, :], 1.0, None, ALU.add).then_inc(sp_one, 1)

            def gates_2(s):
                r, m = rows(s), tiles(s)
                y, e, w, l, t = (a[0:r, 0:m, :] for a in (spy, spe, spw, spl, spr))
                dve.wait_ge(sp_one, s + 1)
                ch.step(v.scalar_tensor_tensor(t, w, -1.0, e, ALU.add, ALU.subtract))
                ch.done(v.reciprocal(e, w))
                ch.wait()
                ch.step(v.tensor_tensor(t, t, e, ALU.mult))
                dve.wait_ge(sp_ln, s + 1)
                ch.step(v.tensor_tensor(l, l, t, ALU.subtract))
                ch.step(v.scalar_tensor_tensor(l, y, 0.0, l, ALU.max, ALU.add))
                if not (isinstance(s, int) and s == 0):
                    dve.wait_ge(small_out, 16 * 2 * s)
                ch.step(v.tensor_scalar(logf[0:r, 0:m, :], l[:, :, 0:6], -1.0, None, ALU.mult))
                v.tensor_tensor(dta[0:r, 0:m, :], l[:, :, 6:12],
                                a_neg[0:r, :].unsqueeze(1).broadcast_to([r, m, 6]), ALU.mult).then_inc(dt_done, 1)

            v.memset(poolw[:, :, :], 0.0)
            v.memset(uT[:, :, 0:PHIST], 0.0)
            v.memset(xr[:, :, 0:CHIST], 0.0).then_inc(init_done, 1)
            v.memset(state[0][:, :], 0.0).then_inc(init_done, 1)
            dve.wait_ge(first_in, 16 * 3)
            for j in range(2):
                norm(0, j)
            h_low(0)
            dve.wait_ge(consts_in, 16 * N_CONST)
            dve.wait_ge(a_exp, 1)
            ch.step(v.tensor_scalar(a_neg[:, :], a_neg[:, :], -1.0, None, ALU.mult))
            dve.wait_ge(st_t, 1)
            v.tensor_copy(state[1][:, :], psT[:, 0, 0:384]).then_inc(init_done, 1)

            def slab(s):
                first = isinstance(s, int) and s == 0
                last = isinstance(s, int) and s == LAST
                if first:
                    for j in range(2):
                        norm(1, j)
                    for k in range(KT):
                        dve.wait_ge(wt_hi, k + 1)
                        v.tensor_tensor(w_tlo[:, k, :], w_tok_raw[k % 3], split_view(w_thi[:, k, :]),
                                        ALU.subtract).then_inc(wt_lo, 1)
                    dve.wait_ge(wt_lo, KT)
                else:
                    scan_0(s - 1, 0)
                    for c in range(tiles(s - 1)):
                        scan_b(s - 1, c)
                        if c + 1 < tiles(s - 1):
                            scan_0(s - 1, c + 1)
                        scan_c(s - 1, c)
                        if not last and c < tiles(s + 1):
                            norm(s + 1, c)
                convolve(s)
                pool_mix(s)
                pool_take(s)
                if not last:
                    h_low(s + 1)
                gates_0(s)
                gates_1(s)
                gates_2(s)

            program(slab, dve, ch, STEPS_1)
            scan_0(LAST, 0)
            scan_b(LAST, 0)
            scan_c(LAST, 0)


STEPS_1 = 84


KEYS_S = PAST + DEC
QG = 4
GROUPS = SEQ // (QG * P)
CT = SEQ // P + PAST // P + 1
KCOLS = CT * P
QCOLS = SEQ + P
KV_X = HD + 4


def attention_constants():
    q, s = np.arange(P)[:, None], np.arange(P)[None, :]
    future = np.where(s > q, np.float32(-1e30), np.float32(0)).astype(np.float32)
    return {"c_future": future}


def attend(nc, sem, cache_k, cache_v, cache_logf, p_logf, s_logf, p_v, s_v, q_ch, k_ch, kc_ch, c_hi_rows, c_lo_rows,
           c_square, c_future, mixed):
    SAMPLE = -1
    NS = 3
    NP = 4
    LEAD = 4
    LAG = 2
    ACT_PREP, DVE_PREP, POOL_PREP, LOADS = 7, 3, 3, 11

    def chunks(G):
        if G == SAMPLE:
            return [(0, 0, SEQ, 3 * P, True)]
        return [(j, c, c * 512, 512 if c < G else (j + 1) * P, c == G) for j in range(QG) for c in range(G + 1)]

    def blocks(G):
        if G == SAMPLE:
            return [(SEQ // P + i, 0, P, i == 2) for i in range(3)]
        return [(QG * G + d, d * P, (QG - d) * P, True) for d in range(QG)] + [(b, 0, 512, False) for b in range(QG * G)]

    def tiles(G):
        return 1 if G == SAMPLE else QG

    def q_first(G):
        return SEQ if G == SAMPLE else G * QG * P

    ORDER = [SAMPLE] + list(range(GROUPS))
    UNITS = [(hh, G) for hh in range(2) for G in ORDER]
    NU = len(UNITS)
    A0 = [sum(len(chunks(G)) for _, G in UNITS[:u]) for u in range(NU + 1)]
    B0 = [sum(len(blocks(G)) for _, G in UNITS[:u]) for u in range(NU + 1)]
    NA, NB = A0[NU], B0[NU]
    WHERE = [(u, i) for u in range(NU) for i in range(len(blocks(UNITS[u][1])))]

    with ExitStack() as ctx:
        def sb(name, shape, dt=F32):
            return ctx.enter_context(nc.sbuf_tensor(name, shape, dt))

        def ps(name, banks):
            return ctx.enter_context(nc.psum_tensor(name, [P, banks, 512], F32))

        square, future = sb("square2", [P, 4, P]), sb("future", [P, P])
        ident, upto, ones = square[:, 0, :], square[:, 1, :], square[:, 3, :]
        zero_one = square[HD:KV_X, 2, HD + 1:HD + 2]
        ident_h, future_h = sb("ident_h", [P, P], BF16), sb("future_h", [P, P], BF16)
        lf, carry, cc = sb("lf", [P, CT, FH]), sb("carry", [P, CT, FH]), sb("cc", [P, CT * FH])
        cT, cT_hi, cT_lo = sb("cT", [P, P]), sb("cT_hi", [P, P], F32R), sb("cT_lo", [P, P])
        k_raw, q_raw, v_raw = sb("k_raw", [P, KCOLS]), sb("q_raw", [P, QCOLS]), sb("v_raw", [P, CT, HD])
        c_raw = sb("c_raw", [P, KCOLS])
        ck = c_raw[:, 0:2 * FOX_W].rearrange("p (i c) -> p i c", i=2)
        ckT = c_raw[:, 2 * FOX_W:2 * FOX_W + 3 * PAST].rearrange("p (b t) -> p b t", b=3)
        k1, k2, k3 = ([sb(f"k{n}_{i}", [P, KCOLS], F32R) for i in range(2)] for n in (1, 2, 3))
        q1, q2 = ([sb(f"q{n}_{i}", [P, QCOLS], F32R) for i in range(2)] for n in (1, 2))
        v_hi, v_lo = ([sb(f"v_{n}{i}", [P, CT, P], F32R) for i in range(2)] for n in ("hi", "lo"))
        p_raw, p_hi, p_lo = sb("p_raw", [P, NP, 512]), sb("p_hi", [P, NP, 512], F32R), sb("p_lo", [P, NP, 512], F32R)
        mx, nmax = sb("mx", [P, 2, QG, GROUPS]), sb("nmax", [P, QG])
        ncol = sb("ncol", [P, QG, HD + 2], F32R)
        oT, ob, rinv = sb("oT", [P, 2, 512]), sb("ob", [P, 2, QG, HD]), sb("rinv", [P, QG])
        A, S, O, X, Z = ps("A2", 2), ps("S2", NS), ps("O2", 1), ps("X2", 1), ps("Z2", 1)

        const2, lf_in, ck_in = sem("const2_in"), sem("logf_in"), sem("cache_k_in")
        lf_clear, cleared, pads_zero = sem("logf_cleared"), sem("rows_cleared"), sem("pads_zero")
        c_mm, c_sum, c_tr, c_row, c_out = sem("c_mm"), sem("c_sum"), sem("c_transposed"), sem("c_rows"), sem("c_out")
        ck_tr, ck_ev, ck_out = sem("ck_tr"), sem("ck_ev"), sem("ck_out")
        pads_in, load_in, c_in = sem("pads_in"), sem("head_in"), sem("head_c_in")
        act_prep, dve_prep, pool_prep = sem("head_hi"), sem("head_rows"), sem("head_lo")
        a_mm, a_red, max_done = sem("a_scores"), sem("a_reduced"), sem("max_done")
        max_tr, max_row = sem("max_transposed"), sem("max_rows")
        s_mm, exps, pv = sem("b_scores"), sem("exps"), sem("values_added")
        lo_done, pool_lo_done = sem("p_lo_done"), sem("p_lo_on_pool_done")
        o_ev, o_tr, o_done = sem("o_copied"), sem("o_transposed"), sem("o_rows_done")
        o_out = [sem(f"o_rows{i}_stored") for i in range(2)]
        dve_chain = sem("dve2_chain")
        block = ctx.enter_context(nc.Block())

        ON_POOL = [G == GROUPS - 1 and b >= QG for _, G in UNITS for b in range(len(blocks(G)))]
        POOLED = [sum(ON_POOL[:i]) for i in range(NB + 1)]

        HB = NB // 2
        PREPARE_AT = [2, 4, 6, 8, 10, 12, 14]

        AHEAD = [(u, k) for u in range(LEAD, NU + LEAD) for k in range(len(chunks(UNITS[u % NU][1])))]

        def due(u):
            return B0[u] if u < NU else NB + B0[u - NU]

        chunk_at = {}
        max_at = {}
        for i, (u, k) in enumerate(AHEAD):
            at = min(i * NB // NA, due(u) - 4)
            chunk_at.setdefault(at, []).append((u, k))
            if k == len(chunks(UNITS[u % NU][1])) - 1:
                max_at.setdefault(min(at + 2, NB - 1), []).append(u)

        def steps(last):
            for i, (u, b) in enumerate(WHERE):
                hh, G = UNITS[u]
                yield "scores", i
                for n in chunk_at.get(i, []):
                    if not (last and n[0] >= NU):
                        yield "chunk", n
                for n in max_at.get(i, []):
                    if not (last and n >= NU):
                        yield "maximum", n
                if i >= LAG:
                    yield "values", i - LAG
                if u and b == LAG - 1:
                    yield "o_copy", u - 1
                if u and b == min(len(blocks(G)) - 1, LAG + 1):
                    yield "o_rows", u - 1
                if i % HB in PREPARE_AT and not (last and hh):
                    yield "prepare", (hh + 1, PREPARE_AT.index(i % HB))
            for i in range(NB - LAG, NB):
                yield "values", i
            yield "o_copy", NU - 1
            yield "o_rows", NU - 1

        def first_steps(do):
            for u in range(LEAD):
                for k in range(len(chunks(UNITS[u][1]))):
                    if "chunk" in do:
                        do["chunk"](0, (u, k))
                if "maximum" in do:
                    do["maximum"](0, u)

        def run(eng, do, chain=None, steps_of_turn=0):
            first_steps(do)

            def turn(p, last):
                for kind, n in steps(last):
                    if kind in do:
                        do[kind](p, n)

            with eng.Fori(0, FH // 2 - 1) as p:
                if chain:
                    chain.enter(p, 0, steps_of_turn)
                turn(p, False)
            if chain:
                chain.leave(FH // 2 - 1)
            turn(FH // 2 - 1, True)

        def unit(u):
            hh, G = UNITS[u % NU]
            return hh, G

        def nu(p, u):
            return p * NU + u

        def na(p, u, k):
            return p * NA + (u // NU * NA + A0[u % NU] + k)

        def nb(p, i):
            return p * NB + i

        def freed(p, i, ring):
            return p * NB + max(0, i - ring + 1) + 1

        def head(p, hh):
            return p * 2 + hh

        def lo_count(p, i):
            n = POOLED[i + 1] if ON_POOL[i] else i + 1 - POOLED[i + 1]
            return p * (POOLED[NB] if ON_POOL[i] else NB - POOLED[NB]) + n

        def lo_half(engine, eng, p, i):
            u, b = WHERE[i]
            w = blocks(unit(u)[1])[b][2]
            eng.wait_ge(exps, 2 * (nb(p, i) + 1) + 1)
            return engine.tensor_tensor(p_lo[:, i % NP, 0:w], p_raw[:, i % NP, 0:w], split_view(p_hi[:, i % NP, 0:w]),
                                        ALU.subtract)

        @block.sync
        def _(sp):
            sp.dma_start(square[:, :, :], c_square).then_inc(const2, 16)
            sp.dma_start(future[:, :], c_future).then_inc(const2, 16)
            sp.dma_start(ck[:, :, :], cache_k.rearrange("(i p) c -> p i c", p=P)).then_inc(ck_in, 16)
            sp.wait_ge(lf_clear, 1)
            sp.dma_start(lf[:, 0:16, :], p_logf.rearrange("(i p) h -> p i h", p=P)).then_inc(lf_in, 16)
            sp.dma_start(lf[:, 16:18, :], cache_logf.rearrange("(i p) h -> p i h", p=P)).then_inc(lf_in, 16)
            sp.dma_start(lf[0:DEC, 18, :], s_logf).then_inc(lf_in, 16)

            def c_rows_in(c_views):
                for r, view in enumerate(c_views):
                    row = c_raw[HD + 2 + r:HD + 3 + r, :]
                    sp.dma_start(row[:, 0:SEQ + PAST].rearrange("o (i t) -> o i t", t=P),
                                 view[:, 0:CT - 1, :]).then_inc(c_in, 16)
                    sp.dma_start(row[:, SEQ + PAST:SEQ + KEYS_S], view[:, CT - 1, 0:DEC]).then_inc(c_in, 16)

            def head_in(hn, free=None):
                head_k, head_q = k_ch[bass.ds(hn * HD, HD), :], q_ch[bass.ds(hn * HD, HD), :]
                head_kc = kc_ch[bass.ds(hn * HD, HD), :]
                c_views = [src.rearrange("(i h) t -> h i t", h=FH)[bass.ds(hn, 1), :, :] for src in (c_hi_rows, c_lo_rows)]
                v_views = [(a, z, src.rearrange("(i p) c -> p i c", p=P)[:, :, bass.ds(hn * HD, HD)])
                           for a, z, src in ((0, 16, p_v), (16, 18, cache_v))]
                head_sv = s_v[:, bass.ds(hn * HD, HD)]
                if free is not None:
                    sp.wait_ge(dve_prep, DVE_PREP * free)
                    c_rows_in(c_views)
                    sp.wait_ge(pool_prep, POOL_PREP * free)
                for r in (0, HD):
                    sp.dma_start(q_raw[r:r + HD, 0:TOKENS], head_q).then_inc(load_in, 16)
                    sp.dma_start(k_raw[r:r + HD, 0:SEQ], head_k[:, 0:SEQ]).then_inc(load_in, 16)
                    sp.dma_start(k_raw[r:r + HD, SEQ + PAST:SEQ + KEYS_S], head_k[:, SEQ:TOKENS]).then_inc(load_in, 16)
                for a, z, view in v_views:
                    sp.dma_start(v_raw[:, a:z, :], view).then_inc(load_in, 16)
                sp.dma_start(v_raw[0:DEC, 18, :], head_sv).then_inc(load_in, 16)
                if free is None:
                    sp.wait_ge(ck_ev, 1)
                    sp.dma_start(kc_ch.rearrange("(b p) t -> p b t", p=P), ckT).then_inc(ck_out, 16)
                    sp.wait_ge(ck_out, 16)
                for r in (0, HD):
                    sp.dma_start(k_raw[r:r + HD, SEQ:SEQ + PAST], head_kc).then_inc(load_in, 16)
                if free is None:
                    sp.wait_ge(c_row, 3)
                    sp.dma_start(c_hi_rows, split_view(cT_hi[0:CT * FH, :])).then_inc(c_out, 16)
                    sp.dma_start(c_lo_rows, cT_lo[0:CT * FH, :]).then_inc(c_out, 16)
                    sp.wait_ge(cleared, 3)
                    sp.dma_start(c_raw[HD + 2:KV_X, KCOLS - DEC:KCOLS],
                                 c_future[0:2, HD:HD + DEC]).then_inc(pads_in, 16)
                    sp.wait_ge(c_out, 32)
                    c_rows_in(c_views)

            head_in(0)
            head_in(1, free=1)

            def o_rows(p, u):
                hh, G = unit(u)
                n = DEC if G == SAMPLE else P
                cols = bass.ds(p * 2 * HD + (MIX_FOX + hh * HD), HD)
                sp.wait_ge(o_done, nu(p, u) + 2)
                if G == SAMPLE:
                    sp.dma_start(mixed[SEQ:TOKENS, cols], ob[0:DEC, u % 2, 0, :]).then_inc(o_out[u % 2], 16)
                else:
                    sp.dma_start(mixed[G * 512:(G + 1) * 512, cols].rearrange("(i p) c -> p i c", p=P),
                                 ob[:, u % 2, :, :]).then_inc(o_out[u % 2], 16)

            def prepare(p, n):
                hh, k = n
                if k == ACT_PREP - 1 and not (isinstance(p, int) and hh == 1):
                    head_in(head(p, hh + 1), head(p, hh + 1))

            run(sp, {"o_rows": o_rows, "prepare": prepare})
            for k in range(2):
                sp.wait_ge(o_out[k], 16 * (FH // 2 * NU // 2 + 1))

        @block.gpsimd
        def _(pool):
            pool.wait_ge(ck_out, 16)
            nc.gpsimd.memset(c_raw[HD:KV_X, :], 1.0).then_inc(cleared, 1)

            def prepare(p, n):
                hh, k = n
                if k < ACT_PREP - 1:
                    return
                s, first = hh % 2, POOL_PREP * head(p, hh)
                g = nc.gpsimd
                pool.wait_ge(act_prep, ACT_PREP * (head(p, hh) + 1))
                g.tensor_tensor(k2[s][0:HD, :], k_raw[0:HD, :], split_view(k1[s][0:HD, :]),
                                ALU.subtract).then_inc(pool_prep, 1)
                pool.wait_ge(pool_prep, first + 1)
                g.tensor_tensor(q1[s][HD:P, :], q_raw[HD:P, :], split_view(q1[s][HD:P, :]),
                                ALU.subtract).then_inc(pool_prep, 1)
                pool.wait_ge(pool_prep, first + 2)
                g.tensor_tensor(v_lo[s][:, :, 0:HD], v_raw[:, :, :], split_view(v_hi[s][:, :, 0:HD]),
                                ALU.subtract).then_inc(pool_prep, 1)
                pool.wait_ge(pool_prep, first + 3)

            def scores(p, i):
                if ON_POOL[i]:
                    lo_half(nc.gpsimd, pool, p, i).then_inc(pool_lo_done, 1)

            prepare(0, (0, ACT_PREP - 1))
            run(pool, {"prepare": prepare, "scores": scores})

        @block.tensor
        def _(pe):
            for s, n in ((pv, 1), (max_tr, 1), (o_tr, 2)):
                pe.sem_inc(s, n)
            pe.wait_ge(const2, 32)
            pe.wait_ge(ck_in, 16)
            for i in range(2):
                for b in range(3):
                    mm = pe.transpose(A[:, i, b * P:(b + 1) * P], ck[:, i, b * P:(b + 1) * P], ident)
            mm.then_inc(ck_tr, 1)
            pe.wait_ge(lf_in, 48)
            lff = lf[:, :, :].rearrange("p i h -> p (i h)")
            pe.matmul(S[:, 0, 0:CT * FH], upto, lff, start=True, stop=True)
            pe.matmul(S[:, 1, 0:CT * FH], ones, lff, start=True, stop=True).then_inc(c_mm, 1)
            pe.wait_ge(c_sum, 1)
            pe.transpose(S[0:CT * FH, 2, 0:P], cc[:, :], ident).then_inc(c_tr, 1)
            pe.wait_ge(ck_ev, 1)
            pe.wait_ge(c_row, 3)
            pe.wait_ge(cleared, 3)

            def future_in(out, lhs, rhs):
                return pe.matmul(out, lhs[:, :], rhs[:, :], start=False, stop=True)

            def chunk(p, n):
                u, k = n
                hh, G = unit(u)
                j, _, first, w, masked = chunks(G)[k]
                if G == SAMPLE:
                    h = head(p, u // len(ORDER))
                    pe.wait_ge(act_prep, ACT_PREP * (h + 1))
                    pe.wait_ge(dve_prep, DVE_PREP * (h + 1))
                pe.wait_ge(a_red, 2 + na(p, u, k) - 2 + 1)
                slot = (A0[u % NU] + k) % 2
                lhs = q2[hh][0:KV_X, q_first(G) + j * P:q_first(G) + (j + 1) * P]
                mm = pe.matmul(A[:, slot, 0:w], lhs, k3[hh][0:KV_X, first:first + w], start=True, stop=not masked)
                if masked:
                    mm = future_in(A[:, slot, w - P:w], ident_h, future_h)
                mm.then_inc(a_mm, 1)

            def maximum(p, u):
                pe.wait_ge(max_done, nu(p, u) + 1)
                pe.wait_ge(max_row, nu(p, u) + 1)
                for j in range(tiles(unit(u)[1])):
                    mm = pe.transpose(X[0:HD + 2, 0, j * P:(j + 1) * P], split_view(ncol[:, j, :]), ident)
                mm.then_inc(max_tr, 1)

            def scores(p, i):
                u, b = WHERE[i]
                hh, G = unit(u)
                kb, at, w, masked = blocks(G)[b]
                if b == 0:
                    pe.wait_ge(max_row, nu(p, u) + 2)
                    if G == SAMPLE:
                        pe.wait_ge(pool_prep, POOL_PREP * (head(p, hh) + 1))
                pe.wait_ge(exps, 2 * freed(p, i, NS) - 1)
                q0 = q_first(G) + at
                out = S[:, i % NS, 0:w]
                pe.matmul(out, k1[hh][:, kb * P:(kb + 1) * P], q1[hh][:, q0:q0 + w], start=True, stop=False)
                mm = pe.matmul(out, k2[hh][0:KV_X, kb * P:(kb + 1) * P], q2[hh][0:KV_X, q0:q0 + w],
                               start=False, stop=not masked)
                if masked:
                    mm = future_in(S[:, i % NS, 0:P], future_h, ident_h)
                mm.then_inc(s_mm, 1)

            def values(p, i):
                u, b = WHERE[i]
                hh, G = unit(u)
                kb, at, w, _ = blocks(G)[b]
                if b == 0:
                    pe.wait_ge(o_ev, nu(p, u) + 1)
                pe.wait_ge(pool_lo_done if ON_POOL[i] else lo_done, lo_count(p, i))
                end = b == len(blocks(G)) - 1
                for m, (v, x) in enumerate(((v_hi, p_hi), (v_lo, p_hi), (v_hi, p_lo))):
                    mm = pe.matmul(O[:, 0, at:at + w], v[hh][:, kb, :], x[:, i % NP, 0:w],
                                   start=(b == 0 and m == 0), stop=(end and m == 2))
                mm.then_inc(pv, 1)

            def o_rows(p, u):
                pe.wait_ge(o_ev, nu(p, u) + 2)
                pe.wait_ge(o_done, nu(p, u) + 1)
                for j in range(tiles(unit(u)[1])):
                    mm = pe.transpose(Z[:, 0, j * P:j * P + HD + 1], oT[0:HD + 1, u % 2, j * P:(j + 1) * P],
                                      ident[0:HD + 1, 0:HD + 1])
                mm.then_inc(o_tr, 1)

            run(pe, {"chunk": chunk, "maximum": maximum, "scores": scores, "values": values, "o_rows": o_rows})

        @block.scalar
        def _(act):
            act.sem_inc(exps, 1)
            act.sem_inc(o_ev, 1)
            act.sem_inc(max_row, 1)
            act.wait_ge(ck_tr, 1)
            nc.scalar.activation(ckT[:, :, :].rearrange("p b (i t) -> p i b t", i=2),
                                 A[:, :, 0:384].rearrange("p i (b t) -> p i b t", b=3), ACT.Copy).then_inc(ck_ev, 1)
            act.wait_ge(c_tr, 1)
            for to in (cT, cT_hi):
                nc.scalar.activation(to[0:CT * FH, :], S[0:CT * FH, 2, 0:P], ACT.Copy, scale=-1.0).then_inc(c_row, 1)
            act.wait_ge(pads_zero, 3)

            def prepare(p, n):
                hh, k = n
                s = hh % 2
                if k == 0:
                    act.wait_ge(load_in, 16 * LOADS * (head(p, hh) + 1))
                    act.wait_ge(pv, nb(p, B0[len(ORDER)] * (hh - 1)) + 1 if hh else 1)
                if k == 4:
                    act_op = (v_hi[s][:, :, 0:HD], v_raw[:, :, :])
                elif k == 5:
                    act_op = (k3[s][0:HD, :], k_raw[0:HD, :])
                elif k == 6:
                    act_op = (q2[s][0:HD, :], q_raw[0:HD, :])
                else:
                    to, src, w = ((k1, k_raw, KCOLS), (q1, q_raw, QCOLS))[k // 2]
                    cols = slice(k % 2 * (w // 2), (k % 2 + 1) * (w // 2))
                    act_op = (to[s][:, cols], src[:, cols])
                nc.scalar.activation(*act_op, ACT.Copy).then_inc(act_prep, 1)

            def maximum(p, u):
                hh, G = unit(u)
                w = tiles(G) * P
                act.wait_ge(max_tr, nu(p, u) + 2)
                nc.scalar.activation(q2[hh][HD:HD + 2, q_first(G):q_first(G) + w], X[HD:HD + 2, 0, 0:w],
                                     ACT.Copy).then_inc(max_row, 1)

            def scores(p, i):
                u, b = WHERE[i]
                w = blocks(unit(u)[1])[b][2]
                act.wait_ge(s_mm, nb(p, i) + 1)
                act.wait_ge(pv, freed(p, i, NP))
                for to in (p_raw, p_hi):
                    nc.scalar.activation(to[:, i % NP, 0:w], S[:, i % NS, 0:w], ACT.Exp).then_inc(exps, 1)

            def o_copy(p, u):
                w = tiles(unit(u)[1]) * P
                act.wait_ge(pv, nb(p, B0[u + 1]) + 1)
                act.wait_ge(o_tr, nu(p, u) + 1)
                nc.scalar.activation(oT[0:HD + 1, u % 2, 0:w], O[0:HD + 1, 0, 0:w], ACT.Copy).then_inc(o_ev, 1)

            for k in range(ACT_PREP):
                prepare(0, (0, k))
            run(act, {"prepare": prepare, "maximum": maximum, "scores": scores, "o_copy": o_copy})

        @block.vector
        def _(dve):
            ch = Chain(dve, dve_chain)
            v = nc.vector
            dve.sem_inc(a_red, 2)
            dve.sem_inc(o_done, 1)
            for k in range(2):
                dve.sem_inc(o_out[k], 16)
            v.memset(lf[:, :, :], 0.0).then_inc(lf_clear, 1)
            ch.done(v.memset(carry[:, :, :], 0.0))
            v.memset(k_raw[:, SEQ + KEYS_S:KCOLS], 0.0).then_inc(pads_zero, 1)
            v.memset(q_raw[:, TOKENS:QCOLS], 0.0).then_inc(pads_zero, 1)
            v.memset(v_raw[DEC:P, CT - 1, :], 0.0).then_inc(pads_zero, 1)
            ch.done(v.memset(p_raw[:, 0, 0:HD], 0.0))
            dve.wait_ge(const2, 32)
            ch.wait()
            for j in range(QG):
                v.tensor_copy(ncol[:, j, 0:HD], p_raw[:, 0, 0:HD])
            zeros = p_raw[:, 0, 0:HD].unsqueeze(1).broadcast_to([P, CT, HD])
            one = ones[:, 0:1].unsqueeze(1).broadcast_to([P, CT, 1])
            for i in range(2):
                v.tensor_copy(v_lo[i][:, :, HD:P], zeros)
                ch.step(v.tensor_copy(v_hi[i][:, :, HD:P], zeros))
                v.tensor_copy(v_hi[i][:, :, HD:HD + 1], one)
            v.tensor_copy(ident_h[:, :], ident).then_inc(cleared, 1)
            v.tensor_copy(future_h[:, :], future[:, :]).then_inc(cleared, 1)
            dve.wait_ge(c_mm, 1)
            ch.wait()
            tot = S[:, 1, 0:CT * FH].rearrange("p (i h) -> p i h", h=FH)
            for i in range(1, CT):
                if i != SEQ // P:
                    ch.step(v.tensor_tensor(carry[:, i, :], carry[:, i - 1, :], tot[:, i - 1, :], ALU.add))
            v.tensor_tensor(cc[:, :], S[:, 0, 0:CT * FH], carry[:, :, :].rearrange("p i h -> p (i h)"),
                            ALU.add).then_inc(c_sum, 1)
            dve.wait_ge(c_row, 2)
            v.tensor_tensor(cT_lo[0:CT * FH, :], cT[0:CT * FH, :], split_view(cT_hi[0:CT * FH, :]),
                            ALU.subtract).then_inc(c_row, 1)

            def prepare(p, n):
                hh, k = n
                s = hh % 2
                if k >= DVE_PREP:
                    return
                if k == 0:
                    dve.wait_ge(c_in, 16 * 4 * (head(p, hh) + 1))
                    dve.wait_ge(pv, nb(p, B0[len(ORDER)] * (hh - 1)) + 1 if hh else 1)
                    v.tensor_copy(k2[s][HD:KV_X, :], c_raw[HD:KV_X, :]).then_inc(dve_prep, 1)
                elif k == 1:
                    v.tensor_copy(k3[s][HD:KV_X, :], c_raw[HD:KV_X, :]).then_inc(dve_prep, 1)
                else:
                    v.tensor_copy(q2[s][HD:KV_X, :], zero_one.broadcast_to([KV_X - HD, QCOLS])).then_inc(dve_prep, 1)

            def chunk(p, n):
                u, k = n
                _, G = unit(u)
                j, c, _, w, _ = chunks(G)[k]
                dve.wait_ge(a_mm, na(p, u, k) + 1)
                v.tensor_reduce(mx[:, u % 2, j, c:c + 1], A[:, (A0[u % NU] + k) % 2, 0:w], AX.X,
                                ALU.max).then_inc(a_red, 1)
                if k < len(chunks(G)) - 1:
                    return
                t, m = tiles(G), c + 1
                dve.wait_ge(a_red, 2 + na(p, u, k) + 1)
                dve.wait_ge(max_tr, nu(p, u) + 1)
                ch.step(v.tensor_reduce(nmax[:, 0:t], mx[:, u % 2, 0:t, 0:m], AX.X, ALU.max, negate=True))
                col = ncol[:, 0:t, HD:HD + 1].rearrange("p t o -> p (t o)")
                low = ncol[:, 0:t, HD + 1:HD + 2].rearrange("p t o -> p (t o)")
                ch.step(v.tensor_copy(col, nmax[:, 0:t]))
                v.tensor_tensor(low, nmax[:, 0:t], split_view(col), ALU.subtract).then_inc(max_done, 1)

            def scores(p, i):
                if not ON_POOL[i]:
                    lo_half(v, dve, p, i).then_inc(lo_done, 1)

            def o_rows(p, u):
                t = tiles(unit(u)[1])
                z = Z[:, 0, :].rearrange("p (t c) -> p t c", c=P)[:, 0:t, :]
                dve.wait_ge(o_tr, nu(p, u) + 3)
                dve.wait_ge(o_out[u % 2], 16 * (p * (NU // 2) + u // 2 + 1))
                ch.step(v.reciprocal(rinv[:, 0:t].unsqueeze(2), z[:, :, HD:HD + 1]))
                v.tensor_tensor(ob[:, u % 2, 0:t, :], z[:, :, 0:HD],
                                rinv[:, 0:t].unsqueeze(2).broadcast_to([P, t, HD]), ALU.mult).then_inc(o_done, 1)

            dve.wait_ge(pads_in, 16)
            for k in range(DVE_PREP):
                prepare(0, (0, k))
            run(dve, {"prepare": prepare, "chunk": chunk, "scores": scores, "o_rows": o_rows}, ch, STEPS_2)


STEPS_2 = 30


NB4 = 4
W4 = TOKENS // NB4


class Ahead:

    def __init__(self, nc, sem, ctx):
        self.y = ctx.enter_context(nc.sbuf_tensor("yT", [P, KT, W4], F32))
        self.raw = [ctx.enter_context(nc.sbuf_tensor(f"w_raw{i}", [P, 2 * KT, P], F32)) for i in range(2)]
        self.w_in = [sem(f"w{i}_in") for i in range(2)]
        self.x0_in = [sem(f"x0_part{i}_in") for i in range(KT // 2)]

    def load_x(self, eng, h2_ch):
        x0 = h2_ch.rearrange("(k p) t -> p k t", p=P)
        for i in range(KT // 2):
            eng.dma_start(self.y[:, 2 * i:2 * i + 2, :], x0[:, 2 * i:2 * i + 2, 0:W4]).then_inc(self.x0_in[i], 16)

    def load_w(self, eng, w_gate, w_up):
        for f in range(2):
            for i, w in enumerate((w_gate, w_up)):
                eng.dma_start(self.raw[f][:, i * KT:(i + 1) * KT, :],
                              w.rearrange("(k p) n -> p k n", p=P)[:, :, f * P:(f + 1) * P]).then_inc(self.w_in[f], 16)


class Twice:

    def __init__(self, r, c=None):
        self.r, self.c = (0, r) if c is None else (r, c)
        self.n = self.r * 2 + self.c
        self.half = self.r + self.c // 2
        self.odd = self.c % 2

    def __add__(self, d):
        return Twice(self.r, self.c + d)

    def under(self, n):
        return isinstance(self.r, int) and self.n < n

    def over(self, n):
        return isinstance(self.r, int) and self.n >= n


def mix_out(nc, sem, w_out, ln_g, ln_b, mixed, h_rows, c_square, h2_ch, w_gate, w_up, ahead):
    TILES = SEQ // P + 1
    LAST = TILES - 1

    def rows(i):
        return DEC if i.over(LAST) else P

    with ExitStack() as ctx:
        def sb(name, shape, dt=F32):
            return ctx.enter_context(nc.sbuf_tensor(name, shape, dt))

        def ps(name):
            return ctx.enter_context(nc.psum_tensor(name, [P, 2, 512], F32))

        ident = sb("ident3", [P, P])
        lng, lnb = sb("lng3", [P, D]), sb("lnb3", [P, D])
        w_raw = sb("wo_raw", [P, KT, D])
        w_hi, w_lo = sb("wo_hi", [P, KT, D], F32R), sb("wo_lo", [P, KT, D], F32R)
        half, idle = sb("half3", [P, 1]), sb("idle3", [1, 1])
        mrow = [sb(f"mrow{i}", [P, D]) for i in range(2)]
        hrow = [sb(f"hrow{i}", [P, D]) for i in range(2)]
        m_hi = [sb(f"m_hi{i}", [P, KT, P], F32R) for i in range(2)]
        m_lo = [sb(f"m_lo{i}", [P, KT, P], F32R) for i in range(2)]
        stats, mv, rstd = sb("stats3", [P, 2, 6]), sb("mv3", [P, 2]), sb("rstd3", [P, 1])
        hT = [sb(f"h2T{i}", [P, KT, P]) for i in range(2)]
        A, B = ps("A"), ps("B")
        Y = [ps(f"Y{i}") for i in range(2)]

        const_in, w_in = sem("const3_in"), [sem(f"wo{i}_in") for i in range(KT // 2)]
        w_hi_done, w_lo_done, half_done = sem("wo_hi_done"), sem("wo_lo_done"), sem("half3_done")
        m_in, h_in = [sem(f"mixed{i}_in") for i in range(2)], [sem(f"h{i}_in") for i in range(2)]
        a_tr, a_hi, a_lo = sem("mixed_transposed"), sem("mixed_hi"), sem("mixed_lo")
        y_mm, y_sum = sem("y_mm"), sem("y_summed")
        moments, rstd_done, h2_done = sem("moments3"), sem("rstd3_done"), sem("h2_done")
        b_tr, b_take, h2_out = sem("h2_transposed"), sem("h2_taken"), [sem(f"h2_stored{i}") for i in range(2)]
        dve_chain = sem("dve3_chain")
        block = ctx.enter_context(nc.Block())

        def program(body, eng, chain=None, steps=0):
            body(Twice(0))
            with eng.Fori(0, (TILES - 5) // 2) as t:
                if chain:
                    chain.enter(t, 0, steps)
                for u in range(2):
                    body(Twice(t, 1 + u))
            if chain:
                chain.leave((TILES - 5) // 2)
            for i in range(TILES - 4, TILES):
                body(Twice(i))

        @block.sync
        def _(sp):
            sp.dma_start(ident[:, :], c_square[:, 0, :]).then_inc(const_in, 16)

            def m_load(i):
                r = rows(i)
                if not i.under(2):
                    sp.wait_ge(a_tr, i.n - 1)
                sp.dma_start(mrow[i.odd][0:r, :], mixed[bass.ds(i.n * P, r), :]).then_inc(m_in[i.odd], 16)

            def h_load(i):
                r = rows(i)
                if not i.under(2):
                    sp.wait_ge(b_tr, i.n - 1)
                sp.dma_start(hrow[i.odd][0:r, :], h_rows[bass.ds(i.n * P, r), :]).then_inc(h_in[i.odd], 16)

            m_load(Twice(0))
            for k in range(KT // 2):
                sp.dma_start(w_raw[:, 2 * k:2 * k + 2, :], w_out.rearrange("(k p) n -> p k n", p=P)[:, 2 * k:2 * k + 2, :]
                             ).then_inc(w_in[k], 16)
                if k == 0:
                    m_load(Twice(1))
                    h_load(Twice(0))
            sp.dma_start(lng[:, :], load_rows(ln_g)).then_inc(const_in, 16)
            sp.dma_start(lnb[:, :], load_rows(ln_b)).then_inc(const_in, 16)

            def body(i):
                if not i.over(LAST - 1):
                    m_load(i + 2)
                if not i.over(LAST):
                    h_load(i + 1)

            program(body, sp)
            ahead.load_w(sp, w_gate, w_up)
            n = -(-W4 // P)
            sp.wait_ge(h2_out[0], 16 * ((n + 1) // 2))
            sp.wait_ge(h2_out[1], 16 * (n // 2))
            ahead.load_x(sp, h2_ch)

        @block.gpsimd
        def _(pool):
            nc.gpsimd.memset(half[:, :], -0.5).then_inc(half_done, 1)
            pool.wait_ge(half_done, 1)

            def body(i):
                pool.wait_ge(moments, i.n + 1)
                nc.gpsimd.tensor_tensor(rstd[0:rows(i), :], mv[0:rows(i), 1:2], half[0:rows(i), :],
                                        ALU.pow).then_inc(rstd_done, 1)

            program(body, pool)

        @block.tensor
        def _(pe):
            pe.wait_ge(const_in, 16)

            def over(dst, src, r):
                for b in range(KT):
                    mm = pe.transpose(dst[:, b // 4, (b % 4) * P:(b % 4) * P + r], src[0:r, b * P:(b + 1) * P],
                                      ident[0:r, 0:r])
                return mm

            def mixed_over(i):
                pe.wait_ge(m_in[i.odd], 16 * (i.half + 1))
                if not i.under(1):
                    pe.wait_ge(a_lo, i.n)
                over(A, mrow[i.odd], rows(i)).then_inc(a_tr, 1)

            def h2_over(i):
                pe.wait_ge(h2_done, i.n + 1)
                if not i.under(1):
                    pe.wait_ge(b_take, i.n)
                over(B, hrow[i.odd], rows(i)).then_inc(b_tr, 1)

            def body(i):
                k = i.odd
                if not i.over(LAST):
                    mixed_over(i + 1)
                pe.wait_ge(a_lo, i.n + 1)
                if not i.under(2):
                    pe.wait_ge(y_sum, i.n - 1)
                for n in range(2):
                    for b in range(KT):
                        if i.under(1) and n == 0:
                            pe.wait_ge(w_lo_done, b + 1)
                        for m, (x, w) in enumerate(((m_hi, w_hi), (m_hi, w_lo), (m_lo, w_hi))):
                            mm = pe.matmul(Y[k][:, n, :], x[k][:, b, :], w[:, b, n * 512:(n + 1) * 512],
                                           start=(b == 0 and m == 0), stop=(b == KT - 1 and m == 2))
                mm.then_inc(y_mm, 1)
                if not i.under(1):
                    h2_over(i + -1)

            mixed_over(Twice(0))
            program(body, pe)
            h2_over(Twice(LAST))

        @block.scalar
        def _(act):
            def tiled(ap, r):
                return ap[:, :, :].rearrange("p n (b c) -> p (n b) c", c=P)[:, :, 0:r]

            def hi(i):
                r = rows(i)
                act.wait_ge(a_tr, i.n + 1)
                if not i.under(2):
                    act.wait_ge(y_mm, i.n - 1)
                nc.scalar.activation(m_hi[i.odd][:, :, 0:r], tiled(A, r), ACT.Copy).then_inc(a_hi, 1)

            def take(i):
                r = rows(i)
                act.wait_ge(b_tr, i.n + 1)
                if not i.under(2):
                    act.wait_ge(h2_out[i.odd], 16 * i.half)
                nc.scalar.activation(hT[i.odd][:, :, 0:r], tiled(B, r), ACT.Copy).then_inc(b_take, 1)
                act.wait_ge(b_take, i.n + 1)
                act.dma_start(h2_ch.rearrange("(k p) t -> p k t", p=P)[:, :, bass.ds(i.n * P, r)],
                              hT[i.odd][:, :, 0:r]).then_inc(h2_out[i.odd], 16)

            def body(i):
                if not i.over(LAST):
                    hi(i + 1)
                if not i.under(1):
                    take(i + -1)

            hi(Twice(0))
            for k in range(KT):
                if k % 2 == 0:
                    act.wait_ge(w_in[k // 2], 16)
                nc.scalar.activation(w_hi[:, k, :], w_raw[:, k, :], ACT.Copy).then_inc(w_hi_done, 1)
            program(body, act)
            take(Twice(LAST))
            act.wait_ge(h2_out[0], 16 * ((TILES + 1) // 2))
            act.wait_ge(h2_out[1], 16 * (TILES // 2))

        @block.vector
        def _(dve):
            ch = Chain(dve, dve_chain)
            v = nc.vector

            def lo(i):
                r, k = rows(i), i.odd
                dve.wait_ge(a_hi, i.n + 1)
                v.tensor_tensor(m_lo[k][:, :, 0:r], A[:, :, :].rearrange("p n (b c) -> p (n b) c", c=P)[:, :, 0:r],
                                split_view(m_hi[k][:, :, 0:r]), ALU.subtract).then_inc(a_lo, 1)

            def norm(i):
                r, k = rows(i), i.odd
                x = hrow[k][0:r, :]
                dve.wait_ge(h_in[k], 16 * (i.half + 1))
                dve.wait_ge(y_mm, i.n + 1)
                v.scalar_tensor_tensor(x, x, ALPHA, Y[k][0:r, :, :].rearrange("p n c -> p (n c)"),
                                       ALU.mult, ALU.add).then_inc(y_sum, 1)
                dve.wait_ge(y_sum, i.n + 1)
                for u in range(2):
                    ch.done(v.bn_stats(stats[0:r, u, :], x[:, u * 512:(u + 1) * 512]))
                ch.wait()
                v.memset(idle[:, :], 0.0)
                ch.step(v.bn_aggr(mv[0:r, :], stats[0:r, :, :]))
                v.tensor_scalar(mv[0:r, 1:2], mv[0:r, 1:2], EPS, None, ALU.add).then_inc(moments, 1)
                dve.wait_ge(rstd_done, i.n + 1)
                ch.step(v.tensor_scalar(x, x, mv[0:r, 0:1], rstd[0:r, 0:1], ALU.subtract, ALU.mult))
                ch.step(v.tensor_tensor(x, x, lng[0:r, :], ALU.mult))
                v.tensor_tensor(x, x, lnb[0:r, :], ALU.add).then_inc(h2_done, 1)

            def body(i):
                if not i.over(LAST):
                    lo(i + 1)
                norm(i)

            lo(Twice(0))
            for k in range(KT):
                dve.wait_ge(w_hi_done, k + 1)
                v.tensor_tensor(w_lo[:, k, :], w_raw[:, k, :], split_view(w_hi[:, k, :]),
                                ALU.subtract).then_inc(w_lo_done, 1)
            dve.wait_ge(const_in, 48)
            program(body, dve, ch, STEPS_3)


STEPS_3 = 10


def feed_forward(nc, sem, w_gate, w_up, w_down, ln_g, ln_b, h2_ch, c_square, y_prompt, y_sample, ahead):
    NB, W = NB4, W4
    H = W // 2
    FS = FT // 2
    UNITS = 2 * (FS + KT)
    NO = 5

    def row_tile(t, r):
        if isinstance(t, int) and t == NB - 1:
            return ((W - DEC) // 4 * r, (W - DEC) // 4) if r < NO - 1 else (W - DEC, DEC)
        a = -(-W // NO)
        return a * r, min(a, W - a * r)

    with ExitStack() as ctx:
        def sb(name, shape, dt=F32):
            return ctx.enter_context(nc.sbuf_tensor(name, shape, dt))

        ident = sb("ident4", [P, P])
        lng, lnb = sb("lng4", [P, D]), sb("lnb4", [P, D])
        half, idle = sb("half4", [P, 1]), sb("idle4", [1, 1])
        x_hi, x_lo = sb("x_hi", [P, KT, W], F32R), sb("x_lo", [P, KT, W], F32R)
        a_hi, a_lo = sb("act_hi", [P, FS, W], F32R), sb("act_lo", [P, FS, W], F32R)
        raw, yT = ahead.raw, ahead.y
        whi = [sb(f"w_hi{i}", [P, 2 * KT, P], F32R) for i in range(2)]
        wlo = [sb(f"w_lo{i}", [P, 2 * KT, P], F32R) for i in range(2)]
        sl = [sb(f"slice{i}", [P, W]) for i in range(2)]
        act_t = [sb(f"silu{i}", [P, H]) for i in range(2)]
        ob = [sb(f"y_rows{i}", [P, D]) for i in range(2)]
        stats, mv, rstd = sb("stats4", [P, 2, 6]), sb("mv4", [P, 2]), sb("rstd4", [P, 1])
        G = [ctx.enter_context(nc.psum_tensor(f"G{i}", [P, 2, 512], F32)) for i in range(2)]
        Y = [ctx.enter_context(nc.psum_tensor(f"Yd{i}", [P, 2, 512], F32)) for i in range(2)]

        const_in = sem("const4_in")
        w_in, s_in = ahead.w_in, [sem(f"slice{i}_in") for i in range(2)]
        hi_done, lo_done, d_done = sem("w_hi_done"), sem("w_lo_done"), sem("down_done")
        s_hi, s_used = sem("slice_hi"), sem("slice_used")
        x0_in, x0_done = ahead.x0_in, sem("x0_done")
        g_done, silu_done, gated = sem("gate_up_done"), sem("silu4_done"), sem("gated")
        act_hi, act_done = sem("act_hi_done"), sem("act_done")
        y_taken, tr_done, ln_taken = sem("y_taken"), sem("y_transposed"), sem("ln_taken")
        moments, rstd_done, half_done = sem("moments4"), sem("rstd4_done"), sem("half4_done")
        rows_done, y_out = sem("y_rows_done"), [sem(f"y_rows{i}_stored") for i in range(2)]
        dve_chain = sem("dve4_chain")
        C = 2
        block = ctx.enter_context(nc.Block())

        def wn(t, sec, m):
            return t * UNITS + (m.n + sec * (FS + KT))

        def wn_half(t, sec, m):
            return t * (UNITS // 2) + (m + sec * (FS + KT)).half

        def slot(sec, m):
            return (m + sec * (FS + KT)).odd

        def gh(t, sec, f, h):
            return (t * 2 + sec) * (2 * FS) + f.n * 2 + h

        def dn(t, sec, b):
            return (t * 2 + sec) * KT + b.n

        def sn(t, sec, b):
            return t * 2 * KT + sec * KT + b.n

        def sections(eng, gate, down, has_next, t, after=None):
            for sec in range(2):
                tail = sec == 0 and not (isinstance(t, int) and t == 0)
                first = NO + 4 if tail else 3
                for f in range(first):
                    gate(t, sec, Twice(f))
                    if tail and after and 1 <= f <= NO + 2:
                        after(t - 1, f - 1)
                with eng.Fori(0, (FS - first) // 2) as r:
                    for u in range(2):
                        gate(t, sec, Twice(r, first + u))
                for b in range(2):
                    down(t, sec, Twice(b), has_next)
                with eng.Fori(0, (KT - 2) // 2) as r:
                    for u in range(2):
                        down(t, sec, Twice(r, 2 + u), has_next)

        def program(eng, gate, down, after=None, chain=None, steps=0):
            sections(eng, gate, down, True, 0)
            with eng.Fori(1, NB - 1) as t:
                if chain:
                    chain.enter(t, 1, steps)
                sections(eng, gate, down, True, t, after)
            if chain:
                chain.leave(NB - 2)
            sections(eng, gate, down, False, NB - 1, after)

        @block.sync
        def _(sp):
            def slice_in(n, k, src):
                sp.wait_ge(s_used, C + n - 2 + 1)
                sp.dma_start(sl[k][:, :], src).then_inc(s_in[k], 16)

            def gate(t, sec, f):
                if isinstance(t, int) and t == 0 and sec == 0 and f.under(2):
                    return
                k = slot(sec, f)
                sp.wait_ge(lo_done, C + wn(t, sec, f) - 2 + 1)
                for i, w in enumerate((w_gate, w_up)):
                    sp.dma_start(raw[k][:, i * KT:(i + 1) * KT, :],
                                 w.rearrange("(k p) n -> p k n", p=P)[:, :, bass.ds((f.n + sec * FS) * P, P)]
                                 ).then_inc(w_in[k], 16)

            def down(t, sec, b, has_next):
                m = b + FS
                k = slot(sec, m)
                sp.wait_ge(lo_done, C + wn(t, sec, m) - 2 + 1)
                for a, z in ((0, 6), (6, FS)):
                    sp.dma_start(raw[k][:, a:z, :],
                                 w_down[(sec * FS + a) * P:(sec * FS + z) * P, bass.ds(b.n * P, P)]
                                 .rearrange("(f p) n -> p f n", p=P)).then_inc(w_in[k], 16)
                if sec == 0:
                    slice_in(sn(t, 0, b), b.odd, h2_ch[bass.ds(b.n * P, P), bass.ds(t * W, W)])
                elif has_next:
                    slice_in(sn(t, 1, b), b.odd, h2_ch[bass.ds(b.n * P, P), bass.ds((t + 1) * W, W)])

            sp.dma_start(ident[:, :], c_square[:, 0, :]).then_inc(const_in, 16)
            sp.dma_start(lng[:, :], load_rows(ln_g)).then_inc(const_in, 16)
            sp.dma_start(lnb[:, :], load_rows(ln_b)).then_inc(const_in, 16)
            program(sp, gate, down)

        @block.gpsimd
        def _(pool):
            nc.gpsimd.memset(half[:, :], -0.5).then_inc(half_done, 1)
            pool.wait_ge(half_done, 1)


            def power(t, r):
                n = row_tile(t, r)[1]
                pool.wait_ge(moments, t * NO + r + 1)
                nc.gpsimd.tensor_tensor(rstd[0:n, :], mv[0:n, 1:2], half[0:n, :], ALU.pow).then_inc(rstd_done, 1)

            with pool.Fori(0, NB - 1) as t:
                for r in range(NO):
                    power(t, r)
            for r in range(NO):
                power(NB - 1, r)

        @block.tensor
        def _(pe):
            def gate(t, sec, f):
                k = slot(sec, f)
                first = isinstance(t, int) and t == 0 and sec == 0 and f.under(1)
                if sec == 0 and f.under(1) and not first:
                    pe.wait_ge(s_used, C + t * 2 * KT)
                pe.wait_ge(lo_done, C + wn(t, sec, f) + 1)
                for h in range(2):
                    pe.wait_ge(gated, C + gh(t, sec, f, h) - 2 + 1)
                    for i in range(2):
                        for kk in range(KT):
                            if first and h == 0 and i == 0:
                                pe.wait_ge(x0_done, kk + 1)
                            for m, (w, x) in enumerate(((whi, x_hi), (whi, x_lo), (wlo, x_hi))):
                                mm = pe.matmul(G[h][:, i, 0:H], w[k][:, i * KT + kk, :], x[:, kk, h * H:(h + 1) * H],
                                               start=(kk == 0 and m == 0), stop=(kk == KT - 1 and m == 2))
                    mm.then_inc(g_done, 1)

            def down(t, sec, b, has_next):
                k, par = slot(sec, b + FS), b.odd
                if b.under(1):
                    pe.wait_ge(act_done, C + gh(t, sec, Twice(FS - 2), 1) + 1)
                    if sec == 0:
                        pe.wait_ge(ln_taken, C + t * NO)
                pe.wait_ge(lo_done, C + wn(t, sec, b + FS) + 1)
                pe.wait_ge(y_taken, C + dn(t, sec, b) - 2 + 1)
                for h in range(2):
                    for f in range(FS):
                        if b.under(1) and f == FS - 1:
                            pe.wait_ge(act_done, C + gh(t, sec, Twice(FS - 1), h) + 1)
                        for m, (w, x) in enumerate(((whi, a_hi), (whi, a_lo), (wlo, a_hi))):
                            mm = pe.matmul(Y[par][:, h, 0:H], w[k][:, f, :], x[:, f, h * H:(h + 1) * H],
                                           start=(f == 0 and m == 0), stop=(f == FS - 1 and m == 2))
                mm.then_inc(d_done, 1)

            def rows_of(t, r):
                a, n = row_tile(t, r)
                if r == 0:
                    pe.wait_ge(const_in, 48)
                    pe.wait_ge(y_taken, C + (t + 1) * 2 * KT)
                pe.wait_ge(ln_taken, C + t * NO + r - 2 + 1)
                for b in range(KT):
                    mm = pe.transpose(Y[r % 2][0:n, b // 4, (b % 4) * P:(b % 4 + 1) * P], yT[:, b, a:a + n], ident[:, :])
                mm.then_inc(tr_done, 1)

            program(pe, gate, down, lambda t, r: rows_of(t, r) if r < NO else None)
            for r in range(NO):
                rows_of(NB - 1, r)

        @block.scalar
        def _(act):
            def gate_used(t, sec, f):
                act.wait_ge(g_done, gh(t, sec, f, 1) + 1)

            def down_used(t, sec, b):
                act.wait_ge(d_done, dn(t, sec, b) + 1)

            def hi(t, sec, m, n):
                k = slot(sec, m)
                act.wait_ge(w_in[k], 32 * (wn_half(t, sec, m) + 1))
                nc.scalar.activation(whi[k][:, 0:n, :], raw[k][:, 0:n, :], ACT.Copy).then_inc(hi_done, 1)

            def slice_hi(n_half, b):
                act.wait_ge(s_in[b.odd], 16 * (n_half + 1))
                nc.scalar.activation(x_hi[:, b.n, :], sl[b.odd][:, :], ACT.Copy).then_inc(s_hi, 1)

            def tail(t, sec, f):
                for h in range(2):
                    act.wait_ge(g_done, gh(t, sec, f, h) + 1)
                    act.wait_ge(act_done, C + gh(t, sec, f, h) - 2 + 1)
                    nc.scalar.activation(act_t[h][:, :], G[h][:, 0, 0:H], ACT.Silu).then_inc(silu_done, 1)

            def gate(t, sec, f):
                if not f.under(2):
                    gate_used(t, sec, f + -2)
                elif sec:
                    down_used(t, 0, f + (KT - 2))
                elif not (isinstance(t, int) and t == 0):
                    down_used(t - 1, 1, f + (KT - 2))
                hi(t, sec, f, 2 * KT)
                if not f.under(1):
                    tail(t, sec, f + -1)

            def down(t, sec, b, has_next):
                if b.under(2):
                    gate_used(t, sec, b + (FS - 2))
                else:
                    down_used(t, sec, b + -2)
                hi(t, sec, b + FS, FS)
                if b.under(1):
                    tail(t, sec, Twice(FS - 1))
                if sec == 1 and has_next:
                    if b.under(1):
                        gate_used(t, 1, Twice(FS - 1))
                    slice_hi(t * KT + (b + KT).half, b)

            def store(t, r):
                a, n = row_tile(t, r)
                if isinstance(t, int) and t == NB - 1 and r == NO - 1:
                    dst = y_sample
                else:
                    dst = y_prompt[bass.ds(t * W + a, n), :]
                act.wait_ge(rows_done, t * NO + r + 1)
                act.dma_start(dst, ob[r % 2][0:n, :]).then_inc(y_out[r % 2], 16)

            for k in range(2):
                act.sem_inc(y_out[k], 16)
            for b in range(KT):
                if b % 2 == 0:
                    act.wait_ge(x0_in[b // 2], 16)
                nc.scalar.activation(x_hi[:, b, :], yT[:, b, :], ACT.Copy).then_inc(s_hi, 1)
            program(act, gate, down, lambda t, r: store(t, r - 2) if r >= 2 else None)
            for r in range(NO):
                store(NB - 1, r)
            act.wait_ge(y_out[0], 16 * (NB * 3 + 1))
            act.wait_ge(y_out[1], 16 * (NB * 2 + 1))

        @block.vector
        def _(dve):
            ch = Chain(dve, dve_chain)
            v = nc.vector
            for s in (lo_done, s_used, gated, act_done, y_taken, ln_taken):
                dve.sem_inc(s, C)

            def lo(t, sec, m, n):
                k = slot(sec, m)
                dve.wait_ge(hi_done, wn(t, sec, m) + 1)
                v.tensor_tensor(wlo[k][:, 0:n, :], raw[k][:, 0:n, :], split_view(whi[k][:, 0:n, :]),
                                ALU.subtract).then_inc(lo_done, 1)

            def slice_lo(n, b):
                dve.wait_ge(s_hi, n + 1)
                v.tensor_tensor(x_lo[:, b.n, :], sl[b.odd][:, :], split_view(x_hi[:, b.n, :]),
                                ALU.subtract).then_inc(s_used, 1)

            def tail(t, sec, f):
                for h in range(2):
                    n = gh(t, sec, f, h)
                    to = a_hi[:, f.n, h * H:(h + 1) * H]
                    dve.wait_ge(silu_done, n + 1)
                    v.tensor_tensor(act_t[h][:, :], act_t[h][:, :], G[h][:, 1, 0:H], ALU.mult).then_inc(gated, 1)
                    dve.wait_ge(gated, C + n + 1)
                    v.tensor_copy(to, act_t[h][:, :]).then_inc(act_hi, 1)
                    dve.wait_ge(act_hi, n + 1)
                    v.tensor_tensor(a_lo[:, f.n, h * H:(h + 1) * H], act_t[h][:, :], split_view(to),
                                    ALU.subtract).then_inc(act_done, 1)

            def y_take(t, sec, b):
                k = b.odd
                dve.wait_ge(d_done, dn(t, sec, b) + 1)
                src = Y[k][:, :, 0:H]
                dst = yT[:, b.n, :].rearrange("p (h c) -> p h c", h=2)
                if sec == 0:
                    dve.wait_ge(s_in[k], 16 * (t * KT + b.half + 1))
                    if b.under(1) and not (isinstance(t, int) and t == 0):
                        dve.wait_ge(tr_done, t * NO)
                    v.scalar_tensor_tensor(dst, sl[k][:, :].rearrange("p (h c) -> p h c", h=2), ALPHA, src,
                                           ALU.mult, ALU.add).then_inc(y_taken, 1)
                    dve.wait_ge(y_taken, C + dn(t, 0, b) + 1)
                    dve.sem_inc(s_used, 1)
                else:
                    dve.wait_ge(y_taken, C + dn(t, 0, b) + 1)
                    v.tensor_tensor(dst, dst, src, ALU.add).then_inc(y_taken, 1)

            def gate(t, sec, f):
                lo(t, sec, f, 2 * KT)
                if not f.under(1):
                    tail(t, sec, f + -1)
                elif sec == 1:
                    y_take(t, 0, Twice(KT - 1))
                elif not (isinstance(t, int) and t == 0):
                    y_take(t - 1, 1, Twice(KT - 1))

            def down(t, sec, b, has_next):
                lo(t, sec, b + FS, FS)
                if b.under(1):
                    tail(t, sec, Twice(FS - 1))
                else:
                    y_take(t, sec, b + -1)
                if sec == 1 and has_next:
                    slice_lo((t + 1) * KT + b.n, b)

            def norm(t, r):
                a, n = row_tile(t, r)
                k = r % 2
                dve.wait_ge(tr_done, t * NO + r + 1)
                dve.wait_ge(y_out[k], 16 * (t * (3 - k) + r // 2 + 1))
                for u in range(2):
                    ch.done(v.bn_stats(stats[0:n, u, :], Y[k][0:n, u, :]))
                ch.wait()
                v.memset(idle[:, :], 0.0)
                ch.step(v.bn_aggr(mv[0:n, :], stats[0:n, :, :]))
                v.tensor_scalar(mv[0:n, 1:2], mv[0:n, 1:2], EPS, None, ALU.add).then_inc(moments, 1)
                dve.wait_ge(rstd_done, t * NO + r + 1)
                x = ob[k][0:n, :]
                v.tensor_scalar(x, Y[k][0:n, :, :].rearrange("p n c -> p (n c)"), mv[0:n, 0:1], rstd[0:n, 0:1],
                                ALU.subtract, ALU.mult).then_inc(ln_taken, 1)
                dve.wait_ge(ln_taken, C + t * NO + r + 1)
                ch.step(v.tensor_tensor(x, x, lng[0:n, :], ALU.mult))
                v.tensor_tensor(x, x, lnb[0:n, :], ALU.add).then_inc(rows_done, 1)

            for b in range(KT):
                dve.wait_ge(s_hi, b + 1)
                v.tensor_tensor(x_lo[:, b, :], yT[:, b, :], split_view(x_hi[:, b, :]), ALU.subtract).then_inc(x0_done, 1)
            program(dve, gate, down, lambda t, r: norm(t, r - 1) if 1 <= r <= NO else None, ch, STEPS_4)
            y_take(NB - 1, 1, Twice(KT - 1))
            for r in range(NO):
                norm(NB - 1, r)


STEPS_4 = 20


def build(nc, x_prompt, x_sample, cache_k, cache_v, cache_logf, state_pool, state_conv, state_ssm, ln_in_g, ln_in_b,
          w_in, pool_w, pool_scale, fox_b_f, conv_w, conv_b, dt_bias, a_log, d_skip, ssm_norm_g, w_out,
          ln_mix_g, ln_mix_b, w_gate, w_up, w_down, ln_ffn_g, ln_ffn_b, c_square, c_inv, c_future,
          y_prompt, y_sample, p_k, p_v, p_logf, p_pool, p_conv, p_ssm, s_k, s_v, s_logf, s_pool, s_conv, s_ssm):
    def scratch(name, shape):
        return nc.dram_tensor(name, shape, F32).ap()

    def rows(a):
        return a[0, 0].rearrange("t h d -> t (h d)")

    def states(a):
        return a[0, 0].rearrange("h p n -> (h p) n")

    h_rows, mixed = scratch("h_rows", [TOKENS, D]), scratch("mixed", [TOKENS, D])
    q_ch, k_ch = scratch("q_ch", [FOX_W, TOKENS]), scratch("k_ch", [FOX_W, TOKENS])
    kc_ch = scratch("kc_ch", [FOX_W, PAST])
    c_hi_rows, c_lo_rows = scratch("c_hi_rows", [CT * FH, P]), scratch("c_lo_rows", [CT * FH, P])
    h2_ch = scratch("h2_ch", [D, TOKENS])
    outs = (rows(p_k), rows(p_v), p_logf[0, 0], p_pool[0, 0], p_conv[0, 0], states(p_ssm),
            rows(s_k), rows(s_v), s_logf[0, 0], s_pool[0, 0], s_conv[0, 0], states(s_ssm))

    with ExitStack() as ctx:
        def sem(name):
            return ctx.enter_context(nc.semaphore(name))

        project_mix_scan(nc, sem, x_prompt[0], x_sample[0], state_pool[0, 0], state_conv[0, 0], states(state_ssm),
                         ln_in_g, ln_in_b, w_in[0], pool_w[0], pool_scale[0], fox_b_f[0], conv_w[0], conv_b[0],
                         dt_bias[0], a_log[0], d_skip[0], ssm_norm_g[0], c_square, c_inv, h_rows, q_ch, k_ch,
                         mixed, outs)
        attend(nc, sem, rows(cache_k), rows(cache_v), cache_logf[0, 0], p_logf[0, 0], s_logf[0, 0], rows(p_v),
               rows(s_v), q_ch, k_ch, kc_ch, c_hi_rows, c_lo_rows, c_square, c_future, mixed)
        ahead = Ahead(nc, sem, ctx)
        mix_out(nc, sem, w_out[0], ln_mix_g[0], ln_mix_b[0], mixed, h_rows, c_square, h2_ch, w_gate[0],
                w_up[0], ahead)
        feed_forward(nc, sem, w_gate[0], w_up[0], w_down[0], ln_ffn_g[0], ln_ffn_b[0], h2_ch, c_square,
                     y_prompt[0], y_sample[0], ahead)


_INS = ["x_prompt", "x_sample", "cache_fox_k", "cache_fox_v", "cache_fox_logf", "state_pool", "state_conv",
        "state_ssm", "ln_in_g", "ln_in_b", "w_in", "pool_w", "pool_scale", "fox_b_f", "conv_w", "conv_b",
        "dt_bias", "a_log", "d_skip", "ssm_norm_g", "w_out", "ln_mix_g", "ln_mix_b", "w_gate", "w_up",
        "w_down", "ln_ffn_g", "ln_ffn_b"]


def _out_shapes():
    def group(t):
        return [(1, 1, t, FH, HD), (1, 1, t, FH, HD), (1, 1, t, FH), (1, 1, PHIST, POOL_W), (1, 1, CHIST, CONV),
                (1, 1, SH, HD, NST)]

    return [(1, SEQ, D), (1, DEC, D)] + group(SEQ) + group(DEC)


def kernel(**inputs):
    import numpy as _np
    import concourse.bacc as _bacc
    from concourse.bass_utils import run_bass_kernel_spmd as _run

    nc = _bacc.Bacc("TRN2", target_bir_lowering=False, num_devices=1)
    given = {name: _np.ascontiguousarray(inputs[name]) for name in _INS}
    given.update(host_constants())
    given.update(attention_constants())
    arrays, args = {}, []
    for name, a in given.items():
        arrays[f"in_{name}"] = a
        args.append(nc.dram_tensor(f"in_{name}", a.shape, F32, kind="ExternalInput").ap())
    for i, shape in enumerate(_out_shapes()):
        args.append(nc.dram_tensor(f"out_{i}", shape, F32, kind="ExternalOutput").ap())
    build(nc, *args)
    r = _run(nc, [arrays], core_ids=[0])
    return tuple(r.results[0][f"out_{i}"] for i in range(len(_out_shapes())))
```
